# Optimizing a Trainium2 kernel written in Bass

```python
import jax, jax.numpy as jnp
from jax import lax
import numpy as np

D_MODEL = 1024
BATCH = 1
SEQ = 512
DEPTH = 2

MEM_LEN = 256
N_BRANCH = 4
CHUNK = 64
EPS = 1e-6
MLSTM_HEADS = 4
MLSTM_HD = D_MODEL // (N_BRANCH * MLSTM_HEADS)
MLSTM_W = MLSTM_HEADS * MLSTM_HD
CONV_WIDTH = 4
GLA_HEADS = 4
GLA_DK = D_MODEL // (2 * N_BRANCH * GLA_HEADS)
GLA_DV = D_MODEL // (N_BRANCH * GLA_HEADS)
GLA_QK_W = GLA_HEADS * GLA_DK
GLA_V_W = GLA_HEADS * GLA_DV
GLA_RANK = 16
GLA_TAU = 16.0
S5_GROUP = 16
S5_GROUPS = D_MODEL // (N_BRANCH * S5_GROUP)
S5_W = S5_GROUPS * S5_GROUP
S5_STATE = 64
S5_DT_MIN = 0.001
S5_DT_MAX = 0.1
HGRN_HEADS = 4
HGRN_DK = D_MODEL // (N_BRANCH * HGRN_HEADS)
HGRN_W = HGRN_HEADS * HGRN_DK
XATTN_HEADS = 4
XATTN_HD = D_MODEL // XATTN_HEADS
MLP_HIDDEN = 4 * D_MODEL
MIX_SPLIT_WIDTHS = (
    MLSTM_W, MLSTM_W, MLSTM_W, MLSTM_HEADS, MLSTM_HEADS, MLSTM_W,
    GLA_QK_W, GLA_QK_W, GLA_V_W, GLA_RANK, GLA_V_W,
    S5_W,
    HGRN_W, HGRN_W, HGRN_W, HGRN_W,
    N_BRANCH * D_MODEL,
)
IN_WIDTH = sum(MIX_SPLIT_WIDTHS)

kernel_name = 'hybrid_gated_parallel_mixer_block'

def rmsnorm(x, g):
    xf = x.astype(jnp.float32)
    ms = jnp.mean(xf * xf, axis=-1, keepdims=True)
    return (xf * lax.rsqrt(ms + EPS) * g.astype(jnp.float32)).astype(x.dtype)

def head_rmsnorm(y, g):
    y = y * lax.rsqrt(jnp.mean(y * y, axis=-1, keepdims=True) + EPS)
    return y.reshape(y.shape[0], y.shape[1], -1) * g.astype(jnp.float32)

def causal_depthwise_conv(x, w, b):
    k = w.shape[0]
    y = lax.conv_general_dilated(x, w.astype(x.dtype)[:, None, :], window_strides=(1,),
                                 padding=[(k - 1, 0)], dimension_numbers=('NWC', 'WIO', 'NWC'),
                                 feature_group_count=x.shape[-1])
    return y + b.astype(x.dtype)

def to_chunks(t):
    b, s, h, d = t.shape
    return t.reshape(b, s // CHUNK, CHUNK, h, d).transpose(0, 3, 1, 2, 4)

def from_chunks(t):
    b, h, nc, l, d = t.shape
    return t.transpose(0, 2, 3, 1, 4).reshape(b, nc * l, h, d)

def gate_chunks(t):
    b, s, h = t.shape
    return t.reshape(b, s // CHUNK, CHUNK, h).transpose(0, 3, 1, 2)

def mlstm_chunkwise(q, k, v, i_pre, f_pre):
    bsz, _, nh, dh = q.shape
    qc = to_chunks(q) * (dh ** -0.5)
    kc = to_chunks(k)
    vc = to_chunks(v)
    li = gate_chunks(i_pre)
    lf = jax.nn.log_sigmoid(gate_chunks(f_pre))
    b = jnp.cumsum(lf, axis=-1)
    b_end = b[..., -1]
    a = b_end[..., None] - b + li
    m_loc = jnp.max(a, axis=-1)
    w = jnp.exp(a - m_loc[..., None])
    kv_loc = jnp.einsum('bhcsk,bhcsv,bhcs->bhckv', kc, vc, w)
    n_loc = jnp.einsum('bhcsk,bhcs->bhck', kc, w)

    def step(carry, inp):
        c_st, n_st, m_st = carry
        kv_c, n_c, mloc_c, bend_c = inp
        m_new = jnp.maximum(bend_c + m_st, mloc_c)
        s_old = jnp.exp(bend_c + m_st - m_new)
        s_new = jnp.exp(mloc_c - m_new)
        c_new = s_old[..., None, None] * c_st + s_new[..., None, None] * kv_c
        n_new = s_old[..., None] * n_st + s_new[..., None] * n_c
        return (c_new, n_new, m_new), (c_st, n_st, m_st)

    init = (jnp.zeros((bsz, nh, dh, dh), q.dtype), jnp.zeros((bsz, nh, dh), q.dtype),
            jnp.zeros((bsz, nh), q.dtype))
    xs = (jnp.moveaxis(kv_loc, 2, 0), jnp.moveaxis(n_loc, 2, 0),
          jnp.moveaxis(m_loc, 2, 0), jnp.moveaxis(b_end, 2, 0))
    _, (c_in, n_in, m_in) = lax.scan(step, init, xs)
    c_in = jnp.moveaxis(c_in, 0, 2)
    n_in = jnp.moveaxis(n_in, 0, 2)
    m_in = jnp.moveaxis(m_in, 0, 2)

    causal = jnp.tril(jnp.ones((CHUNK, CHUNK), dtype=bool))
    log_d = jnp.where(causal, b[..., :, None] - b[..., None, :] + li[..., None, :], -jnp.inf)
    inter_log = b + m_in[..., None]
    m_t = jnp.maximum(jnp.max(log_d, axis=-1), inter_log)
    scores = jnp.einsum('bhctk,bhcsk->bhcts', qc, kc) * jnp.exp(log_d - m_t[..., None])
    inter = jnp.exp(inter_log - m_t)
    num = (jnp.einsum('bhcts,bhcsv->bhctv', scores, vc)
           + inter[..., None] * jnp.einsum('bhctk,bhckv->bhctv', qc, c_in))
    den = jnp.sum(scores, axis=-1) + inter * jnp.einsum('bhctk,bhck->bhct', qc, n_in)
    h = num / jnp.maximum(jnp.abs(den), jnp.exp(-m_t))[..., None]
    return from_chunks(h)

def chunk_gated_linear(q, k, v, log_g):
    qc, kc, vc, gc = [jnp.moveaxis(to_chunks(t), 2, 0) for t in (q, k, v, log_g)]
    g_cum = jnp.cumsum(gc, axis=-2)
    causal = jnp.tril(jnp.ones((CHUNK, CHUNK), dtype=bool))

    def step(s_st, inp):
        qb, kb, vb, gb = inp
        g_end = gb[:, :, -1, :]
        o_inter = jnp.einsum('bhtk,bhkv->bhtv', qb * jnp.exp(gb), s_st)
        diff = gb[:, :, :, None, :] - gb[:, :, None, :, :]
        decay = jnp.exp(jnp.where(causal[:, :, None], diff, -jnp.inf))
        att = jnp.einsum('bhtk,bhsk,bhtsk->bhts', qb, kb, decay)
        o = o_inter + jnp.einsum('bhts,bhsv->bhtv', att, vb)
        s_new = (jnp.exp(g_end)[..., None] * s_st
                 + jnp.einsum('bhsk,bhsv->bhkv', kb * jnp.exp(g_end[:, :, None, :] - gb), vb))
        return s_new, o

    nc, bsz, nh, _, dk = qc.shape
    s0 = jnp.zeros((bsz, nh, dk, vc.shape[-1]), q.dtype)
    _, o = lax.scan(step, s0, (qc, kc, vc, g_cum))
    return from_chunks(jnp.moveaxis(o, 0, 2))

def _diag_combine(e1, e2):
    a1, b1 = e1
    a2, b2 = e2
    return a1 * a2, a2 * b1 + b2

def s5_ssm(u, lam_re, lam_im, b_re, b_im, c_re, c_im, d_skip, log_step):
    f32 = jnp.float32
    bsz, s, _ = u.shape
    u = u.astype(f32).reshape(bsz, s, S5_GROUPS, S5_GROUP)
    lam = lax.complex(lam_re.astype(f32), lam_im.astype(f32))
    step = jnp.exp(log_step.astype(f32))[:, None]
    lam_bar = jnp.exp(lam * step)
    b_bar = ((lam_bar - 1.0) / lam)[..., None] * lax.complex(b_re.astype(f32), b_im.astype(f32))
    bu = jnp.einsum('bsgh,gph->bsgp', u.astype(jnp.complex64), b_bar)
    a = jnp.broadcast_to(lam_bar, bu.shape)
    _, state = lax.associative_scan(_diag_combine, (a, bu), axis=1)
    c = lax.complex(c_re.astype(f32), c_im.astype(f32))
    y = jnp.real(jnp.einsum('bsgp,ghp->bsgh', state, c)) + d_skip.astype(f32) * u
    return y.reshape(bsz, s, S5_W)

def hybrid_mixer(h, w_in, m_conv_w, m_conv_b, m_i_bias, m_f_bias, m_norm, gla_w_a2, gla_b_a,
                 gla_norm, s5_lam_re, s5_lam_im, s5_b_re, s5_b_im, s5_c_re, s5_c_im, s5_d,
                 s5_log_step, s5_w_glu, s5_b_glu, hg_lb, hg_norm, w_branch, w_out):
    f32 = jnp.float32
    dt = h.dtype
    bsz, s, _ = h.shape
    split_points = [int(i) for i in np.cumsum(MIX_SPLIT_WIDTHS)[:-1]]
    (m_q, m_k, m_v, m_i, m_f, m_o, g_q, g_k, g_v, g_a, g_r, s_u,
     r_q, r_f, r_i, r_g, gate_cols) = jnp.split(h @ w_in, split_points, axis=-1)

    def heads(t, n):
        return t.astype(f32).reshape(bsz, s, n, -1)

    qk = jax.nn.silu(causal_depthwise_conv(jnp.concatenate([m_q, m_k], axis=-1), m_conv_w, m_conv_b))
    mq, mk = jnp.split(qk, 2, axis=-1)
    hm = mlstm_chunkwise(heads(mq, MLSTM_HEADS), heads(mk, MLSTM_HEADS), heads(m_v, MLSTM_HEADS),
                         (m_i + m_i_bias).astype(f32), (m_f + m_f_bias).astype(f32))
    y_a = jax.nn.sigmoid(m_o.astype(f32)) * head_rmsnorm(hm, m_norm)

    log_a = jax.nn.log_sigmoid((g_a @ gla_w_a2 + gla_b_a).astype(f32)) / GLA_TAU
    og = chunk_gated_linear(heads(g_q, GLA_HEADS) * (GLA_DK ** -0.5), heads(g_k, GLA_HEADS),
                            heads(g_v, GLA_HEADS), heads(log_a, GLA_HEADS))
    y_b = jax.nn.silu(g_r.astype(f32)) * head_rmsnorm(og, gla_norm)

    ys = s5_ssm(s_u, s5_lam_re, s5_lam_im, s5_b_re, s5_b_im, s5_c_re, s5_c_im, s5_d, s5_log_step)
    glu_val, glu_gate = jnp.split(jax.nn.gelu(ys) @ s5_w_glu.astype(f32) + s5_b_glu.astype(f32), 2, axis=-1)
    y_c = glu_val * jax.nn.sigmoid(glu_gate)

    z = r_f.astype(f32)
    log_f = jnp.logaddexp(jnp.log(hg_lb), jnp.log1p(-hg_lb) + jax.nn.log_sigmoid(z))
    k_hg = (1.0 - hg_lb) * jax.nn.sigmoid(-z)
    oh = chunk_gated_linear(heads(jax.nn.silu(r_q), HGRN_HEADS), heads(k_hg, HGRN_HEADS),
                            heads(r_i, HGRN_HEADS), heads(log_f, HGRN_HEADS))
    y_d = jax.nn.silu(r_g.astype(f32)) * head_rmsnorm(oh, hg_norm)

    gates = jax.nn.sigmoid(gate_cols.astype(f32)).reshape(bsz, s, N_BRANCH, D_MODEL)
    branch_outs = (y_a, y_b, y_c, y_d)
    merged = jnp.zeros((bsz, s, D_MODEL), f32)
    for n in range(N_BRANCH):
        merged = merged + gates[:, :, n, :] * (branch_outs[n].astype(dt) @ w_branch[n]).astype(f32)
    return merged.astype(dt) @ w_out

def cross_attention(h, mem_n, w_q, w_kv, w_o):
    bsz, s, _ = h.shape
    q = (h @ w_q).reshape(bsz, s, XATTN_HEADS, XATTN_HD)
    k, v = jnp.split(mem_n @ w_kv, 2, axis=-1)
    k = k.reshape(bsz, -1, XATTN_HEADS, XATTN_HD)
    v = v.reshape(bsz, -1, XATTN_HEADS, XATTN_HD)
    scores = jnp.einsum('bshd,bmhd->bhsm', q, k).astype(jnp.float32) * (XATTN_HD ** -0.5)
    p = jax.nn.softmax(scores, axis=-1).astype(v.dtype)
    o = jnp.einsum('bhsm,bmhd->bshd', p, v).reshape(bsz, s, D_MODEL)
    return o @ w_o

def sq_relu_mlp(h, w1, w2):
    return jnp.square(jax.nn.relu(h @ w1)) @ w2

def setup_inputs(seed: int = 0) -> dict:
    key = jax.random.key(seed)
    ks = iter(jax.random.split(key, 40))
    f32 = jnp.float32

    def nrm(shape, scale):
        return jax.random.normal(next(ks), shape, f32) * scale

    def gain(shape):
        return 1.0 + 0.02 * jax.random.normal(next(ks), shape, f32)

    lam_im = (jnp.pi * jnp.arange(S5_STATE, dtype=f32))[None, None, :] + nrm((DEPTH, S5_GROUPS, S5_STATE), 0.01)
    return {
        'x': nrm((BATCH, SEQ, D_MODEL), 1.0),
        'mem': nrm((BATCH, MEM_LEN, D_MODEL), 1.0),
        'norm_mix': gain((DEPTH, D_MODEL)),
        'w_in': nrm((DEPTH, D_MODEL, IN_WIDTH), D_MODEL ** -0.5),
        'mlstm_conv_w': nrm((DEPTH, CONV_WIDTH, 2 * MLSTM_W), CONV_WIDTH ** -0.5),
        'mlstm_conv_b': nrm((DEPTH, 2 * MLSTM_W), 0.01),
        'mlstm_i_bias': nrm((DEPTH, MLSTM_HEADS), 0.1),
        'mlstm_f_bias': jnp.linspace(3.0, 6.0, MLSTM_HEADS, dtype=f32)[None, :] + nrm((DEPTH, MLSTM_HEADS), 0.01),
        'mlstm_norm': gain((DEPTH, MLSTM_W)),
        'gla_w_a2': nrm((DEPTH, GLA_RANK, GLA_QK_W), GLA_RANK ** -0.5),
        'gla_b_a': nrm((DEPTH, GLA_QK_W), 0.01),
        'gla_norm': gain((DEPTH, GLA_V_W)),
        's5_lam_re': -0.5 + nrm((DEPTH, S5_GROUPS, S5_STATE), 0.01),
        's5_lam_im': lam_im,
        's5_b_re': nrm((DEPTH, S5_GROUPS, S5_STATE, S5_GROUP), (2 * S5_GROUP) ** -0.5),
        's5_b_im': nrm((DEPTH, S5_GROUPS, S5_STATE, S5_GROUP), (2 * S5_GROUP) ** -0.5),
        's5_c_re': nrm((DEPTH, S5_GROUPS, S5_GROUP, S5_STATE), S5_STATE ** -0.5),
        's5_c_im': nrm((DEPTH, S5_GROUPS, S5_GROUP, S5_STATE), S5_STATE ** -0.5),
        's5_d': nrm((DEPTH, S5_GROUPS, S5_GROUP), 1.0),
        's5_log_step': jax.random.uniform(next(ks), (DEPTH, S5_GROUPS), f32,
                                          minval=float(np.log(S5_DT_MIN)), maxval=float(np.log(S5_DT_MAX))),
        's5_w_glu': nrm((DEPTH, S5_W, 2 * S5_W), S5_W ** -0.5),
        's5_b_glu': nrm((DEPTH, 2 * S5_W), 0.01),
        'hgrn_lb_logits': nrm((DEPTH, HGRN_W), 0.1),
        'hgrn_norm': gain((DEPTH, HGRN_W)),
        'w_branch': nrm((DEPTH, N_BRANCH, D_MODEL // N_BRANCH, D_MODEL), (D_MODEL // N_BRANCH) ** -0.5),
        'w_out': nrm((DEPTH, D_MODEL, D_MODEL), D_MODEL ** -0.5),
        'norm_xattn': gain((DEPTH, D_MODEL)),
        'norm_mem': gain((DEPTH, D_MODEL)),
        'xattn_w_q': nrm((DEPTH, D_MODEL, D_MODEL), D_MODEL ** -0.5),
        'xattn_w_kv': nrm((DEPTH, D_MODEL, 2 * D_MODEL), D_MODEL ** -0.5),
        'xattn_w_o': nrm((DEPTH, D_MODEL, D_MODEL), D_MODEL ** -0.5),
        'norm_mlp': gain((DEPTH, D_MODEL)),
        'mlp_w1': nrm((DEPTH, D_MODEL, MLP_HIDDEN), D_MODEL ** -0.5),
        'mlp_w2': nrm((DEPTH, MLP_HIDDEN, D_MODEL), MLP_HIDDEN ** -0.5),
        'norm_final': gain((D_MODEL,)),
    }

def reference(x, mem, norm_mix, w_in, mlstm_conv_w, mlstm_conv_b, mlstm_i_bias, mlstm_f_bias,
              mlstm_norm, gla_w_a2, gla_b_a, gla_norm, s5_lam_re, s5_lam_im, s5_b_re, s5_b_im,
              s5_c_re, s5_c_im, s5_d, s5_log_step, s5_w_glu, s5_b_glu, hgrn_lb_logits, hgrn_norm,
              w_branch, w_out, norm_xattn, norm_mem, xattn_w_q, xattn_w_kv, xattn_w_o, norm_mlp,
              mlp_w1, mlp_w2, norm_final):
    lb_all = jnp.cumsum(jax.nn.softmax(hgrn_lb_logits.astype(jnp.float32), axis=0), axis=0)
    lb_all = lb_all - lb_all[:1]
    for l in range(DEPTH):
        h = rmsnorm(x, norm_mix[l])
        x = x + hybrid_mixer(h, w_in[l], mlstm_conv_w[l], mlstm_conv_b[l], mlstm_i_bias[l],
                             mlstm_f_bias[l], mlstm_norm[l], gla_w_a2[l], gla_b_a[l], gla_norm[l],
                             s5_lam_re[l], s5_lam_im[l], s5_b_re[l], s5_b_im[l], s5_c_re[l],
                             s5_c_im[l], s5_d[l], s5_log_step[l], s5_w_glu[l], s5_b_glu[l],
                             lb_all[l], hgrn_norm[l], w_branch[l], w_out[l])
        h = rmsnorm(x, norm_xattn[l])
        x = x + cross_attention(h, rmsnorm(mem, norm_mem[l]), xattn_w_q[l], xattn_w_kv[l], xattn_w_o[l])
        h = rmsnorm(x, norm_mlp[l])
        x = x + sq_relu_mlp(h, mlp_w1[l], mlp_w2[l])
    return rmsnorm(x, norm_final)


_drawn_inputs = setup_inputs


def setup_inputs(seed=0):
    import zlib

    import numpy as np

    out = dict(_drawn_inputs(seed))
    spreads = {}
    factors = {'mlstm_conv_b': 8.0,
     'mlstm_i_bias': 64.0,
     'mlstm_norm': 7.735,
     'gla_b_a': 8.0,
     'gla_norm': 7.521,
     's5_lam_re': 64.0,
     's5_lam_im': 2.742,
     's5_b_re': 3.905,
     's5_b_im': 3.854,
     's5_c_re': 3.848,
     's5_c_im': 3.852,
     's5_log_step': 2.773,
     's5_b_glu': 8.0,
     'hgrn_lb_logits': 8.0,
     'hgrn_norm': 7.412,
     'norm_xattn': 8.0,
     'norm_mem': 8.0,
     'norm_final': 8.074,
     'norm_mlp': 2.791}
    for name, (base, spread) in spreads.items():
        noise = np.random.default_rng([zlib.crc32(name.encode()), seed]).standard_normal(out[name].shape)
        drawn = base * np.exp(spread * noise) if base else spread * noise
        out[name] = __import__('jax').numpy.asarray(drawn.astype(out[name].dtype))
    for name, factor in factors.items():
        out[name] = (out[name] * factor).astype(out[name].dtype)
    return out
```

```python
from contextlib import ExitStack

import numpy as np

import concourse.bass as bass
from concourse import mybir

F32 = mybir.dt.float32
F32R = mybir.dt.float32r
I32 = mybir.dt.int32
ALU = mybir.AluOpType
ACT = mybir.ActivationFunctionType

P = 128
D = 1024
KC = D // P
SEQ = 512
DEPTH = 2
MEM = 256
CH = 64
NCH = SEQ // CH
TT = SEQ // P
EPS = 1e-6
HD = 64
GDK = 32
RANK = 16
S5_T = 8
S5_N = SEQ // S5_T
S5_TILES = 8
HIDDEN = 4 * D
BW = 256
NEG = -1e30
LOG_SET = "natural_log_exp_and_others"
EXP_SET = "exp_and_others"
PI = float(np.pi)

COL = {}
_at = 0
for _name, _w in (("m_q", 256), ("m_k", 256), ("m_v", 256), ("m_i", 4), ("m_f", 4), ("m_o", 256), ("g_q", 128),
                  ("g_k", 128), ("g_v", 256), ("g_a", 16), ("g_r", 256), ("s_u", 256), ("r_q", 256), ("r_f", 256),
                  ("r_i", 256), ("r_g", 256), ("gates", 4096)):
    COL[_name] = _at
    _at += _w
IN_WIDTH = _at

PROW = {}
_at = 0
for _name, _n in (("norm_mix", 8), ("norm_xattn", 8), ("norm_mem", 8), ("norm_mlp", 8), ("mlstm_conv_w", 16),
                  ("mlstm_conv_b", 4), ("mlstm_norm", 2), ("gla_norm", 2), ("hgrn_norm", 2), ("s5_d", 2),
                  ("gla_b_a", 1), ("s5_b_glu", 4), ("lb0", 2), ("lb1", 2), ("s5_lam_re", 8), ("s5_lam_im", 8),
                  ("norm_final", 8), ("if_bias", 1), ("step", 8), ("hg_c0", 2), ("hg_c1", 2)):
    PROW[_name] = _at
    _at += _n
NROW = _at

CCOL = {}
_at = 0
for _name, _n in (("ident", 128), ("head_mean", 128), ("mean", 128), ("ones", 64), ("neg", 64), ("reset", 512),
                  ("pair_sel", 256), ("head_sel", 256), ("parity", 2)):
    CCOL[_name] = (_at, _n)
    _at += _n
NCONST = _at
LEVELS = [0, 32, 16, 8, 4, 2, 1]


def shape_constants():
    c = np.zeros((P, NCONST), np.float32)

    def put(name, a):
        at, n = CCOL[name]
        c[:a.shape[0], at:at + n] = a

    r = np.arange(P)
    put("ident", np.eye(P, dtype=np.float32))
    put("head_mean", (r[:, None] // HD == r[None, :] // HD).astype(np.float32) / HD)
    put("mean", np.full((P, P), 1.0 / D, np.float32))
    put("ones", np.ones((P, 64), np.float32))
    t = np.arange(CH)
    put("neg", np.where(r[:, None] % CH <= t[None, :], 0.0, NEG).astype(np.float32))
    put("reset", np.broadcast_to((np.arange(SEQ) % CH != 0).astype(np.float32), (P, SEQ)))
    pair = np.zeros((4, 2, P), np.float32)
    head = np.zeros((4, 4, 64), np.float32)
    for h in range(4):
        pair[h, h // 2, 64 * (h % 2):64 * (h % 2) + 64] = 1.0
        head[h, h, :] = 1.0
    put("pair_sel", pair.reshape(4, 256))
    put("head_sel", head.reshape(4, 256))
    put("parity", np.stack([(r // 16) % 2 == 0, (r // 16) % 2 == 1], 1).astype(np.float32))
    m = np.zeros((P, len(LEVELS), CH), np.int32)
    s = r[:, None] % CH
    tt = t[None, :]
    for n, w in enumerate(LEVELS):
        if w == 0:
            m[:, n] = s == tt
        else:
            m[:, n] = (s // (2 * w) == tt // (2 * w)) & (s % (2 * w) < w) & (tt % (2 * w) >= w)
    return c, m.reshape(P, -1)


def block_order():
    order = [(n, "full") for n in ("r_f", "r_q", "r_i", "g_qk", "g_v", "g_r", "r_g", "gate3_0", "m_q", "m_k", "m_v", "m_o",
                                   "branch3_0", "gate3_1", "branch3_1", "gate3_2", "branch3_2", "gate3_3", "branch3_3", "s_u")]
    for n in (1, 0):
        order += [(f"{what}{n}_{c}", "full") for c in range(4) for what in ("gate", "branch")]
    order += [(n, "full") for n in ("gate2_0", "gate2_1", "branch2_0", "branch2_1", "gate2_2", "branch2_2", "gate2_3", "branch2_3")]
    order += [(f"out{c}", "full") for c in range(4)]
    order += [(f"kv{c}", "full") for c in range(4)]
    for c in range(4):
        order += [(f"q{c}", "full"), (f"kv{4 + c}", "full")]
    order = [(n, "branch" if n.startswith("branch") else kind) for n, kind in order]
    order += [(f"o{c}", "full") for c in range(4)]
    ups, downs = [[(f"up{q}_{c}", "full") for c in range(4)] for q in range(4)], [
        [(f"down{q}_{c}", "full") for c in range(4)] for q in range(4)]
    order += ups[0] + ups[1] + downs[0] + ups[2] + downs[1] + ups[3] + downs[2] + downs[3]
    return order


BLOCKS = block_order()
BLOCK = {name: n for n, (name, _) in enumerate(BLOCKS)}
UNIT, UNITS = {}, []
for _name, _kind in BLOCKS:
    UNIT[_name] = len(UNITS)
    UNITS += [(_name, "first"), (_name, "last")] if _kind == "full" else [(_name, "last")]
NUNIT = len(UNITS)
FIRSTS = [sum(part == "first" for _, part in UNITS[:u + 1]) for u in range(NUNIT)]
RAW = 5
SLOT, BEFORE, _last, _turn = [], [], {}, 0
for _u, (_name, _part) in enumerate(UNITS):
    if _name.startswith("branch"):
        _s = 2
    else:
        _s, _turn = _turn, 1 - _turn
    SLOT.append(_s)
    BEFORE.append(_last.get(_s))
    _last[_s] = _u


def psum_set(name):
    return BLOCK[name] % 2, BLOCK[name] // 2


def build(nc, ins, out):
    (x, mem, norm_mix, w_in, mlstm_conv_w, mlstm_conv_b, mlstm_i_bias, mlstm_f_bias, mlstm_norm, gla_w_a2, gla_b_a,
     gla_norm, s5_lam_re, s5_lam_im, s5_b_re, s5_b_im, s5_c_re, s5_c_im, s5_d, s5_log_step, s5_w_glu, s5_b_glu,
     hgrn_lb_logits, hgrn_norm, w_branch, w_out, norm_xattn, norm_mem, xattn_w_q, xattn_w_kv, xattn_w_o, norm_mlp,
     mlp_w1, mlp_w2, norm_final, consts, level_masks) = ins
    mem_scratch = nc.dram_tensor("mem_scratch", (P, KC * MEM), F32, kind="Internal").ap()

    ctx = ExitStack()
    with ctx:
        def sb(name, shape, dt=F32):
            return ctx.enter_context(nc.sbuf_tensor(name, shape, dt))

        X = sb("x_t", [P, KC, SEQ])
        Hhi = sb("h_hi", [P, KC, SEQ], F32R)
        Hlo = sb("h_lo", [P, KC, SEQ], F32R)
        MG = sb("merged", [P, KC, SEQ])
        WR = sb("w_raw", [P, RAW, 4 * BW])
        WHi = sb("w_hi", [P, 10 * BW], F32R)
        WLo = sb("w_lo", [P, 10 * BW], F32R)
        work_at = nc.sbuf_base
        YR = sb("work", [P, 8 + 33, 512])
        YS_R = nc.alloc_sbuf_tensor_at("work_split", [P, 8 + 33, 512], F32R, offset=work_at)
        TH = sb("gate_t", [P, 2, SEQ])
        CO = sb("consts_sb", [P, NCONST])
        LM = sb("masks_sb", [P, len(LEVELS), CH], I32)
        PTA = sb("params_all", [P, DEPTH, NROW])
        PT = sb("params", [P, NROW])
        WSM = sb("w_small", [P, KC, 80])
        WA2 = sb("w_a2", [RANK, P])
        BRI = sb("s5_b", [P, 2, S5_TILES, 16])
        CRI = sb("s5_c", [P, 2, 2, 64])
        LP = sb("if_rows", [36, SEQ])
        SM = sb("small", [P, 64])

        R = lambda a, n=1: YR[:, 8 + a:8 + a + n, :]
        flat = lambda ap: ap.rearrange("p a b -> p (a b)")
        Rf = lambda a, n: flat(R(a, n))

        def const(name):
            at, n = CCOL[name]
            return CO[:, at:at + n]

        ident, head_mean, mean_w = const("ident"), const("head_mean"), const("mean")
        ones64, neg_mask, reset = const("ones"), const("neg"), const("reset")
        pair_sel = const("pair_sel").rearrange("p (j m) -> p j m", j=2)
        head_sel = const("head_sel").rearrange("p (h m) -> p h m", h=4)
        parity = const("parity")
        col = lambda name, n=0: PT[:, PROW[name] + n:PROW[name] + n + 1]
        colr = lambda name, n, parts: PT[parts, PROW[name] + n:PROW[name] + n + 1]

        G = [[ctx.enter_context(nc.psum_tensor(f"gemm{s}{b}", [P, 512], F32)) for b in range(2)] for s in range(2)]
        M = [ctx.enter_context(nc.psum_tensor(f"mix{b}", [P, 512], F32)) for b in range(4)]

        def bc(ap, axis, n):
            a = ap.unsqueeze(axis)
            shape = list(a.shape)
            shape[axis] = n
            return a.to_broadcast(shape)

        layer_sems = []

        def sem(name):
            s = ctx.enter_context(nc.semaphore(name))
            layer_sems.append(s)
            return s

        def whole(name):
            return ctx.enter_context(nc.semaphore(name))

        p_dma, p_rows, p_vec, p_act, p_pe, p_out = (whole(n) for n in ("pro_loads", "pro_rows", "pro_vector", "pro_scalar", "pro_tensor", "pro_stores"))
        f_vec, f_act, f_pe = (whole(n) for n in ("fin_vector", "fin_scalar", "fin_tensor"))
        layer_end, layer_go = whole("layer_end"), whole("layer_go")

        v_chain, a_chain = sem("vector_steps"), sem("scalar_steps")
        raw_in = [sem(f"raw_in{i}") for i in range(RAW)]
        split_hi, split_ready, split_used = sem("split_hi"), sem("split_ready"), sem("split_used")
        gemm_done = [sem(f"gemm_done{i}") for i in range(2)]
        gemm_free = [sem(f"gemm_free{i}") for i in range(2)]
        params_in, all_ended = sem("params_in"), sem("all_ended")
        head_sq, head_ms, head_rs = sem("head_squares"), sem("head_means"), sem("head_factors")
        sq_ready, sq_used, ms_done, rstd_ready = sem("sq_ready"), sem("sq_used"), sem("ms_done"), sem("rstd_ready")
        hx_ready, hi_ready, h_ready = sem("hx_ready"), sem("hi_ready"), sem("h_ready")
        th_ready, th_used = sem("th_ready"), sem("th_used")
        small_done, rows_ready, ga_ready, ga_done = sem("small_done"), sem("if_rows_ready"), sem("ga_ready"), sem("ga_done")
        y_act, y_hi, y_ready = sem("y_act"), sem("y_hi"), sem("y_ready")
        mg_ready, mghi_ready, mgs_ready = sem("mg_ready"), sem("mghi_ready"), sem("mg_split_ready")
        x_ready = sem("x_ready")

        class Mixer:

            def __init__(self, pre, tiles, dk, q, k, v, g, gr, e, xx, att, attbd, kt, state, o, sq, gscale, oscale, norm):
                self.pre, self.J, self.dk, self.gscale, self.oscale, self.norm = pre, tiles, dk, gscale, oscale, norm
                self.W = tiles * SEQ
                self.Q, self.K, self.Gc = Rf(q, tiles), Rf(k, tiles), Rf(g, tiles)
                self.V = Rf(v, 2).rearrange("p (t c) -> p t c", t=TT)
                self.GR = R(gr, 2)
                self.E = [Rf(e + tiles * i, tiles) for i in range(2)]
                self.X = [Rf(xx + tiles * i, tiles) for i in range(2)]
                self.att = Rf(att, 2)
                self.attbd = Rf(attbd, 4).rearrange("p (h t s) -> p h t s", h=4, t=TT)
                self.KT = Rf(kt, tiles).rearrange("p (t c) -> p t c", t=TT)
                self.per = P // dk
                wide = self.per * HD
                self.S = YR[:, 8 + state:8 + state + 4, :].rearrange("p a b -> p (a b)")[:, :tiles * 7 * wide].rearrange(
                    "p (j c v) -> p j c v", j=tiles, c=7)
                self.O, self.SQ = R(o, 2), R(sq, 2)
                self.gate_in, self.g_ready = sem(pre + "_gate_in"), sem(pre + "_decay_ready")
                self.kq_ready = sem(pre + "_kq_ready")
                self.v_ready = sem(pre + "_v_ready")
                self.d_ready, self.e_ready, self.x_ready = sem(pre + "_diff"), sem(pre + "_exp"), sem(pre + "_x")
                self.lev_done, self.picked = sem(pre + "_scores"), sem(pre + "_picked")
                self.bd_ready, self.kd_ready = sem(pre + "_att_ready"), sem(pre + "_kdecay_ready")
                self.kt_done, self.kt_ready = sem(pre + "_kt_done"), sem(pre + "_kt_ready")
                self.kv_done, self.s_ready = sem(pre + "_kv_done"), sem(pre + "_state_ready")
                self.o_done = sem(pre + "_o_done")

            def score_bank(self, level, h):
                return M[2 * (level % 2) + h % 2] if self.J == 2 else M[h]

            def score_cols(self, h):
                return (h // 2) * 256 if self.J == 2 else 0

            def slot(self, h):
                return (h % 2) * 2 + h // 2 if self.J == 2 else h

        hg = Mixer("hg", 2, HD, 4, 2, 6, 0, 8, 10, 14, 18, 14, 20, 22, 10, 12, 1.0, 0.5, "hgrn_norm")
        gl = Mixer("gl", 1, GDK, 26, 27, 28, 32, 30, 10, 12, 14, 16, 20, 22, 12, 10, 1.0 / 16.0, GDK ** -0.5, "gla_norm")

        CIN = YR[:, 8:8 + 5, :].rearrange("p a b -> p (a b)")[:, 0:4 * 515].rearrange("p (j t) -> p j t", j=4)
        MV = Rf(5, 2).rearrange("p (t c) -> p t c", t=TT)
        MO = R(7, 2)
        MQK = [R(a)[:, 0, :] for a in (9, 0, 1, 2)]
        MTHG = [R(16 + j)[:, 0, :] for j in range(4)]
        MBD = Rf(14, 4).rearrange("p (h t s) -> p h t s", h=4, t=TT)
        MATT = Rf(18, 2).rearrange("p (b c) -> p b c", b=2)
        MKT = Rf(20, 2).rearrange("p (t j b v) -> p t j b v", t=TT, j=2, b=2)
        MS = [YR[:, 8 + a:8 + a + 4, :].rearrange("p a b -> p (a b)")[:, 0:7 * 256].rearrange(
            "p (c b v) -> p c b v", c=7, b=2) for a in (22, 28)]
        MQT, MEM_E = R(10, 2), R(12, 2)
        MDA, MOO, MSQ = R(20, 2), R(18, 2), R(22, 2)
        MC = (HD ** -0.5) / 4.0
        MAW = Rf(32, 1)[:, 0:256].rearrange("p (t c) -> p t c", t=TT)
        MDEC = SM[:, 0:16].rearrange("p (j c) -> p j c", j=2)
        m_names = ("cin_ready", "cv_ready", "mth_ready", "mv_ready", "a1", "v1", "aw_done", "aw_ready",
                   "ib_done", "ib_ready", "mex_done", "mex_v", "mex_ready", "mqk_done", "matt_ready", "mbd_ready",
                   "mkt_done", "mkt_ready", "mkv_done", "ms_ready", "mo_done", "mabs_ready", "mh_ready", "stack_ready", "emb_ready")
        ms = {n: sem("mlstm_" + n) for n in m_names}

        XP = Rf(0, 8).rearrange("p (r u t c) -> p r u t c", r=2, u=8, t=8)
        CL = Rf(0, 8).rearrange("p (r j t c) -> p r j t c", r=2, j=8, t=8)
        BT = Rf(8, 8).rearrange("p (a r u s) -> p a r u s", a=2, r=2, u=8)
        KTm = Rf(16, 4).rearrange("p (a u c) -> p a u c", a=2, u=8)
        SW = [Rf(20, 1).rearrange("p (t n) -> p t n", t=8), Rf(21, 1).rearrange("p (t n) -> p t n", t=8)]
        TB = [Rf(22, 1).rearrange("p (t n) -> p t n", t=8), Rf(23, 1).rearrange("p (t n) -> p t n", t=8)]
        SZ = [Rf(24, 1), Rf(25, 1)]
        ST = [Rf(28, 1), Rf(29, 1), Rf(30, 1)]
        SX = [Rf(31, 1).rearrange("p (t n) -> p t n", t=8), Rf(32, 1).rearrange("p (t n) -> p t n", t=8)]
        UU = R(26, 2)
        T4 = [Rf(20, 4), Rf(28, 4)]
        WGLU = Rf(8, 2).rearrange("p (k c) -> p k c", k=2)
        YS, GE = R(20, 2), R(22, 2)
        CT = YR[:, 4, :].rearrange("p (r c) -> p r c", r=2)
        PW = sb("s5_pw", [P, 2, 9, 8])
        PS = sb("s5_small", [P, 24, 8])
        S5T = [sb("s5_tmp", [P, 32]), PS[:, 19:23, :].rearrange("p a b -> p (a b)")]
        s_names = ("prm", "sin_in", "sin_ready", "xp_ready", "cp_ready", "ct_done", "ct_ready", "bt_done", "bt_ready", "kk_done", "kk_ready",
                   "cl_ready", "u_ready", "w_done", "x_ready", "y_done", "wglu_in", "ys_ready", "sq", "poly", "tanh",
                   "ge_ready", "glu_done", "val_ready")
        ss = {n: sem("s5_" + n) for n in s_names}

        MHhi = YS_R[:, 8:16, :]
        MHlo = YS_R[:, 16:24, :]
        MBASE = Rf(28, 4).rearrange("p (k m) -> p k m", k=KC)
        MMhi = YS_R[:, 28:32, :].rearrange("p a b -> p (a b)").rearrange("p (k m) -> p k m", k=KC)
        MMlo = YS_R[:, 32:36, :].rearrange("p a b -> p (a b)").rearrange("p (k m) -> p k m", k=KC)
        MMX = Rf(16, 4).rearrange("p (k m) -> p k m", k=KC)
        KTt = Rf(28, 4).rearrange("p (k m) -> p k m", k=KC)
        VM = YR[:, 0:4, :].rearrange("p a b -> p (a b)").rearrange("p (m c) -> p m c", m=2)
        PB = [Rf(0, 2).rearrange("p (t m) -> p t m", t=TT), Rf(2, 2).rearrange("p (t m) -> p t m", t=TT)]
        PTB = [R(4, 2), R(6, 2)]
        AST = PS[:, 0:8, :].rearrange("p a b -> p (a b)").rearrange("p (n t) -> p n t", n=4)
        a_names = ("base_free", "mem_base_in", "mmx", "mm_hi", "mm_ready", "kt_ready", "vm_ready", "q_ready", "sc_done", "mx_ready", "p_exp", "p_ready",
                   "pt_done", "pt_ready", "o_done", "oc_ready", "ohi_ready", "osplit_ready")
        at = {n: sem("attn_" + n) for n in a_names}
        up_a, up_v, uphi, uplo = sem("up_relu"), sem("up_squared"), sem("up_hi"), sem("up_ready")
        UPX = R(32, 1)
        MHID = [[YS_R[:, 16 * b + 8 * p:16 * b + 8 * p + 8, :] for p in range(2)] for b in range(2)]

        YB = [[YS_R[:, 4 * b:4 * b + 2, :], YS_R[:, 4 * b + 2:4 * b + 4, :]] for b in range(2)]
        BRANCH_AT = {3: 0, 1: 1, 0: 0, 2: 1}
        BRANCH_NO = {3: 0, 1: 1, 0: 2, 2: 3}

        block = ctx.enter_context(nc.Block())

        def chained(eng, chain):
            count = {}

            def do(ins, s=None):
                s = chain if s is None else s
                count[s.name] = count.get(s.name, 0) + 1
                ins.then_inc(s, 1)
                eng.wait_ge(s, count[s.name])
            return do

        @block.sync
        def _(sp):
            sp.dma_start(CO[:, :], consts).then_inc(p_dma, 16)
            sp.dma_start(LM[:, :, :], level_masks.rearrange("p (l c) -> p l c", c=CH)).then_inc(p_dma, 16)
            sp.dma_start(R(0, 8).rearrange("p (t a) b -> p t (a b)", t=TT),
                         x[0].rearrange("(t p) d -> p t d", p=P)).then_inc(p_dma, 16)
            sp.dma_start(R(8, 4).rearrange("p (t a) b -> p t (a b)", t=2),
                         mem[0].rearrange("(t p) d -> p t d", p=P)).then_inc(p_dma, 16)
            sp.wait_ge(p_vec, 1)
            for l in range(DEPTH):
                stage = Rf(20 + l, 1)[:, 0:P]
                for name, src in (("norm_mix", norm_mix), ("norm_xattn", norm_xattn), ("norm_mem", norm_mem),
                                  ("norm_mlp", norm_mlp), ("mlstm_conv_b", mlstm_conv_b), ("mlstm_norm", mlstm_norm),
                                  ("gla_norm", gla_norm), ("hgrn_norm", hgrn_norm), ("gla_b_a", gla_b_a),
                                  ("s5_b_glu", s5_b_glu)):
                    n = src.shape[1] // P
                    sp.dma_start(stage[PROW[name]:PROW[name] + n, :],
                                 src[l].rearrange("(a b) -> a b", b=P)).then_inc(p_rows, 16)
                sp.dma_start(stage[PROW["mlstm_conv_w"]:PROW["mlstm_conv_w"] + 16, :],
                             mlstm_conv_w[l].rearrange("k (a b) -> (k a) b", b=P)).then_inc(p_rows, 16)
                sp.dma_start(stage[PROW["s5_d"]:PROW["s5_d"] + 2, :],
                             s5_d[l].rearrange("(a g) h -> a (g h)", a=2)).then_inc(p_rows, 16)
                for name, src in (("s5_lam_re", s5_lam_re), ("s5_lam_im", s5_lam_im)):
                    sp.dma_start(stage[PROW[name]:PROW[name] + 8, :],
                                 src[l].rearrange("(t a) q -> t (a q)", a=2)).then_inc(p_rows, 16)
                for m in range(2):
                    sp.dma_start(stage[PROW[f"lb{m}"]:PROW[f"lb{m}"] + 2, :],
                                 hgrn_lb_logits[m].rearrange("(a b) -> a b", b=P)).then_inc(p_rows, 16)
                sp.dma_start(stage[PROW["norm_final"]:PROW["norm_final"] + 8, :],
                             norm_final.rearrange("(a b) -> a b", b=P)).then_inc(p_rows, 16)
                r = PROW["if_bias"]
                sp.dma_start(stage[r:r + 1, 0:4], mlstm_i_bias[l:l + 1, :]).then_inc(p_rows, 16)
                sp.dma_start(stage[r:r + 1, 32:36], mlstm_f_bias[l:l + 1, :]).then_inc(p_rows, 16)
                for a in range(2):
                    src = s5_log_step[l].rearrange("(t a) -> a t", a=2)[a:a + 1, :]
                    sp.dma_start(SM[64 * a:64 * a + 64, 16 + 8 * l:24 + 8 * l],
                                 src.to_broadcast([64, 8]), allow_slow_non_contiguous=True).then_inc(p_rows, 16)
            sp.wait_ge(p_vec, 3)
            sp.dma_start(mem_scratch, Rf(28, 4)).then_inc(p_out, 16)
            sp.wait_ge(p_out, 16)
            sp.wait_ge(layer_go, 1)

            with sp.Fori(0, DEPTH) as L:
                for n, (name, w, to) in enumerate((("m_i", 4, 0), ("m_f", 4, 32), ("g_a", 16, 64))):
                    sp.dma_start(WSM[:, :, to:to + w],
                                 w_in[L].rearrange("(k p) c -> p k c", p=P)[:, :, COL[name]:COL[name] + w],
                                 allow_slow_non_contiguous=True).then_inc(params_in, 16)
                sp.dma_start(WA2[:, :], gla_w_a2[L]).then_inc(params_in, 16)
                for r, (b, c) in enumerate(((s5_b_re, s5_c_re), (s5_b_im, s5_c_im))):
                    sp.dma_start(BRI[:, r, :, :], b[L].rearrange("(t a) q h -> (a q) t h", a=2)).then_inc(params_in, 16)
                    sp.dma_start(CRI[:, r, :, :], c[L].rearrange("(f g) h q -> (g h) f q", f=2)).then_inc(params_in, 16)

                for u, (name, part) in enumerate(UNITS):
                    row = 0 if part == "first" else D // 2

                    def rows(src, c, r0=0):
                        return src[r0 + row:r0 + row + D // 2, c:c + BW]

                    if name.startswith("branch"):
                        b, c = int(name[6]), int(name[8])
                        src = w_branch[L][b, :, c * BW:(c + 1) * BW]
                    elif name == "g_qk":
                        src = rows(w_in[L], COL["g_q"])
                    elif name in COL:
                        src = rows(w_in[L], COL[name])
                    elif name.startswith("gate"):
                        src = rows(w_in[L], COL["gates"] + int(name[4]) * D + int(name[6]) * BW)
                    elif name.startswith("out"):
                        src = rows(w_out[L], int(name[3]) * BW)
                    elif name.startswith("kv"):
                        src = rows(xattn_w_kv[L], int(name[2]) * BW)
                    elif name.startswith("q"):
                        src = rows(xattn_w_q[L], int(name[1]) * BW)
                    elif name.startswith("o"):
                        src = rows(xattn_w_o[L], int(name[1]) * BW)
                    elif name.startswith("up"):
                        src = rows(mlp_w1[L], (4 * int(name[2]) + int(name[4])) * BW)
                    else:
                        src = rows(mlp_w2[L], int(name[6]) * BW, int(name[4]) * D)
                    k = 2 if name.startswith("branch") else 4
                    if u >= RAW:
                        sp.wait_ge(split_ready, u - RAW + 1)
                    sp.dma_start(WR[:, u % RAW, 0:k * BW].rearrange("p (k c) -> p k c", k=k),
                                 src.rearrange("(k p) c -> p k c", p=P)).then_inc(raw_in[u % RAW], 16)
                    if name == "branch0_3":
                        sp.wait_ge(ss["w_done"], 1)
                        sp.dma_start(WGLU, s5_w_glu[L].rearrange("(k p) c -> p k c", p=P)).then_inc(ss["wglu_in"], 16)
                    if name == "branch2_1":
                        sp.wait_ge(at["base_free"], 1)
                        sp.dma_start(Rf(28, 4), mem_scratch).then_inc(at["mem_base_in"], 16)
                sp.wait_ge(layer_end, 4 * L + 4)
                sp.sem_inc(all_ended, 1)
                sp.wait_ge(params_in, 16 * 8)
                sp.wait_ge(all_ended, 1)
                nums = sorted(s.num for s in layer_sems)
                assert nums == list(range(nums[0], nums[-1] + 1))
                sp.sem_clear(range(nums[0], nums[-1] + 1)).then_inc(layer_go, 1)
            sp.wait_ge(f_vec, 1)
            for t in range(TT):
                sp.wait_ge(f_vec, 1 + 2 * (t + 1))
                sp.dma_start(out[0, t * P:(t + 1) * P, :], flat(R(2 * t, 2))).then_inc(p_out, 16)
            sp.wait_ge(p_out, 16 + 16 * TT)

        @block.gpsimd
        def _(pool):
            pool.wait_ge(layer_go, 1)
            with pool.Fori(0, DEPTH) as L:
                for u, (name, part) in enumerate(UNITS):
                    pool.wait_ge(raw_in[u % RAW], 16 * (u // RAW + 1))
                    if BEFORE[u] is not None:
                        before, its_part = UNITS[BEFORE[u]]
                        if its_part == "first":
                            pool.wait_ge(split_used, FIRSTS[BEFORE[u]])
                        else:
                            bank_set, used = psum_set(before)
                            pool.wait_ge(gemm_done[bank_set], 2 * used + 2)
                    w = 2 * BW if name.startswith("branch") else 4 * BW
                    raw = WR[:, u % RAW, 0:w]
                    hi, lo = (part_[:, SLOT[u] * 4 * BW:SLOT[u] * 4 * BW + w] for part_ in (WHi, WLo))
                    pool.tensor_tensor(hi, raw, SM[:, 62:63].to_broadcast([P, w]), ALU.mult).then_inc(split_hi, 1)
                    pool.wait_ge(split_hi, u + 1)
                    pool.tensor_tensor(lo, raw, hi.bitcast(F32), ALU.subtract).then_inc(split_ready, 1)
                pool.wait_ge(split_ready, NUNIT)
                pool.nop().then_inc(layer_end, 1)
                pool.wait_ge(layer_go, L + 2)

        @block.tensor
        def _(pe):
            def mm(o, w, a, start=True, stop=True):
                return pe.matmul(o, w, a, start=start, stop=stop, skip_group_check=True)

            pe.wait_ge(p_dma, 64)
            for n in range(8):
                if n >= 4:
                    pe.wait_ge(p_act, 5 + n - 4)
                for t in range(TT):
                    i = pe.transpose(M[n % 4][:, t * P:(t + 1) * P], Rf(2 * t + n // 4, 1)[:, (n % 4) * P:(n % 4 + 1) * P], ident)
                i.then_inc(p_pe, 1)
            pe.wait_ge(p_act, 12)
            pe.wait_ge(p_vec, 2)
            for n in range(4):
                for k in range(2):
                    for t in range(2):
                        kc = 2 * n + k
                        i = pe.transpose(M[n][:, k * 256 + t * P:k * 256 + (t + 1) * P],
                                         Rf(8 + 2 * t + kc // 4, 1)[:, (kc % 4) * P:(kc % 4 + 1) * P], ident)
                i.then_inc(p_pe, 1)
            pe.wait_ge(p_rows, 16 * 21 * DEPTH)
            for l in range(DEPTH):
                i = pe.transpose(G[0][l][:, 0:P], Rf(20 + l, 1)[:, 0:P], ident)
            i.then_inc(p_pe, 1)
            pe.wait_ge(layer_go, 1)

            def gemm(name, hi, lo, kind="fm", n=SEQ, ready=None, ready_at=0, kcs=4):
                s, used = psum_set(name)
                if used:
                    pe.wait_ge(gemm_free[s], 2 * used)
                u0, units = UNIT[name], (1 if name.startswith("branch") else 2)
                for un in range(units):
                    u = u0 + un
                    w_at = lambda W, k, c, m: W[:, (4 * SLOT[u] + k) * BW + c:(4 * SLOT[u] + k) * BW + c + m]
                    nt = 2 if kind == "fm" else n // P
                    first = True
                    for reg in range(nt):
                        for k in range(kcs):
                            kc = kcs * un + k
                            if ready is not None and reg == 0:
                                pe.wait_ge(ready, ready_at + kc + 1)
                            if first:
                                pe.wait_ge(split_ready, u + 1)
                                first = False
                            last = kc == kcs * units - 1
                            if kind == "fm":
                                o = G[s][reg][:, 0:n]
                                ops = ((w_at(WHi, k, reg * P, P), hi(kc)), (w_at(WHi, k, reg * P, P), lo(kc)),
                                       (w_at(WLo, k, reg * P, P), hi(kc)))
                                start = kc == 0
                                ends = last
                            else:
                                per = 2 if nt == 4 else 1
                                o = G[s][reg // per][:, (reg % per) * BW:(reg % per) * BW + BW]
                                tok = slice(reg * P, reg * P + P)
                                ops = ((hi(kc)[:, tok], w_at(WHi, k, 0, BW)), (lo(kc)[:, tok], w_at(WHi, k, 0, BW)),
                                       (hi(kc)[:, tok], w_at(WLo, k, 0, BW)))
                                start = kc == 0 and reg % per == 0
                                ends = last and reg % per == per - 1
                            for q, (a, b) in enumerate(ops):
                                i = mm(o, a, b, start=start and q == 0, stop=last and q == 2)
                            if ends:
                                i.then_inc(gemm_done[s], 1)
                    if un < units - 1:
                        i.then_inc(split_used, 1)

            def norm(base, bank):
                for k in range(KC):
                    pe.wait_ge(sq_ready, base + k + 1)
                    i = mm(bank[:, :], mean_w, TH[:, k % 2, :], start=k == 0, stop=k == KC - 1)
                    i.then_inc(sq_used if k < KC - 1 else ms_done, 1)

            def scores(m, l):
                if l == 0:
                    pe.wait_ge(m.kq_ready, 3 - m.J)
                    if m.J == 2:
                        pe.wait_ge(m.g_ready, 5)
                    else:
                        pe.wait_ge(head_rs, 4)
                else:
                    pe.wait_ge(m.x_ready, l)
                if m.J == 2 and l >= 2:
                    pe.wait_ge(m.picked, 2 * (l - 1))
                if m.J == 1 and l >= 1:
                    pe.wait_ge(m.picked, 4 * l)
                kk, qq = (m.K, m.Q) if l == 0 else (m.X[l % 2], m.X[l % 2])
                for h in range(4):
                    rows = slice(m.dk * (h % m.per), m.dk * (h % m.per) + m.dk)
                    base = (h // m.per) * SEQ
                    for c in range(NCH):
                        at_ = m.score_cols(h) + (c // 2) * CH
                        tok = slice(base + c * CH, base + c * CH + CH)
                        i = mm(m.score_bank(l, h)[64 * (c % 2):64 * (c % 2) + 64, at_:at_ + CH], kk[rows, tok], qq[rows, tok])
                i.then_inc(m.lev_done, 1)

            def state_in(m):
                pe.wait_ge(m.kd_ready, 1)
                pe.wait_ge(m.picked, 2 * 7 if m.J == 2 else 4 * 7)
                for j in range(m.J):
                    for t in range(TT):
                        i = pe.transpose(M[j][:, t * P:(t + 1) * P], m.E[0][:, j * SEQ + t * P:j * SEQ + (t + 1) * P], ident)
                    i.then_inc(m.kt_done, 1)
                pe.wait_ge(m.kt_ready, m.J)
                pe.wait_ge(m.v_ready, 2)
                for h in range(4):
                    r0 = m.dk * (h % m.per)
                    for c in range(NCH):
                        p0 = 64 * (c % 2)
                        at_ = (h // m.per) * 256 + (c // 2) * HD
                        i = mm(M[2 + c % 2][r0:r0 + m.dk, at_:at_ + HD], m.KT[p0:p0 + 64, c // 2, m.dk * h:m.dk * h + m.dk],
                               m.V[p0:p0 + 64, c // 2, HD * h:HD * h + HD])
                i.then_inc(m.kv_done, 1)

            def outputs(m):
                pe.wait_ge(m.bd_ready, 1)
                pe.wait_ge(m.s_ready, 2)
                for h in range(4):
                    rows = slice(64 * (h % 2), 64 * (h % 2) + 64)
                    j, jt = h // 2, h // m.per
                    for t in range(TT):
                        mm(M[j][rows, t * P:(t + 1) * P], m.V[:, t, HD * h:HD * h + HD], m.attbd[:, m.slot(h), t, :], stop=False)
                        for c in (2 * t, 2 * t + 1):
                            if c:
                                i = mm(M[j][rows, c * CH:(c + 1) * CH], m.S[:, jt, c - 1, HD * (h % m.per):HD * (h % m.per) + HD],
                                       m.Q[:, jt * SEQ + c * CH:jt * SEQ + (c + 1) * CH], start=False, stop=True)
                    if h % 2:
                        i.then_inc(m.o_done, 1)

            def head_norm(n, sq):
                for j in range(2):
                    pe.wait_ge(head_sq, 2 * n + j + 1)
                    mm(M[2 + j][:, :], head_mean, sq[:, j, :]).then_inc(head_ms, 1)

            H = (lambda k: Hhi[:, k, :], lambda k: Hlo[:, k, :])

            def gate_gemm(n, c):
                gemm(f"gate{n}_{c}", *H)

            def branch_gemm(n, c):
                if c == 0:
                    pe.wait_ge(y_ready, 2 * BRANCH_NO[n] + 2)
                y = YB[BRANCH_AT[n]]
                gemm(f"branch{n}_{c}", lambda k: y[0][:, k, :], lambda k: y[1][:, k, :], kcs=2)

            with pe.Fori(0, DEPTH) as L:
                norm(0, M[3])
                gemm("r_f", *H, ready=h_ready)
                gemm("r_q", *H)
                gemm("r_i", *H, kind="tm")
                gemm("g_qk", *H)
                scores(hg, 0)
                pe.wait_ge(params_in, 16 * 8)
                pe.wait_ge(rstd_ready, 2)
                k = 0
                for kc in range(KC):
                    for part in (Hhi, Hlo):
                        i = mm(M[3][0:80, :], WSM[:, kc, :], part[:, kc, :].bitcast(F32), start=k == 0, stop=k == 15)
                        k += 1
                i.then_inc(small_done, 1)
                gemm("g_v", *H, kind="tm")
                pe.wait_ge(ga_ready, 3)
                mm(M[2][:, :], WA2[:, :], R(32)[0:RANK, 0, :]).then_inc(ga_done, 1)
                gemm("g_r", *H)
                pe.wait_ge(gl.gate_in, 2)
                scores(hg, 1)
                scores(hg, 2)
                scores(hg, 3)
                gemm("r_g", *H)
                scores(hg, 4)
                scores(hg, 5)
                scores(hg, 6)
                state_in(hg)
                gate_gemm(3, 0)
                outputs(hg)
                head_norm(0, hg.SQ)
                gemm("m_q", *H)
                gemm("m_k", *H)
                scores(gl, 0)
                gemm("m_v", *H, kind="tm")
                scores(gl, 1)
                gemm("m_o", *H)
                scores(gl, 2)
                branch_gemm(3, 0)
                scores(gl, 3)
                gate_gemm(3, 1)
                scores(gl, 4)
                branch_gemm(3, 1)
                scores(gl, 5)
                gate_gemm(3, 2)
                scores(gl, 6)
                branch_gemm(3, 2)
                state_in(gl)
                gate_gemm(3, 3)
                branch_gemm(3, 3)
                outputs(gl)
                head_norm(1, gl.SQ)
                gemm("s_u", *H)
                gate_gemm(1, 0)

                pe.wait_ge(ms["stack_ready"], 1)
                for t in range(TT):
                    i = pe.transpose(M[0][:, t * 64:(t + 1) * 64], R(23)[0:64, 0, t * P:(t + 1) * P], ident[0:64, 0:64])
                i.then_inc(ms["aw_done"], 1)
                pe.wait_ge(head_rs, 8)
                for j in range(2):
                    mm(M[1 + j][:, :], pair_sel[0:4, j, :], R(24)[0:4, 0, :]).then_inc(ms["ib_done"], 1)
                pe.wait_ge(ms["aw_ready"], 1)
                for j in range(2):
                    mm(M[3 if j == 0 else 0][:, :], pair_sel[0:4, j, :], R(28)[0:4, 0, :]).then_inc(ms["ib_done"], 1)
                branch_gemm(1, 0)
                gate_gemm(1, 1)
                pe.wait_ge(ms["ib_ready"], 4)
                pe.wait_ge(ms["emb_ready"], 2)
                bm = R(22)[0:4, 0, :].rearrange("p (t a c) -> p t a c", a=2, c=CH)
                for hp in range(2):
                    mm(M[hp][:, :], ident, bc(neg_mask, 1, 8), stop=False)
                    for j in range(2):
                        for a in range(2):
                            i = mm(M[hp][64 * a:64 * a + 64, j * 256:j * 256 + 256], head_sel[0:4, 2 * j + hp, :], bm[:, :, a, :],
                                   start=False, stop=j == 1)
                    i.then_inc(ms["mex_done"], 1)
                for h in range(4):
                    rows = slice(64 * (h % 2), 64 * (h % 2) + 64)
                    for c in range(NCH):
                        tok = slice(c * CH, c * CH + CH)
                        at_ = (h // 2) * 256 + (c // 2) * CH
                        i = mm(M[2 + h % 2][64 * (c % 2):64 * (c % 2) + 64, at_:at_ + CH], MQK[2 + h // 2][rows, tok], MQK[h // 2][rows, tok])
                i.then_inc(ms["mqk_done"], 1)
                branch_gemm(1, 1)
                pe.wait_ge(ms["mex_v"], 2)
                for j in range(2):
                    for t in range(TT):
                        i = pe.transpose(M[j][:, t * P:(t + 1) * P], MQK[2 + j][:, t * P:(t + 1) * P], ident)
                    i.then_inc(ms["mkt_done"], 1)
                gate_gemm(1, 2)
                pe.wait_ge(ms["mkt_ready"], 2)
                pe.wait_ge(ms["matt_ready"], 2)
                pe.wait_ge(ms["mv_ready"], 2)
                for h in range(4):
                    rows = slice(64 * (h % 2), 64 * (h % 2) + 64)
                    for c in range(NCH):
                        p0 = 64 * (c % 2)
                        bank = M[2 * (c % 2) + h // 2]
                        at_ = (c // 2) * 128
                        w = MKT[p0:p0 + 64, c // 2, h // 2, h % 2, :]
                        mm(bank[rows, at_:at_ + 64], w, MV[p0:p0 + 64, c // 2, HD * h:HD * h + HD])
                        i = mm(bank[rows, at_ + 64:at_ + 128], w, ones64[p0:p0 + 64, :])
                i.then_inc(ms["mkv_done"], 1)
                branch_gemm(1, 2)
                gate_gemm(1, 3)
                pe.wait_ge(ms["mbd_ready"], 1)
                pe.wait_ge(ms["ms_ready"], 2)
                for h in range(4):
                    rows = slice(64 * (h % 2), 64 * (h % 2) + 64)
                    j, hp = h // 2, h % 2
                    for part in range(2):
                        bank = M[2 * part + j]
                        for t in range(TT):
                            w = MV[:, t, HD * h:HD * h + HD] if part == 0 else ones64
                            i = mm(bank[rows, t * P:(t + 1) * P], w, MBD[:, hp * 2 + j, t, :], stop=False)
                            for c in (2 * t, 2 * t + 1):
                                if c:
                                    i = mm(bank[rows, c * CH:(c + 1) * CH], MS[j][:, c - 1, hp, 64 * part:64 * part + 64],
                                           MQT[:, j, c * CH:(c + 1) * CH], start=False, stop=True)
                i.then_inc(ms["mo_done"], 1)
                branch_gemm(1, 3)
                gate_gemm(0, 0)
                head_norm(2, MSQ)

                branch_gemm(0, 0)
                gate_gemm(0, 1)
                pe.wait_ge(ss["cp_ready"], 2)
                for r in range(2):
                    for f in range(2):
                        i = pe.transpose(M[0][:, (2 * r + f) * P:(2 * r + f + 1) * P], R(24 + r)[:, 0, f * P:(f + 1) * P], ident)
                i.then_inc(ss["ct_done"], 1)
                pe.wait_ge(ss["xp_ready"], 1)
                n = 0
                pe.wait_ge(head_rs, 12)
                for f in range(2):
                    for r in range(2):
                        for q in range(2):
                            if n >= 3:
                                pe.wait_ge(ss["bt_ready"], n - 2)
                            for uu in range(4):
                                i = pe.transpose(M[1 + n % 3][:, uu * P:(uu + 1) * P],
                                                 XP[:, r, 4 * q + uu, 4 * f:4 * f + 4, :], ident)
                            i.then_inc(ss["bt_done"], 1)
                            n += 1
                pe.wait_ge(ss["cp_ready"], 3)
                kk = M[0][:, :].rearrange("p (f u c) -> p f u c", f=2, u=8)
                for f in range(2):
                    for u in range(8):
                        for i4 in range(4):
                            t = 4 * f + i4
                            for r in range(2):
                                i = mm(kk[32 * i4:32 * i4 + 32, f, u, :], XP[:, r, u, t, :], CT[:, r, 32 * t:32 * t + 32],
                                       start=r == 0, stop=r == 1)
                i.then_inc(ss["kk_done"], 1)
                branch_gemm(0, 1)
                gate_gemm(0, 2)
                pe.wait_ge(ss["u_ready"], 2)
                pe.wait_ge(ss["bt_ready"], 8)
                pe.wait_ge(ss["kk_ready"], 4)
                un = UU[:, :, :].rearrange("p f (n j) -> p f n j", j=S5_T)
                for i4 in range(4):
                    rows = slice(32 * i4, 32 * i4 + 32)
                    for f in range(2):
                        for r in range(2):
                            for j in range(S5_T):
                                i = mm(M[i4][:, (2 * f + r) * 64:(2 * f + r) * 64 + 64], BT[rows, f, r, S5_T - 1 - j, :],
                                       un[rows, f, :, j], start=j == 0, stop=j == S5_T - 1)
                i.then_inc(ss["w_done"], 1)
                branch_gemm(0, 2)
                gate_gemm(0, 3)
                branch_gemm(0, 3)
                pe.wait_ge(ss["cl_ready"], 1)
                pe.wait_ge(ss["x_ready"], 1)
                for f in range(2):
                    for j in range(S5_T):
                        for i_ in range(j + 1):
                            i = mm(M[f][:, j * 64:j * 64 + 64], KTm[:, f, j - i_, :], un[:, f, :, i_], start=i_ == 0, stop=False)
                        for i4 in range(4):
                            t = 4 * f + i4
                            for r in range(2):
                                i = mm(M[f][32 * i4:32 * i4 + 32, j * 64 + 1:j * 64 + 64], CL[:, r, j, t, :], SX[r][:, t, 0:63],
                                       start=False, stop=r == 1)
                    i.then_inc(ss["y_done"], 1)
                gate_gemm(2, 0)
                pe.wait_ge(ss["wglu_in"], 16)
                pe.wait_ge(ss["ge_ready"], 2)
                for n in range(4):
                    for k in range(2):
                        i = mm(M[n][:, :], WGLU[:, k, n * P:(n + 1) * P], GE[:, k, :], start=k == 0, stop=k == 1)
                    i.then_inc(ss["glu_done"], 1)
                gate_gemm(2, 1)
                branch_gemm(2, 0)
                branch_gemm(2, 1)
                for c in (2, 3):
                    gate_gemm(2, c)
                    branch_gemm(2, c)

                for c in range(4):
                    gemm(f"out{c}", lambda k: MHhi[:, k, :], lambda k: MHlo[:, k, :], ready=mgs_ready if c == 0 else None)
                mmin = (lambda k: MMhi[:, k, :], lambda k: MMlo[:, k, :])
                gemm("kv0", *mmin, n=MEM, ready=at["mm_ready"])
                gemm("kv1", *mmin, n=MEM)
                norm(8, M[3])
                for c in range(2, 4):
                    gemm(f"kv{c}", *mmin, n=MEM)
                for c in range(4):
                    gemm(f"q{c}", *H, ready=h_ready if c == 0 else None, ready_at=8)
                    gemm(f"kv{4 + c}", *mmin, kind="tm", n=MEM)
                pe.wait_ge(at["q_ready"], 8)
                pe.wait_ge(at["kt_ready"], 8)
                pe.wait_ge(at["vm_ready"], 8)
                pe.wait_ge(rstd_ready, 4)

                def attn_scores(h):
                    if h:
                        pe.wait_ge(at["p_exp"], 4 * h)
                    for t in range(TT):
                        for k in range(2):
                            i = mm(M[t // 2][:, (t % 2) * 256:(t % 2) * 256 + 256], MG[:, 2 * h + k, t * P:(t + 1) * P],
                                   KTt[:, 2 * h + k, :], start=k == 0, stop=k == 1)
                    i.then_inc(at["sc_done"], 1)

                def attn_out(h):
                    pe.wait_ge(at["p_ready"], 4 * h + 4)
                    if h:
                        pe.wait_ge(at["oc_ready"], 2 * h)
                    for m in range(2):
                        for t in range(TT):
                            i = pe.transpose(M[2 + m][:, t * P:(t + 1) * P], PB[h % 2][:, t, m * P:(m + 1) * P], ident)
                        i.then_inc(at["pt_done"], 1)
                    pe.wait_ge(at["pt_ready"], 2 * h + 2)
                    for k in range(2):
                        for m in range(2):
                            i = mm(M[2 + k][:, :], VM[:, m, h * 256 + k * P:h * 256 + (k + 1) * P], PTB[h % 2][:, m, :],
                                   start=m == 0, stop=m == 1)
                        i.then_inc(at["o_done"], 1)

                attn_scores(0)
                for h in range(4):
                    if h < 3:
                        attn_scores(h + 1)
                    attn_out(h)
                for c in range(4):
                    gemm(f"o{c}", *H, ready=at["osplit_ready"] if c == 0 else None)
                norm(16, M[3])
                done = 0
                for q in (0, 1):
                    for c in range(4):
                        gemm(f"up{q}_{c}", *H, ready=h_ready if (q, c) == (0, 0) else None, ready_at=16)

                def down(q):
                    hb = MHID[q % 2]
                    for c in range(4):
                        gemm(f"down{q}_{c}", lambda k: hb[0][:, k, :], lambda k: hb[1][:, k, :],
                             ready=uplo if c == 0 else None, ready_at=8 * q)

                down(0)
                for c in range(4):
                    gemm(f"up2_{c}", *H)
                down(1)
                for c in range(4):
                    gemm(f"up3_{c}", *H)
                down(2)
                down(3)
                pe.nop().then_inc(layer_end, 1)
                pe.wait_ge(layer_go, L + 2)

            for k in range(KC):
                pe.wait_ge(f_act, k + 1)
                i = mm(M[3][:, :], mean_w, R(8 + k)[:, 0, :], start=k == 0, stop=k == KC - 1)
            i.then_inc(f_pe, 1)
            pe.wait_ge(f_vec, 1)
            for t in range(TT):
                if t:
                    pe.wait_ge(f_vec, 1 + 2 * t)
                for k in range(KC):
                    i = pe.transpose(G[0][k // 4][:, (k % 4) * P:(k % 4 + 1) * P], MG[:, k, t * P:(t + 1) * P], ident)
                i.then_inc(f_pe, 1)

        @block.scalar
        def _(act):
            do = chained(act, a_chain)
            def pdo(ins, n=[0]):
                n[0] += 1
                ins.then_inc(p_act, 1)
                act.wait_ge(p_act, n[0])
            act.wait_ge(p_dma, 64)
            act.preload_act_table_set(LOG_SET)
            for t in range(2):
                pdo(act.activation(flat(R(12 + 2 * t, 2)), flat(R(8 + 2 * t, 2)), ACT.Square, accum_out=SM[:, 40 + t:41 + t]))
            act.wait_ge(p_vec, 1)
            pdo(act.activation(SM[:, 42:44], SM[:, 40:42], ACT.Ln, scale=1.0 / D, bias=SM[:, 63:64]))
            pdo(act.activation(SM[:, 44:46], SM[:, 42:44], ACT.Exp, scale=-0.5))
            for n in range(8):
                act.wait_ge(p_pe, n + 1)
                pdo(act.activation(X[:, n, :], M[n % 4][:, :], ACT.Copy))
            for n in range(4):
                act.wait_ge(p_pe, 9 + n)
                pdo(act.activation(R(28 + n)[:, 0, :], M[n][:, :], ACT.Copy))
            act.wait_ge(p_vec, 4)
            pdo(act.activation(PS[:, 0:2, 0:2], PS[:, 0:2, 0:2], ACT.Abs))
            pdo(act.activation(PS[:, 0:2, 0:2], PS[:, 0:2, 0:2], ACT.Exp, scale=-1.0))
            pdo(act.activation(PS[:, 0:2, 0:2], PS[:, 0:2, 0:2], ACT.Ln, bias=SM[:, 62:63]))
            act.wait_ge(layer_go, 1)
            eps, one = SM[:, 63:64], SM[:, 62:63]

            def norm(base, rstd):
                for k in range(KC):
                    if k >= 2:
                        act.wait_ge(sq_used, (base // 8) * 7 + k - 1)
                    if base:
                        act.wait_ge(x_ready, base // 8 * 8 - 8 + k + 1)
                    do(act.activation(TH[:, k % 2, :], X[:, k, :], ACT.Square), sq_ready)
                act.wait_ge(ms_done, base // 8 + 1)
                act.preload_act_table_set(LOG_SET)
                do(act.activation(rstd, M[3][:, :], ACT.Ln, bias=eps), rstd_ready)
                do(act.activation(rstd, rstd, ACT.Exp, scale=-0.5), rstd_ready)
                for k in range(KC):
                    act.wait_ge(hx_ready, base + k + 1)
                    do(act.activation(Hhi[:, k, :], TH[:, k % 2, :], ACT.Copy), hi_ready)

            def banks(name):
                s, used = psum_set(name)
                for b in range(2):
                    act.wait_ge(gemm_done[s], 2 * used + b + 1)
                    yield b, G[s][b], gemm_free[s]

            th_n = [0]

            def tanh_out(name):
                s, used = psum_set(name)
                for b in range(2):
                    act.wait_ge(gemm_done[s], 2 * used + b + 1)
                    if th_n[0] >= 2:
                        act.wait_ge(th_used, th_n[0] - 1)
                    do(act.activation(TH[:, b, :], G[s][b][:, :], ACT.Tanh, scale=0.5), th_ready)
                    th_n[0] += 1

            def gate(n, c):
                s, used = psum_set(f"gate{n}_{c}")
                for b in range(2):
                    act.wait_ge(gemm_done[s], 2 * used + b + 1)
                    act.wait_ge(th_used, th_n[0] - 1)
                    do(act.activation(TH[:, b, :], G[s][b][:, :], ACT.Tanh, scale=0.5), th_ready)
                    act.nop().then_inc(gemm_free[s], 1)
                    th_n[0] += 1

            def level_exp(m, l):
                act.wait_ge(m.d_ready, 2 * l)
                do(act.activation(m.E[l % 2], m.E[l % 2], ACT.Exp, scale=m.gscale), m.e_ready)

            def decays(m):
                act.wait_ge(m.d_ready, 13)
                do(act.activation(m.E[0], m.E[0], ACT.Exp, scale=m.gscale), m.e_ready)
                do(act.activation(m.E[1], m.Gc, ACT.Exp, scale=m.gscale), m.e_ready)

            def kt_copy(m):
                for j in range(m.J):
                    act.wait_ge(m.kt_done, j + 1)
                    do(act.activation(m.KT[:, :, j * P:(j + 1) * P], M[j][:, :].rearrange("p (t c) -> p t c", t=TT), ACT.Copy), m.kt_ready)

            def head_out(m):
                for j in range(2):
                    act.wait_ge(m.o_done, j + 1)
                    do(act.activation(m.O[:, j, :], M[j][:, :], ACT.Copy, scale=m.oscale))
                    do(act.activation(m.SQ[:, j, :], M[j][:, :], ACT.Square, scale=m.oscale), head_sq)

            def head_rstd(n, sq):
                act.preload_act_table_set(LOG_SET)
                for j in range(2):
                    act.wait_ge(head_ms, 2 * n + j + 1)
                    do(act.activation(sq[:, j, :], M[2 + j][:, :], ACT.Ln, bias=eps), head_rs)
                    do(act.activation(sq[:, j, :], sq[:, j, :], ACT.Exp, scale=-0.5), head_rs)

            def y_split(n):
                no = BRANCH_NO[n]
                for j in range(2):
                    act.wait_ge(y_act, 2 * no + j + 1)
                    do(act.activation(YB[BRANCH_AT[n]][0][:, j, :], YSRC[n][:, j, :], ACT.Copy, scale=0.5), y_hi)

            YSRC = {3: hg.O, 1: gl.O, 0: MOO, 2: YS}

            with act.Fori(0, DEPTH) as L:
                norm(0, R(32)[:, 0, :])
                for b, bank, free in banks("r_f"):
                    do(act.activation(hg.E[0][:, b * SEQ:(b + 1) * SEQ], bank[:, :], ACT.Copy), hg.gate_in)
                    do(act.activation(hg.E[1][:, b * SEQ:(b + 1) * SEQ], bank[:, :], ACT.Abs))
                    act.nop().then_inc(free, 1)
                do(act.activation(hg.E[1], hg.E[1], ACT.Exp, scale=-1.0))
                do(act.activation(hg.E[1], hg.E[1], ACT.Ln, bias=one), hg.gate_in)
                act.wait_ge(hg.g_ready, 4)
                for j in range(2):
                    do(act.activation(hg.K[:, j * SEQ:(j + 1) * SEQ], hg.K[:, j * SEQ:(j + 1) * SEQ], ACT.Exp, bias=col("hg_c1", j)),
                       hg.kq_ready if j else None)
                do(act.activation(hg.X[1], hg.X[1], ACT.Abs))
                do(act.activation(hg.X[1], hg.X[1], ACT.Exp, scale=-1.0))
                do(act.activation(hg.X[1], hg.X[1], ACT.Ln, bias=one), hg.gate_in)
                tanh_out("r_q")
                for b, bank, free in banks("r_i"):
                    do(act.activation(hg.V[:, 2 * b:2 * b + 2, :], bank[:, :].rearrange("p (t c) -> p t c", t=2), ACT.Copy), hg.v_ready)
                    act.nop().then_inc(free, 1)
                for b, bank, free in banks("g_qk"):
                    do(act.activation(gl.Q if b == 0 else gl.K, bank[:, :], ACT.Copy), gl.kq_ready)
                    act.nop().then_inc(free, 1)
                def ps(n, w=1):
                    return PS[:, n:n + w, :]
                act.wait_ge(hx_ready, 1)
                do(act.activation(PS[:, 0, :], PT[:, PROW["step"]:PROW["step"] + 8], ACT.Exp), ss["sin_in"])
                act.wait_ge(ss["prm"], 1)
                for n in range(9):
                    do(act.activation(PS[:, 8 + n, :], PS[:, 1, :], ACT.Exp, scale=float(n)))
                do(act.activation(PS[:, 3, :], PS[:, 2, :], ACT.Abs))
                do(act.activation(PS[:, 4, :], PS[:, 2, :], ACT.Sin), ss["sin_in"])
                do(act.activation(PS[:, 3, :], PS[:, 3, :], ACT.Sin, scale=-1.0, bias=SM[:, 61:62]), ss["sin_ready"])
                act.wait_ge(small_done, 1)
                do(act.activation(LP[0:4, :], M[3][0:4, :], ACT.Identity, bias=colr("if_bias", 0, slice(0, 4))))
                do(act.activation(LP[32:36, :], M[3][32:36, :], ACT.Identity, bias=colr("if_bias", 0, slice(32, 36))), rows_ready)
                act.wait_ge(h_ready, 8)
                do(act.activation(R(32)[0:RANK, 0, :], M[3][64:80, :], ACT.Copy), ga_ready)
                act.wait_ge(hg.lev_done, 1)
                do(act.nop(), ga_ready)
                act.wait_ge(hg.picked, 2)
                do(act.nop(), ga_ready)
                for b, bank, free in banks("g_v"):
                    do(act.activation(gl.V[:, 2 * b:2 * b + 2, :], bank[:, :].rearrange("p (t c) -> p t c", t=2), ACT.Copy), gl.v_ready)
                    act.nop().then_inc(free, 1)
                act.wait_ge(ga_done, 1)
                do(act.activation(R(30)[:, 0, :], M[2][:, :], ACT.Identity, bias=col("gla_b_a")), gl.gate_in)
                do(act.activation(R(31)[:, 0, :], M[2][:, :], ACT.Abs, bias=col("gla_b_a")), gl.gate_in)
                do(act.activation(R(31)[:, 0, :], R(31)[:, 0, :], ACT.Exp, scale=-1.0))
                do(act.activation(R(31)[:, 0, :], R(31)[:, 0, :], ACT.Ln, bias=one), gl.gate_in)
                level_exp(hg, 1)
                level_exp(hg, 2)
                tanh_out("g_r")
                level_exp(hg, 3)
                level_exp(hg, 4)
                tanh_out("r_g")
                level_exp(hg, 5)
                level_exp(hg, 6)
                decays(hg)
                kt_copy(hg)
                gate(3, 0)
                head_out(hg)
                head_rstd(0, hg.SQ)
                for name, j0 in (("m_q", 0), ("m_k", 2)):
                    for b, bank, free in banks(name):
                        do(act.activation(CIN[:, j0 + b, 3:515], bank[:, :], ACT.Copy), ms["cin_ready"])
                        act.nop().then_inc(free, 1)
                y_split(3)
                level_exp(gl, 1)
                for b, bank, free in banks("m_v"):
                    do(act.activation(MV[:, 2 * b:2 * b + 2, :], bank[:, :].rearrange("p (t c) -> p t c", t=2), ACT.Copy), ms["mv_ready"])
                    act.nop().then_inc(free, 1)
                level_exp(gl, 2)
                for b, bank, free in banks("m_o"):
                    do(act.activation(MO[:, b, :], bank[:, :], ACT.Tanh, scale=0.5))
                    act.nop().then_inc(free, 1)
                level_exp(gl, 3)
                level_exp(gl, 4)
                gate(3, 1)
                level_exp(gl, 5)
                level_exp(gl, 6)
                for j in range(4):
                    act.wait_ge(ms["cv_ready"], j + 1)
                    do(act.activation(MTHG[j], MQK[j], ACT.Tanh, scale=0.5), ms["mth_ready"])
                gate(3, 2)
                decays(gl)
                kt_copy(gl)
                gate(3, 3)
                head_out(gl)
                head_rstd(1, gl.SQ)
                y_split(1)
                for b, bank, free in banks("s_u"):
                    act.wait_ge(y_ready, 4)
                    do(act.activation(UU[:, b, :], bank[:, :], ACT.Copy), ss["u_ready"])
                    act.nop().then_inc(free, 1)

                r32 = slice(32, 36)
                act.preload_act_table_set(LOG_SET)
                do(act.activation(R(18)[r32, 0, :], LP[r32, :], ACT.Abs))
                do(act.activation(R(18)[r32, 0, :], R(18)[r32, 0, :], ACT.Exp, scale=-1.0))
                do(act.activation(R(18)[r32, 0, :], R(18)[r32, 0, :], ACT.Ln, bias=SM[r32, 62:63]), ms["a1"])
                act.wait_ge(ms["v1"], 1)
                do(act.activation(R(19)[0:4, 0, :], R(18)[r32, 0, :], ACT.Copy), ms["a1"])
                act.wait_ge(ms["v1"], 2)
                do(act.activation(R(24)[0:4, 0, :], R(24)[0:4, 0, :], ACT.Exp))
                do(act.activation(R(23)[r32, 0, :], R(25)[0:4, 0, :], ACT.Exp))
                do(act.activation(R(28)[0:4, 0, :], R(21)[0:4, 0, :], ACT.Exp, scale=-1.0), ms["stack_ready"])
                gate(1, 0)
                act.wait_ge(ms["aw_done"], 1)
                do(act.activation(flat(MAW), M[0][:, 0:256], ACT.Copy), ms["aw_ready"])
                for j in range(2):
                    act.wait_ge(ms["ib_done"], 3 + j)
                    do(act.activation(MEM_E[:, j, :], M[3 if j == 0 else 0][:, :], ACT.Copy), ms["emb_ready"])
                gate(1, 1)
                act.wait_ge(ms["mex_v"], 2)
                do(act.activation(flat(MATT), flat(MATT), ACT.Exp), ms["mex_ready"])
                act.wait_ge(ms["matt_ready"], 2)
                av = MATT.rearrange("p b (j t c) -> p (b j) t c", j=2, t=TT)
                for a in range(2):
                    rows = slice(64 * a, 64 * a + 64)
                    do(act.activation(MBD[rows, :, :, 64 * a:64 * a + 64], av[rows], ACT.Copy))
                do(act.nop(), ms["mbd_ready"])
                gate(1, 2)
                gate(1, 3)
                for j in range(2):
                    act.wait_ge(ms["mo_done"], 1)
                    do(act.activation(MDA[:, j, :], M[2 + j][:, :], ACT.Abs, scale=MC), ms["mabs_ready"])
                gate(0, 0)
                for j in range(2):
                    act.wait_ge(ms["mh_ready"], j + 1)
                    do(act.activation(MSQ[:, j, :], MOO[:, j, :], ACT.Square), head_sq)
                head_rstd(2, MSQ)
                y_split(0)

                gate(0, 1)
                act.wait_ge(ss["ct_done"], 1)
                do(act.activation(flat(CT), M[0][:, :], ACT.Copy), ss["ct_ready"])
                n = 0
                for f in range(2):
                    for r in range(2):
                        for q in range(2):
                            act.wait_ge(ss["bt_done"], n + 1)
                            do(act.activation(BT[:, f, r, 4 * q:4 * q + 4, :], M[1 + n % 3][:, :].rearrange("p (u s) -> p u s", u=4), ACT.Copy),
                               ss["bt_ready"])
                            n += 1
                gate(0, 2)
                act.wait_ge(ss["w_done"], 1)
                act.wait_ge(ss["cl_ready"], 1)
                for i4 in range(4):
                    for r in range(2):
                        src = M[i4][:, 0:256].rearrange("p (f r n) -> p f r n", f=2, r=2)[:, :, r, :]
                        do(act.activation(SW[r][:, i4::4, :], src, ACT.Copy), ss["ct_ready"] if (i4, r) == (3, 1) else None)
                gate(0, 3)
                for f in range(2):
                    act.wait_ge(ss["ys_ready"], f + 1)
                    do(act.activation(GE[:, f, :], YS[:, f, :], ACT.Square), ss["sq"])
                for f in range(2):
                    act.wait_ge(ss["poly"], f + 1)
                    do(act.activation(GE[:, f, :], GE[:, f, :], ACT.Tanh, scale=float(np.sqrt(2.0 / np.pi))), ss["tanh"])
                gate(2, 0)
                for j in range(2):
                    act.wait_ge(ss["glu_done"], 3 + j)
                    do(act.activation(R(24 + j)[:, 0, :], M[2 + j][:, :], ACT.Tanh, scale=0.25, bias=SM[:, 48 + j:49 + j]))
                    do(act.activation(R(28 + j)[:, 0, :], M[j][:, :], ACT.Identity, scale=0.5, bias=col("s5_b_glu", j)), ss["val_ready"])
                y_split(2)
                for c in range(4):
                    if c:
                        gate(2, c)
                    for b in range(2):
                        k = 2 * c + b
                        act.wait_ge(mg_ready, k + 1)
                        do(act.activation(MHhi[:, k, :], MG[:, k, :], ACT.Copy, scale=0.5), mghi_ready)
                for k in range(KC):
                    act.wait_ge(at["mmx"], k + 1)
                    do(act.activation(MMhi[:, k, :], MMX[:, k, :], ACT.Copy), at["mm_hi"])

                def kv_copy(c):
                    for b, bank, free in banks(f"kv{c}"):
                        if c < 4:
                            do(act.activation(KTt[:, 2 * c + b, :], bank[:, 0:MEM], ACT.Copy), at["kt_ready"])
                        else:
                            do(act.activation(VM[:, b, (c - 4) * BW:(c - 3) * BW], bank[:, 0:BW], ACT.Copy), at["vm_ready"])
                        act.nop().then_inc(free, 1)

                for k in range(KC):
                    if k >= 2:
                        act.wait_ge(sq_used, 7 + k - 1)
                    else:
                        act.wait_ge(th_used, th_n[0] - 1 + k)
                    act.wait_ge(x_ready, k + 1)
                    do(act.activation(TH[:, k % 2, :], X[:, k, :], ACT.Square), sq_ready)
                act.wait_ge(at["mm_ready"], 8)
                kv_copy(0)
                kv_copy(1)
                act.wait_ge(ms_done, 2)
                act.preload_act_table_set(LOG_SET)
                do(act.activation(R(32)[:, 0, :], M[3][:, :], ACT.Ln, bias=eps), rstd_ready)
                do(act.activation(R(32)[:, 0, :], R(32)[:, 0, :], ACT.Exp, scale=-0.5), rstd_ready)
                kv_copy(2)
                kv_copy(3)
                for k in range(KC):
                    act.wait_ge(hx_ready, 8 + k + 1)
                    do(act.activation(Hhi[:, k, :], TH[:, k % 2, :], ACT.Copy), hi_ready)
                for c in range(4):
                    for b, bank, free in banks(f"q{c}"):
                        do(act.activation(MG[:, 2 * c + b, :], bank[:, :], ACT.Copy), at["q_ready"])
                        act.nop().then_inc(free, 1)
                    kv_copy(4 + c)
                for h in range(4):
                    if h >= 2:
                        act.wait_ge(at["pt_done"], 2 * (h - 1))
                    for t in range(TT):
                        act.wait_ge(at["mx_ready"], h * 4 + 4)
                        do(act.activation(PB[h % 2][:, t, :], M[t // 2][:, (t % 2) * 256:(t % 2) * 256 + 256], ACT.Exp,
                                          scale=1.0 / 16.0, bias=AST[:, 1, h * 4 + t:h * 4 + t + 1],
                                          accum_out=AST[:, 2, h * 4 + t:h * 4 + t + 1]), at["p_exp"])
                    for m in range(2):
                        act.wait_ge(at["pt_done"], 2 * h + m + 1)
                        do(act.activation(PTB[h % 2][:, m, :], M[2 + m][:, :], ACT.Copy), at["pt_ready"])
                    for k in range(2):
                        act.wait_ge(at["oc_ready"], 2 * h + k + 1)
                        do(act.activation(Hhi[:, 2 * h + k, :], MG[:, 2 * h + k, :], ACT.Copy), at["ohi_ready"])
                norm(16, R(32)[:, 0, :])
                n = 0
                for q in range(4):
                    for c in range(4):
                        for b, bank, free in banks(f"up{q}_{c}"):
                            if n:
                                act.wait_ge(uplo, n)
                            else:
                                act.wait_ge(h_ready, 24)
                            if q >= 2 and (c, b) == (0, 0):
                                last = f"down{q - 2}_3"
                                s, used = psum_set(last)
                                act.wait_ge(gemm_done[s], 2 * used + 2)
                            do(act.activation(UPX[:, 0, :], bank[:, :], ACT.Relu), up_a)
                            act.nop().then_inc(free, 1)
                            act.wait_ge(up_v, n + 1)
                            do(act.activation(MHID[q % 2][0][:, 2 * c + b, :], UPX[:, 0, :], ACT.Copy), uphi)
                            n += 1
                act.nop().then_inc(layer_end, 1)
                act.wait_ge(layer_go, L + 2)
            n = [0]

            def fdo(ins):
                n[0] += 1
                ins.then_inc(f_act, 1)
                act.wait_ge(f_act, n[0])
            for k in range(KC):
                fdo(act.activation(R(8 + k)[:, 0, :], X[:, k, :], ACT.Square))
            act.wait_ge(f_pe, 1)
            act.preload_act_table_set(LOG_SET)
            fdo(act.activation(R(32)[:, 0, :], M[3][:, :], ACT.Ln, bias=eps))
            fdo(act.activation(R(32)[:, 0, :], R(32)[:, 0, :], ACT.Exp, scale=-0.5))

        @block.vector
        def _(dve):
            do = chained(dve, v_chain)
            p_own = whole("pro_vector_steps")
            pn, po = [0], [0]

            def own(ins):
                po[0] += 1
                ins.then_inc(p_own, 1)
                dve.wait_ge(p_own, po[0])

            own(dve.memset(SM[:, 61:62], PI / 2))
            own(dve.memset(SM[:, 62:63], 1.0))
            own(dve.memset(SM[:, 63:64], EPS))
            own(dve.memset(WSM[:, :, :], 0.0))
            own(dve.memset(PS[:, :, :], 0.0))
            dve.memset(R(20, 2)[:, :, 0:P], 0.0).then_inc(p_vec, 1)
            dve.wait_ge(p_act, 4)
            for t in range(2):
                i = dve.tensor_scalar(flat(R(8 + 2 * t, 2)), flat(R(8 + 2 * t, 2)), SM[:, 44 + t:45 + t], None, ALU.mult)
                if t == 0:
                    own(i)
            i.then_inc(p_vec, 1)
            dve.wait_ge(p_vec, 2)
            dve.wait_ge(p_act, 16)
            own(dve.nop())
            dve.nop().then_inc(p_vec, 1)
            dve.wait_ge(p_vec, 3)
            dve.wait_ge(p_pe, 13)
            for l in range(DEPTH):
                own(dve.tensor_copy(PTA[:, l, :], G[0][l][:, 0:NROW]))
                own(dve.tensor_copy(PTA[:, l, PROW["step"]:PROW["step"] + 8], SM[:, 16 + 8 * l:24 + 8 * l]))
            l0, l1 = PTA[:, 0, PROW["lb0"]:PROW["lb0"] + 2], PTA[:, 0, PROW["lb1"]:PROW["lb1"] + 2]
            own(dve.tensor_tensor(PS[:, 0, 0:2], l1, l0, ALU.subtract))
            own(dve.tensor_tensor(PS[:, 1, 0:2], l0, l1, ALU.subtract))
            own(dve.tensor_copy(PS[:, 2:4, 0:2], PS[:, 0:2, 0:2]))
            dve.nop().then_inc(p_vec, 1)
            dve.wait_ge(p_act, 19)
            for n, name in enumerate(("hg_c0", "hg_c1")):
                own(dve.scalar_tensor_tensor(PTA[:, 1, PROW[name]:PROW[name] + 2], PS[:, 2 + n, 0:2], 0.0, PS[:, n, 0:2], ALU.min, ALU.subtract))
            own(dve.memset(PTA[:, 0, PROW["hg_c0"]:PROW["hg_c0"] + 2], NEG))
            own(dve.memset(PTA[:, 0, PROW["hg_c1"]:PROW["hg_c1"] + 2], 0.0))
            own(dve.nop())
            dve.nop().then_inc(layer_go, 1)

            def tt(o, a, b, op, s=None):
                do(dve.tensor_tensor(o, a, b, op), s)

            def ts(o, a, s1, s2, op0, op1=None, s=None):
                if op1 is None:
                    do(dve.tensor_scalar(o, a, s1, None, op0), s)
                else:
                    do(dve.tensor_scalar(o, a, s1, s2, op0, op1), s)

            def stt(o, a, sc, b, op0, op1, s=None):
                do(dve.scalar_tensor_tensor(out=o, in0=a, scalar=sc, in1=b, op0=op0, op1=op1), s)

            def norm_out(base, gain):
                dve.wait_ge(rstd_ready, base // 4 + 2)
                for k in range(KC + 1):
                    if k < KC:
                        stt(TH[:, k % 2, :], X[:, k, :], col(gain, k), R(32)[:, 0, :], ALU.mult, ALU.mult, hx_ready)
                    if k:
                        dve.wait_ge(hi_ready, base + k)
                        stt(Hlo[:, k - 1, :], TH[:, (k - 1) % 2, :], 1.0, Hhi[:, k - 1, :].bitcast(F32), ALU.mult, ALU.subtract, h_ready)

            th_n = [0]

            def gate_out(name, dst, s=None):
                st, used = psum_set(name)
                for b in range(2):
                    th_n[0] += 1
                    dve.wait_ge(th_ready, th_n[0])
                    stt(dst[:, b, :], TH[:, b, :], 1.0, G[st][b][:, :], ALU.add, ALU.mult, th_used)
                    dve.nop().then_inc(gemm_free[st], 1)

            def merge(n, c):
                s, used = psum_set(f"branch{n}_{c}")
                for b in range(2):
                    th_n[0] += 1
                    dve.wait_ge(th_ready, th_n[0])
                    dve.wait_ge(gemm_done[s], 2 * used + b + 1)
                    k = 2 * c + b
                    if n == 3:
                        stt(MG[:, k, :], TH[:, b, :], 1.0, G[s][b][:, :], ALU.add, ALU.mult, th_used)
                        dve.nop().then_inc(gemm_free[s], 1)
                    else:
                        stt(TH[:, b, :], TH[:, b, :], 1.0, G[s][b][:, :], ALU.add, ALU.mult)
                        dve.nop().then_inc(gemm_free[s], 1)
                        tt(MG[:, k, :], MG[:, k, :], TH[:, b, :], ALU.add, th_used)

            def ends(m):
                return m.Gc.rearrange("p (c t) -> p c t", t=CH)[:, :, CH - 1:CH]

            def level_diff(m, l):
                w = LEVELS[l]
                if l >= 3:
                    dve.wait_ge(m.x_ready, l - 2)
                g = m.Gc.rearrange("p (n a c) -> p n a c", a=2, c=w)
                e = m.E[l % 2].rearrange("p (n a c) -> p n a c", a=2, c=w)
                n = m.W // (2 * w)
                mid = g[:, :, 0, w - 1:w].to_broadcast([P, n, w])
                tt(e[:, :, 0, :], mid, g[:, :, 0, :], ALU.subtract, m.d_ready)
                tt(e[:, :, 1, :], g[:, :, 1, :], mid, ALU.subtract, m.d_ready)

            def level_mul(m, l):
                w = LEVELS[l]
                dve.wait_ge(m.e_ready, l)
                if l >= 3:
                    dve.wait_ge(m.lev_done, l - 1)
                v = lambda ap: ap.rearrange("p (n a c) -> p n a c", a=2, c=w)
                e, xx, k, q = v(m.E[l % 2]), v(m.X[l % 2]), v(m.K), v(m.Q)
                tt(xx[:, :, 0, :], e[:, :, 0, :], k[:, :, 0, :], ALU.mult)
                tt(xx[:, :, 1, :], e[:, :, 1, :], q[:, :, 1, :], ALU.mult, m.x_ready)

            def pick(m, l):
                dve.wait_ge(m.lev_done, l + 1)
                nb = 2 if m.J == 2 else 4
                w = 1024 // nb
                for b in range(nb):
                    bank = m.score_bank(l, b)
                    r = lambda ap: ap.rearrange("p (n c) -> p n c", c=CH)
                    do(dve.copy_predicated(r(m.att[:, b * w:(b + 1) * w]), bc(LM[:, l, :], 1, w // CH), r(bank[:, 0:w])), m.picked)

            def tail(m):
                g = m.Gc.rearrange("p (c t) -> p c t", t=CH)
                e0 = m.E[0].rearrange("p (c t) -> p c t", t=CH)
                tt(e0, ends(m).to_broadcast([P, m.W // CH, CH]), g, ALU.subtract, m.d_ready)
                dve.wait_ge(m.e_ready, 7)
                tt(m.E[0], m.E[0], m.K, ALU.mult, m.kd_ready)
                pick(m, 6)
                dve.wait_ge(m.e_ready, 8)
                if m.J == 1:
                    merge(3, 2)
                do(dve.memset(m.attbd[0:64, :, :, 64:128], 0.0))
                do(dve.memset(m.attbd[64:128, :, :, 0:64], 0.0))
                av = m.att.rearrange("p (h t c) -> p h t c", h=4, t=TT)
                for a in range(2):
                    rows = slice(64 * a, 64 * a + 64)
                    do(dve.tensor_copy(m.attbd[rows, :, :, 64 * a:64 * a + 64], av[rows]), m.bd_ready if a else None)
                do(dve.memset(m.S.rearrange("p j c v -> p (j c v)"), 0.0))
                do(dve.tensor_tensor(m.Q, m.Q, m.E[1], ALU.mult), m.s_ready)
                dve.wait_ge(m.kv_done, 1)
                eg = m.E[1].rearrange("p (c t) -> p c t", t=CH)
                for c in range(7):
                    for h in range(4):
                        jt, r0 = h // m.per, m.dk * (h % m.per)
                        rows, vs = slice(r0, r0 + m.dk), slice(HD * (h % m.per), HD * (h % m.per) + HD)
                        kv = M[2 + c % 2][rows, (h // m.per) * 256 + (c // 2) * HD:(h // m.per) * 256 + (c // 2) * HD + HD]
                        last = m.s_ready if (c, h) == (6, 3) else None
                        if c == 0:
                            do(dve.tensor_copy(m.S[rows, jt, 0, vs], kv), last)
                        else:
                            stt(m.S[rows, jt, c, vs], m.S[rows, jt, c - 1, vs], eg[rows, jt * NCH + c, CH - 1:CH], kv, ALU.mult, ALU.add, last)

            def branch_out(n, o, rs, order, gain, gate):
                for j in range(2):
                    dve.wait_ge(head_rs, 4 * order + 2 * j + 2)
                    stt(o[:, j, :], o[:, j, :], col(gain, j), rs[:, j, :], ALU.mult, ALU.mult)
                    gate(j)
                y_low(n, o)

            def y_low(n, o):
                for j in range(2):
                    dve.wait_ge(y_hi, 2 * BRANCH_NO[n] + j + 1)
                    b = YB[BRANCH_AT[n]]
                    stt(b[1][:, j, :], o[:, j, :], 0.5, b[0][:, j, :].bitcast(F32), ALU.mult, ALU.subtract, y_ready)

            def conv(j):
                dve.wait_ge(ms["cin_ready"], j + 1)
                ts(MQK[j], CIN[:, j, 3:515], col("mlstm_conv_w", 12 + j), col("mlstm_conv_b", j), ALU.mult, ALU.add)
                for k in range(3):
                    stt(MQK[j], CIN[:, j, k:k + SEQ], col("mlstm_conv_w", 4 * k + j), MQK[j], ALU.mult, ALU.add,
                        ms["cv_ready"] if k == 2 else None)

            with dve.Fori(0, DEPTH) as L:
                do(dve.tensor_copy(PT[:, :], PTA[:, bass.ds(L, 1), :].rearrange("p a c -> p (a c)")))
                norm_out(0, "norm_mix")
                E0, E1, X0, X1 = hg.E[0], hg.E[1], hg.X[0], hg.X[1]
                dve.wait_ge(hg.gate_in, 3)
                stt(X0, E0, 0.0, E1, ALU.min, ALU.subtract, hg.g_ready)
                tt(hg.K, X0, E0, ALU.subtract, hg.g_ready)
                for j in range(2):
                    js = slice(j * SEQ, (j + 1) * SEQ)
                    do(dve.tensor_tensor(SM[:, 50 + j:51 + j], col("hg_c1", j), col("hg_c0", j), ALU.subtract))
                    ts(X1[:, js], X0[:, js], SM[:, 50 + j:51 + j], None, ALU.add, s=hg.g_ready)
                for j in range(2):
                    js = slice(j * SEQ, (j + 1) * SEQ)
                    ts(X0[:, js], X0[:, js], col("hg_c1", j), col("hg_c0", j), ALU.add, ALU.max)
                dve.wait_ge(hg.gate_in, 4)
                tt(X0, X0, X1, ALU.add)
                for j in range(2):
                    js = slice(j * SEQ, (j + 1) * SEQ)
                    do(dve.tensor_tensor_scan(hg.Gc[:, js], reset, X0[:, js], 0.0, ALU.mult, ALU.add))
                gate_out("r_q", hg.Q.rearrange("p (j t) -> p j t", j=2))
                do(dve.nop(), hg.g_ready)
                level_diff(hg, 1)
                level_diff(hg, 2)
                do(dve.memset(hg.att, 0.0))
                pick(hg, 0)
                pr = lambda n: PS[:, n, :]
                re_, im_ = PT[:, PROW["s5_lam_re"]:PROW["s5_lam_re"] + 8], PT[:, PROW["s5_lam_im"]:PROW["s5_lam_im"] + 8]
                dve.wait_ge(params_in, 16 * 8)
                dve.wait_ge(ss["sin_in"], 1)
                tt(pr(1), re_, pr(0), ALU.mult)
                tt(pr(2), im_, pr(0), ALU.mult)
                ts(pr(5), pr(2), 1.0 / (2 * PI), None, ALU.mult)
                ts(pr(5), pr(5), 12582912.0, None, ALU.add)
                ts(pr(5), pr(5), 12582912.0, None, ALU.subtract)
                stt(pr(2), pr(5), -6.28125, pr(2), ALU.mult, ALU.add)
                stt(pr(2), pr(5), -(2 * PI - 6.28125), pr(2), ALU.mult, ALU.add)
                ts(pr(2), pr(2), PI, -PI, ALU.min, ALU.max, s=ss["prm"])
                dve.wait_ge(ss["sin_ready"], 1)
                Ur, Ui = PW[:, 0], PW[:, 1]
                do(dve.memset(Ur[:, 0, :], 1.0))
                do(dve.memset(Ui[:, 0, :], 0.0))
                do(dve.tensor_copy(Ur[:, 1, :], pr(3)))
                do(dve.tensor_copy(Ui[:, 1, :], pr(4)))

                def cmul(orr, oi, ar, ai, br, bi, t1, t2, s=None):
                    tt(t1, ar, br, ALU.mult)
                    tt(t2, ai, bi, ALU.mult)
                    tt(orr, t1, t2, ALU.subtract)
                    tt(t1, ar, bi, ALU.mult)
                    tt(t2, ai, br, ALU.mult)
                    tt(oi, t1, t2, ALU.add, s)

                for w in (1, 2, 4):
                    t1, t2 = S5T[0][:, 0:8 * w].rearrange("p (a b) -> p a b", b=8), S5T[1][:, 0:8 * w].rearrange("p (a b) -> p a b", b=8)
                    cmul(Ur[:, w + 1:2 * w + 1, :], Ui[:, w + 1:2 * w + 1, :], Ur[:, 1:w + 1, :], Ui[:, 1:w + 1, :],
                         Ur[:, w:w + 1, :].to_broadcast([P, w, 8]), Ui[:, w:w + 1, :].to_broadcast([P, w, 8]), t1, t2)
                do(dve.tensor_copy(pr(17), Ur[:, 8, :]))
                do(dve.tensor_copy(pr(18), Ui[:, 8, :]))
                tt(Ur[:, :, :], Ur[:, :, :], PS[:, 8:17, :], ALU.mult)
                tt(Ui[:, :, :], Ui[:, :, :], PS[:, 8:17, :], ALU.mult)
                tt(pr(5), re_, re_, ALU.mult)
                tt(pr(6), im_, im_, ALU.mult)
                tt(pr(5), pr(5), pr(6), ALU.add)
                do(dve.reciprocal(pr(5), pr(5)))
                ts(pr(6), Ur[:, 1, :], -1.0, None, ALU.add)
                tt(pr(7), pr(6), re_, ALU.mult)
                tt(pr(19), Ui[:, 1, :], im_, ALU.mult)
                tt(pr(7), pr(7), pr(19), ALU.add)
                tt(pr(7), pr(7), pr(5), ALU.mult)
                tt(pr(19), Ui[:, 1, :], re_, ALU.mult)
                tt(pr(20), pr(6), im_, ALU.mult)
                tt(pr(19), pr(19), pr(20), ALU.subtract)
                tt(pr(19), pr(19), pr(5), ALU.mult)
                level_mul(hg, 1)
                level_diff(hg, 3)
                dve.wait_ge(gl.gate_in, 3)
                stt(R(30)[:, 0, :], R(30)[:, 0, :], 0.0, R(31)[:, 0, :], ALU.min, ALU.subtract)
                do(dve.tensor_tensor_scan(gl.Gc, reset, R(30)[:, 0, :], 0.0, ALU.mult, ALU.add))
                pick(hg, 1)
                level_mul(hg, 2)
                level_diff(hg, 4)
                gate_out("g_r", gl.GR)
                level_mul(hg, 3)
                pick(hg, 2)
                level_diff(hg, 5)
                level_mul(hg, 4)
                pick(hg, 3)
                level_diff(hg, 6)
                gate_out("r_g", hg.GR)
                level_mul(hg, 5)
                pick(hg, 4)
                level_mul(hg, 6)
                pick(hg, 5)
                tail(hg)

                def silu_gate(m):
                    return lambda j: tt(m.O[:, j, :], m.O[:, j, :], m.GR[:, j, :], ALU.mult, y_act)
                branch_out(3, hg.O, hg.SQ, 0, "hgrn_norm", silu_gate(hg))
                level_diff(gl, 1)
                level_diff(gl, 2)
                do(dve.memset(CIN[:, :, 0:3], 0.0))
                do(dve.memset(gl.att, 0.0))
                pick(gl, 0)
                level_mul(gl, 1)
                level_diff(gl, 3)
                pick(gl, 1)
                level_mul(gl, 2)
                level_diff(gl, 4)
                pick(gl, 2)
                level_mul(gl, 3)
                level_mul(gl, 4)
                level_diff(gl, 5)
                level_diff(gl, 6)
                pick(gl, 3)
                merge(3, 0)
                conv(0)
                conv(1)
                pick(gl, 4)
                level_mul(gl, 5)
                level_mul(gl, 6)
                conv(2)
                conv(3)
                merge(3, 1)
                pick(gl, 5)
                for j in range(4):
                    dve.wait_ge(ms["mth_ready"], j + 1)
                    stt(MQK[j], MTHG[j], 1.0, MQK[j], ALU.add, ALU.mult)
                tail(gl)
                merge(3, 3)
                branch_out(1, gl.O, gl.SQ, 1, "gla_norm", silu_gate(gl))

                dve.wait_ge(ms["a1"], 1)
                stt(R(18)[32:36, 0, :], LP[32:36, :], 0.0, R(18)[32:36, 0, :], ALU.min, ALU.subtract, ms["v1"])
                dve.wait_ge(ms["a1"], 2)
                lf, bb, mt, bmr, st, it, wx = (R(n)[0:4, 0, :] for n in (19, 20, 21, 22, 23, 24, 25))
                do(dve.memset(R(23)[0:64, 0, :], 0.0))
                do(dve.tensor_tensor_scan(bb, reset[0:4, :], lf, 0.0, ALU.mult, ALU.add))
                do(dve.tensor_tensor_scan(mt, lf, LP[0:4, :], 0.0, ALU.add, ALU.max))
                tt(bmr, bb, mt, ALU.subtract)
                tt(st, LP[0:4, :], bb, ALU.subtract)
                ck = lambda ap: ap.rearrange("p (c t) -> p c t", t=CH)
                do(dve.memset(SM[0:4, 52:53], 0.0))
                do(dve.tensor_copy(SM[0:4, 53:60], ck(mt)[:, 0:7, CH - 1]))
                tt(ck(it), ck(bmr), SM[0:4, 52:60].unsqueeze(2).to_broadcast([4, NCH, CH]), ALU.add)
                tt(ck(wx), ck(st), ck(bmr)[:, :, CH - 1:CH].to_broadcast([4, NCH, CH]), ALU.add, ms["v1"])
                for j in range(2):
                    dve.wait_ge(ms["ib_done"], j + 1)
                    tt(MQT[:, j, :], MQK[j], M[1 + j][:, :], ALU.mult)
                    do(dve.tensor_copy(MDEC[:, j, :], ck(M[1 + j][:, :])[:, :, CH - 1]), ms["ib_ready"])
                do(dve.nop(), ms["ib_ready"])
                do(dve.nop(), ms["ib_ready"])
                merge(1, 0)
                for hp in range(2):
                    dve.wait_ge(ms["mex_done"], hp + 1)
                    for j in range(2):
                        o = MATT[:, hp, j * 256:(j + 1) * 256].rearrange("p (t c) -> p t c", t=TT)
                        a = MAW[:, :, 2 * j + hp:2 * j + hp + 1].to_broadcast([P, TT, CH])
                        tt(o, M[hp][:, j * 256:(j + 1) * 256].rearrange("p (t c) -> p t c", t=TT), a, ALU.add, ms["mex_v"] if j else None)
                do(dve.memset(MBD[0:64, :, :, 64:128], 0.0))
                do(dve.memset(MBD[64:128, :, :, 0:64], 0.0))
                dve.wait_ge(ms["mex_ready"], 1)
                dve.wait_ge(ms["mqk_done"], 1)
                for hp in range(2):
                    tt(MATT[:, hp, :], MATT[:, hp, :], M[2 + hp][:, :], ALU.mult, ms["matt_ready"])
                merge(1, 1)
                for j in range(2):
                    dve.wait_ge(ms["mkt_done"], j + 1)
                    w = MAW[:, :, 32 + 2 * j:34 + 2 * j].unsqueeze(3).to_broadcast([P, TT, 2, HD])
                    tt(MKT[:, :, j, :, :], M[j][:, :].rearrange("p (t b v) -> p t b v", t=TT, b=2), w, ALU.mult, ms["mkt_ready"])
                for j in range(2):
                    do(dve.memset(MS[j].rearrange("p c b v -> p (c b v)"), 0.0))
                dve.wait_ge(ms["mkv_done"], 1)
                for c in range(7):
                    for h in range(4):
                        j, hp = h // 2, h % 2
                        rows = slice(64 * hp, 64 * hp + 64)
                        kv = M[2 * (c % 2) + j][rows, (c // 2) * 128:(c // 2) * 128 + 128]
                        last = ms["ms_ready"] if c == 6 and h >= 2 else None
                        if c == 0:
                            do(dve.tensor_copy(MS[j][rows, 0, hp, :], kv))
                        else:
                            stt(MS[j][rows, c, hp, :], MS[j][rows, c - 1, hp, :], MDEC[rows, j, c:c + 1], kv, ALU.mult, ALU.add, last)
                merge(1, 2)
                for j in range(2):
                    dve.wait_ge(ms["mabs_ready"], j + 1)
                    tt(MDA[:, j, :], MDA[:, j, :], MEM_E[:, j, :], ALU.max)
                    do(dve.reciprocal(MDA[:, j, :], MDA[:, j, :]))
                    stt(MOO[:, j, :], M[j][:, :], MC, MDA[:, j, :], ALU.mult, ALU.mult, ms["mh_ready"])
                merge(1, 3)
                branch_out(0, MOO, MSQ, 2, "mlstm_norm",
                           lambda j: stt(MOO[:, j, :], MO[:, j, :], 1.0, MOO[:, j, :], ALU.add, ALU.mult, y_act))

                merge(0, 0)
                c8 = lambda ap: ap.unsqueeze(2).to_broadcast([P, 8, 16])
                bb_r, bb_i = (ST[2][:, n * 128:(n + 1) * 128].rearrange("p (t h) -> p t h", t=8) for n in range(2))
                t1, t2 = (ST[2][:, n * 128:(n + 1) * 128].rearrange("p (t h) -> p t h", t=8) for n in range(2, 4))
                cmul(bb_r, bb_i, BRI[:, 0], BRI[:, 1], c8(pr(7)), c8(pr(19)), t1, t2)
                do(dve.memset(XP.rearrange("p r u t c -> p (r u t c)"), 0.0))
                four = [Rf(20 + 2 * n, 2).rearrange("p (u t h) -> p u t h", u=8, t=8) for n in range(2)]
                pw = lambda n: PW[:, n, 0:8, :].unsqueeze(3).to_broadcast([P, 8, 8, 16])
                bx = lambda ap: ap.unsqueeze(1).to_broadcast([P, 8, 8, 16])
                for r, (b1, b2, op) in enumerate(((bb_r, bb_i, ALU.subtract), (bb_i, bb_r, ALU.add))):
                    tt(four[0], pw(0), bx(b1), ALU.mult)
                    tt(four[1], pw(1), bx(b2), ALU.mult)
                    for a in range(2):
                        rows = slice(64 * a, 64 * a + 64)
                        tt(XP[rows, r, :, :, 16 * a:16 * a + 16], four[0][rows], four[1][rows], op, ss["xp_ready"] if (r, a) == (1, 1) else None)
                for r in range(2):
                    for f in range(2):
                        for a in range(2):
                            ts(R(24 + r)[:, 0, f * P + 64 * a:f * P + 64 * a + 64], CRI[:, r, f, :], parity[:, a:a + 1], None, ALU.mult,
                               s=ss["cp_ready"] if (f, a) == (1, 1) else None)
                dve.wait_ge(ss["ct_ready"], 1)
                ts(CT[:, 1, :], CT[:, 1, :], -1.0, None, ALU.mult, s=ss["cp_ready"])
                do(dve.memset(KTm.rearrange("p a u c -> p (a u c)"), 0.0))
                dve.wait_ge(ss["kk_done"], 1)
                kk = M[0][:, :].rearrange("p (f u c) -> p f u c", f=2, u=8)
                for i4 in range(4):
                    rows = slice(32 * i4, 32 * i4 + 32)
                    do(dve.tensor_copy(KTm[rows, :, :, 32 * i4:32 * i4 + 32], kk[rows]), ss["kk_ready"])
                t1, t2 = (a.rearrange("p (j t c) -> p j t c", j=8, t=8) for a in T4)
                pj = lambda n: PW[:, n, 1:9, :].unsqueeze(3).to_broadcast([P, 8, 8, 32])
                cx = lambda n: CT[:, n, :].rearrange("p (t c) -> p t c", t=8).unsqueeze(1).to_broadcast([P, 8, 8, 32])
                tt(t1, pj(0), cx(0), ALU.mult)
                tt(t2, pj(1), cx(1), ALU.mult)
                tt(CL[:, 0], t1, t2, ALU.add)
                tt(t1, pj(0), cx(1), ALU.mult)
                tt(t2, pj(1), cx(0), ALU.mult)
                tt(CL[:, 1], t1, t2, ALU.subtract, ss["cl_ready"])
                merge(0, 1)
                do(dve.tensor_copy(TB[0][:, :, 0], pr(17)))
                do(dve.tensor_copy(TB[1][:, :, 0], pr(18)))
                w = 1
                while w < S5_N:
                    t1, t2 = (ST[n][:, 0:8 * w].rearrange("p (t n) -> p t n", t=8) for n in range(2))
                    cmul(TB[0][:, :, w:2 * w], TB[1][:, :, w:2 * w], TB[0][:, :, 0:w], TB[1][:, :, 0:w],
                         TB[0][:, :, w - 1:w].to_broadcast([P, 8, w]), TB[1][:, :, w - 1:w].to_broadcast([P, 8, w]), t1, t2)
                    w *= 2
                rr = ST[2].rearrange("p (t n) -> p t n", t=8)
                do(dve.tensor_copy(rr, PS[:, 16, :].unsqueeze(2).to_broadcast([P, 8, S5_N])))
                do(dve.memset(rr[:, :, 0:1], 0.0))
                dve.wait_ge(ss["ct_ready"], 2)
                w3 = lambda ap: ap.rearrange("p (t n) -> p t n", t=8)
                a0, a1 = w3(ST[0]), w3(ST[1])
                tt(a0, TB[0], SW[0], ALU.mult)
                tt(a1, TB[1], SW[1], ALU.mult)
                tt(w3(SZ[0]), a0, a1, ALU.add)
                tt(a0, TB[0], SW[1], ALU.mult)
                tt(a1, TB[1], SW[0], ALU.mult)
                tt(w3(SZ[1]), a0, a1, ALU.subtract)
                for r in range(2):
                    do(dve.tensor_tensor_scan(SZ[r], ST[2], SZ[r], 0.0, ALU.mult, ALU.add))
                cmul(SX[0], SX[1], w3(SZ[0]), w3(SZ[1]), TB[0], TB[1], a0, a1, ss["x_ready"])
                merge(0, 2)
                merge(0, 3)
                for f in range(2):
                    dve.wait_ge(ss["y_done"], f + 1)
                    ys = YS[:, f, :].rearrange("p (n j) -> p j n", j=S5_T)
                    uf = UU[:, f, :].rearrange("p (n j) -> p j n", j=S5_T)
                    stt(ys, uf, col("s5_d", f), M[f][:, :].rearrange("p (j n) -> p j n", j=S5_T), ALU.mult, ALU.add, ss["ys_ready"])
                for f in range(2):
                    dve.wait_ge(ss["sq"], f + 1)
                    ts(GE[:, f, :], GE[:, f, :], 0.044715, 1.0, ALU.mult, ALU.add)
                    tt(GE[:, f, :], GE[:, f, :], YS[:, f, :], ALU.mult, ss["poly"])
                do(dve.tensor_scalar(SM[:, 48:50], PT[:, PROW["s5_b_glu"] + 2:PROW["s5_b_glu"] + 4], 0.5, None, ALU.mult))
                for f in range(2):
                    dve.wait_ge(ss["tanh"], f + 1)
                    stt(GE[:, f, :], GE[:, f, :], 1.0, YS[:, f, :], ALU.add, ALU.mult, ss["ge_ready"])
                for j in range(2):
                    dve.wait_ge(ss["val_ready"], j + 1)
                    stt(YS[:, j, :], R(24 + j)[:, 0, :], 1.0, R(28 + j)[:, 0, :], ALU.add, ALU.mult, y_act)
                do(dve.nop(), at["base_free"])
                y_low(2, YS)
                for c in range(4):
                    s, used = psum_set(f"branch2_{c}")
                    for b in range(2):
                        th_n[0] += 1
                        dve.wait_ge(th_ready, th_n[0])
                        dve.wait_ge(gemm_done[s], 2 * used + b + 1)
                        k = 2 * c + b
                        stt(TH[:, b, :], TH[:, b, :], 1.0, G[s][b][:, :], ALU.add, ALU.mult)
                        dve.nop().then_inc(gemm_free[s], 1)
                        tt(MG[:, k, :], MG[:, k, :], TH[:, b, :], ALU.add, mg_ready)
                        do(dve.nop(), th_used)
                    for b in range(2):
                        k = 2 * c + b
                        dve.wait_ge(mghi_ready, k + 1)
                        stt(MHlo[:, k, :], MG[:, k, :], 0.5, MHhi[:, k, :].bitcast(F32), ALU.mult, ALU.subtract, mgs_ready)
                dve.wait_ge(at["mem_base_in"], 16)
                for k in range(KC):
                    ts(MMX[:, k, :], MBASE[:, k, :], col("norm_mem", k), None, ALU.mult, s=at["mmx"])
                for k in range(KC):
                    dve.wait_ge(at["mm_hi"], k + 1)
                    stt(MMlo[:, k, :], MMX[:, k, :], 1.0, MMhi[:, k, :].bitcast(F32), ALU.mult, ALU.subtract, at["mm_ready"])

                def residual(name):
                    s, used = psum_set(name)
                    c = int(name[-1])
                    for b in range(2):
                        dve.wait_ge(gemm_done[s], 2 * used + b + 1)
                        tt(X[:, 2 * c + b, :], X[:, 2 * c + b, :], G[s][b][:, :], ALU.add, x_ready)
                        dve.nop().then_inc(gemm_free[s], 1)

                for c in range(4):
                    residual(f"out{c}")
                norm_out(8, "norm_xattn")
                for h in range(4):
                    dve.wait_ge(at["sc_done"], h + 1)
                    for b in range(2):
                        do(dve.tensor_reduce(AST[:, 0, h * 4 + 2 * b:h * 4 + 2 * b + 2], M[b][:, :].rearrange("p (t m) -> p t m", t=2),
                                             mybir.AxisListType.X, ALU.max))
                    ts(AST[:, 1, h * 4:h * 4 + 4], AST[:, 0, h * 4:h * 4 + 4], -1.0 / 16.0, None, ALU.mult)
                    for n in range(4):
                        do(dve.nop(), at["mx_ready"])
                    dve.wait_ge(at["p_exp"], 4 * h + 4)
                    do(dve.reciprocal(AST[:, 3, h * 4:h * 4 + 4], AST[:, 2, h * 4:h * 4 + 4]))
                    for t in range(TT):
                        ts(PB[h % 2][:, t, :], PB[h % 2][:, t, :], AST[:, 3, h * 4 + t:h * 4 + t + 1], None, ALU.mult, s=at["p_ready"])
                    for k in range(2):
                        dve.wait_ge(at["o_done"], 2 * h + k + 1)
                        do(dve.tensor_copy(MG[:, 2 * h + k, :], M[2 + k][:, :]), at["oc_ready"])
                    for k in range(2):
                        dve.wait_ge(at["ohi_ready"], 2 * h + k + 1)
                        stt(Hlo[:, 2 * h + k, :], MG[:, 2 * h + k, :], 1.0, Hhi[:, 2 * h + k, :].bitcast(F32), ALU.mult, ALU.subtract,
                            at["osplit_ready"])
                for c in range(4):
                    residual(f"o{c}")
                norm_out(16, "norm_mlp")
                n = [0]

                def up(q):
                    for c in range(4):
                        for b in range(2):
                            dve.wait_ge(up_a, n[0] + 1)
                            tt(UPX[:, 0, :], UPX[:, 0, :], UPX[:, 0, :], ALU.mult, up_v)
                            dve.wait_ge(uphi, n[0] + 1)
                            hb = MHID[q % 2]
                            stt(hb[1][:, 2 * c + b, :], UPX[:, 0, :], 1.0, hb[0][:, 2 * c + b, :].bitcast(F32), ALU.mult, ALU.subtract, uplo)
                            n[0] += 1

                def down(q):
                    for c in range(4):
                        residual(f"down{q}_{c}")

                up(0)
                up(1)
                down(0)
                up(2)
                down(1)
                up(3)
                down(2)
                down(3)
                dve.nop().then_inc(layer_end, 1)
                dve.wait_ge(layer_go, L + 2)

            def fown(ins):
                po[0] += 1
                ins.then_inc(p_own, 1)
                dve.wait_ge(p_own, po[0])
            dve.wait_ge(f_act, KC + 2)
            for k in range(KC):
                fown(dve.scalar_tensor_tensor(out=MG[:, k, :], in0=X[:, k, :], scalar=col("norm_final", k), in1=R(32)[:, 0, :],
                                              op0=ALU.mult, op1=ALU.mult))
            dve.nop().then_inc(f_vec, 1)
            for t in range(TT):
                dve.wait_ge(f_pe, 2 + t)
                for b in range(2):
                    dve.tensor_copy(R(2 * t + b)[:, 0, :], G[0][b][:, :]).then_inc(f_vec, 1)


_INS = ['x', 'mem', 'norm_mix', 'w_in', 'mlstm_conv_w', 'mlstm_conv_b', 'mlstm_i_bias', 'mlstm_f_bias', 'mlstm_norm',
        'gla_w_a2', 'gla_b_a', 'gla_norm', 's5_lam_re', 's5_lam_im', 's5_b_re', 's5_b_im', 's5_c_re', 's5_c_im', 's5_d',
        's5_log_step', 's5_w_glu', 's5_b_glu', 'hgrn_lb_logits', 'hgrn_norm', 'w_branch', 'w_out', 'norm_xattn',
        'norm_mem', 'xattn_w_q', 'xattn_w_kv', 'xattn_w_o', 'norm_mlp', 'mlp_w1', 'mlp_w2', 'norm_final']


def kernel(**inputs):
    import numpy as _np
    import concourse.bacc as _bacc
    from concourse import mybir as _mybir
    from concourse.bass_utils import run_bass_kernel_spmd as _run

    nc = _bacc.Bacc("TRN2", target_bir_lowering=False, num_devices=1)
    arrays, args = {}, []
    consts, masks = shape_constants()
    for name, a in [(n, inputs[n]) for n in _INS] + [("consts", consts), ("level_masks", masks)]:
        a = _np.ascontiguousarray(a)
        arrays[f"in_{name}_dram"] = a
        args.append(nc.dram_tensor(f"in_{name}_dram", a.shape, _mybir.dt.from_np(a.dtype), kind="ExternalInput").ap())
    out = nc.dram_tensor("out_0_dram", (1, SEQ, D), _mybir.dt.float32, kind="ExternalOutput").ap()
    build(nc, args, out)
    r = _run(nc, [arrays], core_ids=[0])
    return r.results[0]["out_0_dram"]
```

```python
from contextlib import ExitStack

import numpy as np

import concourse.bass as bass
from concourse import mybir

F32 = mybir.dt.float32
F32R = mybir.dt.float32r
I32 = mybir.dt.int32
ALU = mybir.AluOpType
ACT = mybir.ActivationFunctionType

P = 128
D = 1024
KC = D // P
SEQ = 512
DEPTH = 2
MEM = 256
CH = 64
NCH = SEQ // CH
TT = SEQ // P
EPS = 1e-6
HD = 64
GDK = 32
RANK = 16
S5_T = 8
S5_N = SEQ // S5_T
S5_TILES = 8
HIDDEN = 4 * D
BW = 256
NEG = -1e30
LOG_SET = "natural_log_exp_and_others"
EXP_SET = "exp_and_others"
PI = float(np.pi)

COL = {}
_at = 0
for _name, _w in (("m_q", 256), ("m_k", 256), ("m_v", 256), ("m_i", 4), ("m_f", 4), ("m_o", 256), ("g_q", 128),
                  ("g_k", 128), ("g_v", 256), ("g_a", 16), ("g_r", 256), ("s_u", 256), ("r_q", 256), ("r_f", 256),
                  ("r_i", 256), ("r_g", 256), ("gates", 4096)):
    COL[_name] = _at
    _at += _w
IN_WIDTH = _at

PROW = {}
_at = 0
for _name, _n in (("norm_mix", 8), ("norm_xattn", 8), ("norm_mem", 8), ("norm_mlp", 8), ("mlstm_conv_w", 16),
                  ("mlstm_conv_b", 4), ("mlstm_norm", 2), ("gla_norm", 2), ("hgrn_norm", 2), ("s5_d", 2),
                  ("gla_b_a", 1), ("s5_b_glu", 4), ("lb0", 2), ("lb1", 2), ("s5_lam_re", 8), ("s5_lam_im", 8),
                  ("norm_final", 8), ("if_bias", 1), ("step", 8), ("hg_c0", 2), ("hg_c1", 2)):
    PROW[_name] = _at
    _at += _n
NROW = _at

CCOL = {}
_at = 0
for _name, _n in (("ident", 128), ("head_mean", 128), ("mean", 128), ("ones", 64), ("neg", 64), ("reset", 512),
                  ("pair_sel", 256), ("head_sel", 256), ("parity", 2)):
    CCOL[_name] = (_at, _n)
    _at += _n
NCONST = _at
LEVELS = [0, 32, 16, 8, 4, 2, 1]


def shape_constants():
    c = np.zeros((P, NCONST), np.float32)

    def put(name, a):
        at, n = CCOL[name]
        c[:a.shape[0], at:at + n] = a

    r = np.arange(P)
    put("ident", np.eye(P, dtype=np.float32))
    put("head_mean", (r[:, None] // HD == r[None, :] // HD).astype(np.float32) / HD)
    put("mean", np.full((P, P), 1.0 / D, np.float32))
    put("ones", np.ones((P, 64), np.float32))
    t = np.arange(CH)
    put("neg", np.where(r[:, None] % CH <= t[None, :], 0.0, NEG).astype(np.float32))
    put("reset", np.broadcast_to((np.arange(SEQ) % CH != 0).astype(np.float32), (P, SEQ)))
    pair = np.zeros((4, 2, P), np.float32)
    head = np.zeros((4, 4, 64), np.float32)
    for h in range(4):
        pair[h, h // 2, 64 * (h % 2):64 * (h % 2) + 64] = 1.0
        head[h, h, :] = 1.0
    put("pair_sel", pair.reshape(4, 256))
    put("head_sel", head.reshape(4, 256))
    put("parity", np.stack([(r // 16) % 2 == 0, (r // 16) % 2 == 1], 1).astype(np.float32))
    m = np.zeros((P, len(LEVELS), CH), np.int32)
    s = r[:, None] % CH
    tt = t[None, :]
    for n, w in enumerate(LEVELS):
        if w == 0:
            m[:, n] = s == tt
        else:
            m[:, n] = (s // (2 * w) == tt // (2 * w)) & (s % (2 * w) < w) & (tt % (2 * w) >= w)
    return c, m.reshape(P, -1)


def block_order():
    order = [(n, "full") for n in ("r_f", "r_q", "r_i", "g_qk", "narrow", "g_v", "g_r", "r_g", "gate3_0", "m_q", "m_k", "m_v", "m_o",
                                   "branch3_0", "gate3_1", "branch3_1", "gate3_2", "branch3_2", "gate3_3", "branch3_3", "s_u")]
    order += [(f"{what}1_{c}", "full") for c in range(4) for what in ("gate", "branch")]
    order += [(n, "full") for n in ("gate0_0", "gate0_1", "branch0_0", "branch0_1", "gate0_2", "branch0_2", "gate0_3", "branch0_3",
                                    "gate2_0", "gate2_1", "branch2_0", "branch2_1", "gate2_2", "branch2_2", "gate2_3", "branch2_3")]
    order += [(f"out{c}", "full") for c in range(4)]
    order += [(f"kv{c}", "full") for c in range(4)]
    for c in range(4):
        order += [(f"q{c}", "full"), (f"kv{4 + c}", "full")]
    order = [(n, "branch" if n.startswith("branch") else kind) for n, kind in order]
    order += [(f"o{c}", "full") for c in range(4)]
    ups, downs = [[(f"up{q}_{c}", "full") for c in range(4)] for q in range(4)], [
        [(f"down{q}_{c}", "full") for c in range(4)] for q in range(4)]
    order += ups[0] + ups[1] + downs[0] + ups[2] + downs[1] + ups[3] + downs[2] + downs[3]
    return order


BLOCKS = block_order()
BLOCK = {name: n for n, (name, _) in enumerate(BLOCKS)}
UNIT, UNITS = {}, []
for _name, _kind in BLOCKS:
    UNIT[_name] = len(UNITS)
    UNITS += [(_name, "first"), (_name, "last")] if _kind == "full" else [(_name, "last")]
NUNIT = len(UNITS)
FIRSTS = [sum(part == "first" for _, part in UNITS[:u + 1]) for u in range(NUNIT)]
RAW = 4
BY_VECTOR = [0] + [UNIT[n] + h for n in ("kv0", "kv1") for h in range(2)]
for _n in range(4):
    BY_VECTOR += ([UNIT[f"q{_n}"]] if _n else []) + [UNIT[f"kv{4 + _n}"] + h for h in range(2)]
BY_SCALAR = [UNIT[n] + h for n in ("kv2", "kv3") for h in range(2)]
NARROW = 80
COME = [16 * sum(3 if UNITS[v][0] == "narrow" else 1 for v in range(_u % RAW, _u + 1, RAW)) for _u in range(NUNIT)]
SLOT, BEFORE, _last, _turn = [], [], {}, 0
for _u, (_name, _part) in enumerate(UNITS):
    if _name.startswith("branch"):
        _s = 2
    else:
        _s, _turn = _turn, 1 - _turn
    SLOT.append(_s)
    BEFORE.append(_last.get(_s))
    _last[_s] = _u


def psum_set(name):
    return BLOCK[name] % 2, BLOCK[name] // 2


def build(nc, ins, out):
    (x, mem, norm_mix, w_in, mlstm_conv_w, mlstm_conv_b, mlstm_i_bias, mlstm_f_bias, mlstm_norm, gla_w_a2, gla_b_a,
     gla_norm, s5_lam_re, s5_lam_im, s5_b_re, s5_b_im, s5_c_re, s5_c_im, s5_d, s5_log_step, s5_w_glu, s5_b_glu,
     hgrn_lb_logits, hgrn_norm, w_branch, w_out, norm_xattn, norm_mem, xattn_w_q, xattn_w_kv, xattn_w_o, norm_mlp,
     mlp_w1, mlp_w2, norm_final, consts, level_masks) = ins
    mem_scratch = nc.dram_tensor("mem_scratch", (P, KC * MEM), F32, kind="Internal").ap()

    ctx = ExitStack()
    with ctx:
        def sb(name, shape, dt=F32):
            return ctx.enter_context(nc.sbuf_tensor(name, shape, dt))

        X = sb("x_t", [P, KC, SEQ])
        Hhi = sb("h_hi", [P, KC, SEQ], F32R)
        Hlo = sb("h_lo", [P, KC, SEQ], F32R)
        MG = sb("merged", [P, KC, SEQ])
        WR = sb("w_raw", [P, RAW, 4 * BW])
        WHi = sb("w_hi", [P, 10 * BW], F32R)
        WLo = sb("w_lo", [P, 10 * BW], F32R)
        work_at = nc.sbuf_base
        YR = sb("work", [P, 8 + 33, 512])
        YS_R = nc.alloc_sbuf_tensor_at("work_split", [P, 8 + 33, 512], F32R, offset=work_at)
        TH = sb("gate_t", [P, 2, SEQ])
        CO = sb("consts_sb", [P, NCONST])
        LM = sb("masks_sb", [P, len(LEVELS), CH], I32)
        PTA = sb("params_all", [P, DEPTH, NROW])
        PT = sb("params", [P, NROW])
        WA2 = sb("w_a2", [RANK, P])
        BRI = sb("s5_b", [P, 2, S5_TILES, 16])
        CRI = sb("s5_c", [P, 2, 2, 64])
        LP = sb("if_rows", [36, SEQ])
        SM = sb("small", [P, 64])

        R = lambda a, n=1: YR[:, 8 + a:8 + a + n, :]
        flat = lambda ap: ap.rearrange("p a b -> p (a b)")
        Rf = lambda a, n: flat(R(a, n))

        def const(name):
            at, n = CCOL[name]
            return CO[:, at:at + n]

        ident, head_mean, mean_w = const("ident"), const("head_mean"), const("mean")
        ones64, neg_mask, reset = const("ones"), const("neg"), const("reset")
        pair_sel = const("pair_sel").rearrange("p (j m) -> p j m", j=2)
        head_sel = const("head_sel").rearrange("p (h m) -> p h m", h=4)
        parity = const("parity")
        col = lambda name, n=0: PT[:, PROW[name] + n:PROW[name] + n + 1]
        colr = lambda name, n, parts: PT[parts, PROW[name] + n:PROW[name] + n + 1]

        G = [[ctx.enter_context(nc.psum_tensor(f"gemm{s}{b}", [P, 512], F32)) for b in range(2)] for s in range(2)]
        M = [ctx.enter_context(nc.psum_tensor(f"mix{b}", [P, 512], F32)) for b in range(4)]

        def bc(ap, axis, n):
            a = ap.unsqueeze(axis)
            shape = list(a.shape)
            shape[axis] = n
            return a.to_broadcast(shape)

        layer_sems = []

        def sem(name):
            s = ctx.enter_context(nc.semaphore(name))
            layer_sems.append(s)
            return s

        def whole(name):
            return ctx.enter_context(nc.semaphore(name))

        p_dma, p_rows, p_vec, p_act, p_pe, p_out = (whole(n) for n in ("pro_loads", "pro_rows", "pro_vector", "pro_scalar", "pro_tensor", "pro_stores"))
        p_x, p_sq = whole("pro_x_in"), whole("pro_squares")
        f_vec, f_act, f_pe = (whole(n) for n in ("fin_vector", "fin_scalar", "fin_tensor"))
        layer_end, layer_go = whole("layer_end"), whole("layer_go")

        v_chain, a_chain = sem("vector_steps"), sem("scalar_steps")
        raw_in = [sem(f"raw_in{i}") for i in range(RAW)]
        split_hi_vector, split_hi_scalar, split_hi, split_ready, split_used = sem("split_hi_vector"), sem("split_hi_scalar"), sem("split_hi"), sem("split_ready"), sem("split_used")
        gemm_done = [sem(f"gemm_done{i}") for i in range(2)]
        gemm_free = [sem(f"gemm_free{i}") for i in range(2)]
        params_in, all_ended = sem("params_in"), sem("all_ended")
        head_sq, head_ms, head_rs = sem("head_squares"), sem("head_means"), sem("head_factors")
        sq_ready, sq_used, ms_done, rstd_ready = sem("sq_ready"), sem("sq_used"), sem("ms_done"), sem("rstd_ready")
        hx_ready, hi_ready, h_ready = sem("hx_ready"), sem("hi_ready"), sem("h_ready")
        th_ready, th_used = sem("th_ready"), sem("th_used")
        ga_ready, ga_done = sem("ga_ready"), sem("ga_done")
        y_act, y_hi, y_ready = sem("y_act"), sem("y_hi"), sem("y_ready")
        mg_ready, mghi_ready, mgs_ready = sem("mg_ready"), sem("mghi_ready"), sem("mg_split_ready")
        x_ready = sem("x_ready")

        class Mixer:

            def __init__(self, pre, tiles, dk, q, k, v, g, gr, e, xx, att, attbd, kt, state, o, sq, gscale, oscale, norm):
                self.pre, self.J, self.dk, self.gscale, self.oscale, self.norm = pre, tiles, dk, gscale, oscale, norm
                self.W = tiles * SEQ
                self.Q, self.K, self.Gc = Rf(q, tiles), Rf(k, tiles), Rf(g, tiles)
                self.V = Rf(v, 2).rearrange("p (t c) -> p t c", t=TT)
                self.GR = R(gr, 2)
                self.E = [Rf(e + tiles * i, tiles) for i in range(2)]
                self.X = [Rf(xx + tiles * i, tiles) for i in range(2)]
                self.att = Rf(att, 2)
                self.attbd = Rf(attbd, 4).rearrange("p (h t s) -> p h t s", h=4, t=TT)
                self.KT = Rf(kt, tiles).rearrange("p (t c) -> p t c", t=TT)
                self.per = P // dk
                wide = self.per * HD
                self.S = YR[:, 8 + state:8 + state + 4, :].rearrange("p a b -> p (a b)")[:, :tiles * 7 * wide].rearrange(
                    "p (j c v) -> p j c v", j=tiles, c=7)
                self.O, self.SQ = R(o, 2), R(sq, 2)
                self.gate_in, self.g_ready = sem(pre + "_gate_in"), sem(pre + "_decay_ready")
                self.kq_ready = sem(pre + "_kq_ready")
                self.v_ready = sem(pre + "_v_ready")
                self.d_ready, self.e_ready, self.x_ready = sem(pre + "_diff"), sem(pre + "_exp"), sem(pre + "_x")
                self.lev_done, self.picked = sem(pre + "_scores"), sem(pre + "_picked")
                self.bd_ready, self.kd_ready = sem(pre + "_att_ready"), sem(pre + "_kdecay_ready")
                self.kt_done, self.kt_ready = sem(pre + "_kt_done"), sem(pre + "_kt_ready")
                self.kv_done, self.s_ready = sem(pre + "_kv_done"), sem(pre + "_state_ready")
                self.o_done = sem(pre + "_o_done")

            def score_bank(self, level, h):
                return M[2 * (level % 2) + h % 2] if self.J == 2 else M[h]

            def score_cols(self, h):
                return (h // 2) * 256 if self.J == 2 else 0

            def slot(self, h):
                return (h % 2) * 2 + h // 2 if self.J == 2 else h

        hg = Mixer("hg", 2, HD, 4, 2, 6, 0, 8, 10, 14, 18, 14, 20, 22, 10, 12, 1.0, 0.5, "hgrn_norm")
        gl = Mixer("gl", 1, GDK, 26, 27, 28, 32, 30, 10, 12, 14, 16, 20, 22, 12, 10, 1.0 / 16.0, GDK ** -0.5, "gla_norm")

        CIN = YR[:, 8:8 + 5, :].rearrange("p a b -> p (a b)")[:, 0:4 * 515].rearrange("p (j t) -> p j t", j=4)
        MV = Rf(5, 2).rearrange("p (t c) -> p t c", t=TT)
        MO = [R(8)[:, 0, :], sb("m_out_gate", [P, SEQ])[:, :]]
        MQK = [R(a)[:, 0, :] for a in (9, 0, 1, 2)]
        MTHG = [R(16 + j)[:, 0, :] for j in range(4)]
        MBD = Rf(14, 4).rearrange("p (h t s) -> p h t s", h=4, t=TT)
        MATT = Rf(18, 2).rearrange("p (b c) -> p b c", b=2)
        MKT = Rf(20, 2).rearrange("p (t j b v) -> p t j b v", t=TT, j=2, b=2)
        MS = [YR[:, 8 + a:8 + a + 4, :].rearrange("p a b -> p (a b)")[:, 0:7 * 256].rearrange(
            "p (c b v) -> p c b v", c=7, b=2) for a in (22, 28)]
        MQT, MEM_E = R(10, 2), R(12, 2)
        MDA, MOO, MSQ = R(20, 2), R(18, 2), R(22, 2)
        MC = (HD ** -0.5) / 4.0
        MAW = Rf(32, 1)[:, 0:256].rearrange("p (t c) -> p t c", t=TT)
        MDEC = SM[:, 0:16].rearrange("p (j c) -> p j c", j=2)
        m_names = ("cin_ready", "cv_ready", "mth_ready", "mv_ready", "a1", "v1", "aw_done", "aw_ready",
                   "ib_done", "ib_ready", "mex_done", "mex_v", "mex_ready", "mqk_done", "matt_ready", "mbd_ready",
                   "mkt_done", "mkt_ready", "mkv_done", "ms_ready", "mo_done", "mabs_ready", "mh_ready", "stack_ready", "emb_ready")
        ms = {n: sem("mlstm_" + n) for n in m_names}

        XP = Rf(0, 8).rearrange("p (r t u c) -> p r u t c", r=2, u=8, t=8)
        CL = Rf(0, 8).rearrange("p (r j t c) -> p r j t c", r=2, j=8, t=8)
        BT = Rf(8, 8).rearrange("p (t r q s) -> p t r q s", t=8, r=2, q=2)
        U4 = Rf(24, 2).rearrange("p (t q n) -> p t q n", t=8, q=2)
        KTm = Rf(16, 4).rearrange("p (a u c) -> p a u c", a=2, u=8)
        SW = [Rf(20, 1).rearrange("p (t n) -> p t n", t=8), Rf(21, 1).rearrange("p (t n) -> p t n", t=8)]
        TB = [sb(f"s5_phases{n}", [P, 512])[:, :].rearrange("p (t n) -> p t n", t=8) for n in range(2)]
        SZ = [Rf(24, 1), Rf(25, 1)]
        ST = [Rf(28, 1), Rf(29, 1), Rf(30, 1)]
        SX = [Rf(31, 1).rearrange("p (t n) -> p t n", t=8), Rf(32, 1).rearrange("p (t n) -> p t n", t=8)]
        UU = R(26, 2)
        T4 = [Rf(20, 4), Rf(28, 4)]
        GATE_AHEAD = R(10, 2)
        WGLU = Rf(8, 2).rearrange("p (k c) -> p k c", k=2)
        YS, GE = R(20, 2), R(22, 2)
        CT = YR[:, 4, :].rearrange("p (r c) -> p r c", r=2)
        PW = sb("s5_pw", [P, 2, 9, 8])
        PS = sb("s5_small", [P, 24, 8])
        S5T = [sb("s5_tmp", [P, 32]), PS[:, 19:23, :].rearrange("p a b -> p (a b)")]
        s_names = ("prm", "sin_in", "sin_ready", "xp_zero", "xp_ready", "cp_ready", "ct_done", "ct_ready", "bt_done", "bt_ready", "kk_done", "kk_ready",
                   "cl_ready", "u_ready", "w_done", "u4_in", "x_ready", "y_done", "wglu_in", "ys_ready", "sq", "poly", "tanh",
                   "ge_ready", "glu_done", "val_ready")
        ss = {n: sem("s5_" + n) for n in s_names}

        MHhi = YS_R[:, 8:16, :]
        MHlo = YS_R[:, 16:24, :]
        MBASE = Rf(28, 4).rearrange("p (k m) -> p k m", k=KC)
        MMhi = YS_R[:, 28:32, :].rearrange("p a b -> p (a b)").rearrange("p (k m) -> p k m", k=KC)
        MMlo = YS_R[:, 32:36, :].rearrange("p a b -> p (a b)").rearrange("p (k m) -> p k m", k=KC)
        MMX = Rf(16, 4).rearrange("p (k m) -> p k m", k=KC)
        KTt = Rf(28, 4).rearrange("p (k m) -> p k m", k=KC)
        VM = YR[:, 0:4, :].rearrange("p a b -> p (a b)").rearrange("p (m c) -> p m c", m=2)
        PB = [Rf(0, 2).rearrange("p (t m) -> p t m", t=TT), Rf(2, 2).rearrange("p (t m) -> p t m", t=TT)]
        PTB = [R(4, 2), R(6, 2)]
        AST = PS[:, 0:8, :].rearrange("p a b -> p (a b)").rearrange("p (n t) -> p n t", n=4)
        a_names = ("base_free", "mem_base_in", "mmx", "mm_hi", "mm_ready", "kt_ready", "vm_ready", "q_ready", "sc_done", "mx_ready", "p_exp", "p_ready",
                   "pt_done", "pt_ready", "o_done", "oc_ready", "ohi_ready", "osplit_ready")
        at = {n: sem("attn_" + n) for n in a_names}
        ASB = [M[0:2], G[psum_set("o0")[0]]]
        APT, AOB = M[2:4], G[psum_set("o1")[0]]
        up_a, up_v, uphi, uplo = sem("up_relu"), sem("up_squared"), sem("up_hi"), sem("up_ready")
        FB = [G[0], G[1], M[0:2], M[2:4]]
        UPX = R(32, 1)
        NS = R(32)[:, 0, :]
        MHID = [[YS_R[:, 16 * b + 8 * p:16 * b + 8 * p + 8, :] for p in range(2)] for b in range(2)]

        YB = [[YS_R[:, 4 * b:4 * b + 2, :], YS_R[:, 4 * b + 2:4 * b + 4, :]] for b in range(2)]
        BRANCH_AT = {3: 0, 1: 1, 0: 0, 2: 1}
        BRANCH_NO = {3: 0, 1: 1, 0: 2, 2: 3}

        block = ctx.enter_context(nc.Block())

        def chained(eng, chain):
            count = {}

            def do(ins, s=None):
                s = chain if s is None else s
                count[s.name] = count.get(s.name, 0) + 1
                ins.then_inc(s, 1)
                eng.wait_ge(s, count[s.name])
            return do

        @block.sync
        def _(sp):
            for t in range(TT):
                sp.dma_start(R(2 * t, 2).rearrange("p a b -> p (a b)"), x[0, t * P:(t + 1) * P, :]).then_inc(p_x, 16)
            sp.dma_start(CO[:, :], consts).then_inc(p_x, 16)
            sp.dma_start(R(8, 4).rearrange("p (t a) b -> p t (a b)", t=2),
                         mem[0].rearrange("(t p) d -> p t d", p=P)).then_inc(p_dma, 16)
            sp.dma_start(LM[:, :, :], level_masks.rearrange("p (l c) -> p l c", c=CH)).then_inc(p_dma, 16)
            sp.wait_ge(p_vec, 1)
            for l in range(DEPTH):
                stage = Rf(20 + l, 1)[:, 0:P]
                for name, src in (("norm_mix", norm_mix), ("norm_xattn", norm_xattn), ("norm_mem", norm_mem),
                                  ("norm_mlp", norm_mlp), ("mlstm_conv_b", mlstm_conv_b), ("mlstm_norm", mlstm_norm),
                                  ("gla_norm", gla_norm), ("hgrn_norm", hgrn_norm), ("gla_b_a", gla_b_a),
                                  ("s5_b_glu", s5_b_glu)):
                    n = src.shape[1] // P
                    sp.dma_start(stage[PROW[name]:PROW[name] + n, :],
                                 src[l].rearrange("(a b) -> a b", b=P)).then_inc(p_rows, 16)
                sp.dma_start(stage[PROW["mlstm_conv_w"]:PROW["mlstm_conv_w"] + 16, :],
                             mlstm_conv_w[l].rearrange("k (a b) -> (k a) b", b=P)).then_inc(p_rows, 16)
                sp.dma_start(stage[PROW["s5_d"]:PROW["s5_d"] + 2, :],
                             s5_d[l].rearrange("(a g) h -> a (g h)", a=2)).then_inc(p_rows, 16)
                for name, src in (("s5_lam_re", s5_lam_re), ("s5_lam_im", s5_lam_im)):
                    sp.dma_start(stage[PROW[name]:PROW[name] + 8, :],
                                 src[l].rearrange("(t a) q -> t (a q)", a=2)).then_inc(p_rows, 16)
                for m in range(2):
                    sp.dma_start(stage[PROW[f"lb{m}"]:PROW[f"lb{m}"] + 2, :],
                                 hgrn_lb_logits[m].rearrange("(a b) -> a b", b=P)).then_inc(p_rows, 16)
                sp.dma_start(stage[PROW["norm_final"]:PROW["norm_final"] + 8, :],
                             norm_final.rearrange("(a b) -> a b", b=P)).then_inc(p_rows, 16)
                r = PROW["if_bias"]
                sp.dma_start(stage[r:r + 1, 0:4], mlstm_i_bias[l:l + 1, :]).then_inc(p_rows, 16)
                sp.dma_start(stage[r:r + 1, 32:36], mlstm_f_bias[l:l + 1, :]).then_inc(p_rows, 16)
                for a in range(2):
                    src = s5_log_step[l].rearrange("(t a) -> a t", a=2)[a:a + 1, :]
                    sp.dma_start(SM[64 * a:64 * a + 64, 16 + 8 * l:24 + 8 * l],
                                 src.to_broadcast([64, 8]), allow_slow_non_contiguous=True).then_inc(p_rows, 16)
            sp.wait_ge(p_vec, 4)
            sp.dma_start(mem_scratch, Rf(28, 4)).then_inc(p_out, 16)
            sp.wait_ge(layer_go, 1)

            with sp.Fori(0, DEPTH) as L:
                for u, (name, part) in enumerate(UNITS):
                    row = 0 if part == "first" else D // 2

                    def rows(src, c, r0=0):
                        return src[r0 + row:r0 + row + D // 2, c:c + BW]

                    if name == "narrow":
                        src = None
                    elif name.startswith("branch"):
                        b, c = int(name[6]), int(name[8])
                        src = w_branch[L][b, :, c * BW:(c + 1) * BW]
                    elif name == "g_qk":
                        src = rows(w_in[L], COL["g_q"])
                    elif name in COL:
                        src = rows(w_in[L], COL[name])
                    elif name.startswith("gate"):
                        src = rows(w_in[L], COL["gates"] + int(name[4]) * D + int(name[6]) * BW)
                    elif name.startswith("out"):
                        src = rows(w_out[L], int(name[3]) * BW)
                    elif name.startswith("kv"):
                        src = rows(xattn_w_kv[L], int(name[2]) * BW)
                    elif name.startswith("q"):
                        src = rows(xattn_w_q[L], int(name[1]) * BW)
                    elif name.startswith("o"):
                        src = rows(xattn_w_o[L], int(name[1]) * BW)
                    elif name.startswith("up"):
                        src = rows(mlp_w1[L], (4 * int(name[2]) + int(name[4])) * BW)
                    else:
                        src = rows(mlp_w2[L], int(name[6]) * BW, int(name[4]) * D)
                    k = 2 if name.startswith("branch") else 4
                    if u == 2:
                        sp.wait_ge(p_out, 16)
                    if u >= RAW:
                        sp.wait_ge(split_ready, u - RAW + 1)
                    if name == "narrow":
                        dst = WR[:, u % RAW, 0:k * NARROW].rearrange("p (k c) -> p k c", k=k)
                        for n_, (what, wide, to) in enumerate((("m_i", 4, 0), ("m_f", 4, 32), ("g_a", 16, 64))):
                            src = w_in[L][row:row + D // 2, COL[what]:COL[what] + wide].rearrange("(k p) c -> p k c", p=P)
                            sp.dma_start(dst[:, :, to:to + wide], src, allow_slow_non_contiguous=True).then_inc(raw_in[u % RAW], 16)
                    else:
                        sp.dma_start(WR[:, u % RAW, 0:k * BW].rearrange("p (k c) -> p k c", k=k),
                                     src.rearrange("(k p) c -> p k c", p=P)).then_inc(raw_in[u % RAW], 16)
                    if u == 2:
                        sp.dma_start(WA2[:, :], gla_w_a2[L]).then_inc(params_in, 16)
                        for r, (b, c) in enumerate(((s5_b_re, s5_c_re), (s5_b_im, s5_c_im))):
                            sp.dma_start(BRI[:, r, :, :], b[L].rearrange("(t a) q h -> (a q) t h", a=2)).then_inc(params_in, 16)
                            sp.dma_start(CRI[:, r, :, :], c[L].rearrange("(f g) h q -> (g h) f q", f=2)).then_inc(params_in, 16)
                    if (name, part) == ("gate0_2", "last"):
                        sp.wait_ge(ss["u_ready"], 2)
                        sp.wait_ge(ss["ct_done"], 1)
                        for i4 in range(4):
                            for uu in range(4):
                                for q in range(2):
                                    j = S5_T - 1 - 4 * q - uu
                                    src = UU[32 * i4:32 * i4 + 32, :, :].rearrange("p f (j n) -> p f j n", j=S5_T)[:, :, j, :]
                                    sp.dma_start(U4[32 * uu:32 * uu + 32, i4::4, q, :], src).then_inc(ss["u4_in"], 16)
                    if name == "branch0_3":
                        sp.wait_ge(ss["w_done"], 1)
                        sp.dma_start(WGLU, s5_w_glu[L].rearrange("(k p) c -> p k c", p=P)).then_inc(ss["wglu_in"], 16)
                    if name == "branch2_1":
                        sp.wait_ge(at["base_free"], 1)
                        sp.dma_start(Rf(28, 4), mem_scratch).then_inc(at["mem_base_in"], 16)
                sp.wait_ge(layer_end, 4 * L + 4)
                sp.sem_inc(all_ended, 1)
                sp.wait_ge(params_in, 16 * 5)
                sp.wait_ge(all_ended, 1)
                nums = sorted(s.num for s in layer_sems)
                assert nums == list(range(nums[0], nums[-1] + 1))
                sp.sem_clear(range(nums[0], nums[-1] + 1)).then_inc(layer_go, 1)
            for t in range(TT):
                sp.wait_ge(f_act, 2 + t + 1)
                sp.wait_ge(f_vec, KC + t + 1)
                sp.dma_start(out[0, t * P:(t + 1) * P, :], flat(R(2 * t, 2))).then_inc(p_out, 16)
            sp.wait_ge(p_out, 16 + 16 * TT)

        def wait_for_half_block(eng, u):
            eng.wait_ge(raw_in[u % RAW], COME[u])
            if BEFORE[u] is not None:
                before, its_part = UNITS[BEFORE[u]]
                if its_part == "first":
                    eng.wait_ge(split_used, FIRSTS[BEFORE[u]])
                else:
                    bank_set, used = psum_set(before)
                    eng.wait_ge(gemm_done[bank_set], 2 * used + 2)
            name = UNITS[u][0]
            w = 2 * BW if name.startswith("branch") else 4 * NARROW if name == "narrow" else 4 * BW
            at_ = SLOT[u] * 4 * BW
            return WR[:, u % RAW, 0:w], WHi[:, at_:at_ + w], WLo[:, at_:at_ + w]

        @block.gpsimd
        def _(pool):
            pool.wait_ge(layer_go, 1)
            with pool.Fori(0, DEPTH) as L:
                own = 0
                for u, (name, part) in enumerate(UNITS):
                    raw, hi, lo = wait_for_half_block(pool, u)
                    if u in BY_VECTOR:
                        pool.wait_ge(split_hi_vector, BY_VECTOR.index(u) + 1)
                    elif u in BY_SCALAR:
                        pool.wait_ge(split_hi_scalar, BY_SCALAR.index(u) + 1)
                    else:
                        own += 1
                        pool.tensor_tensor(hi, raw, SM[:, 62:63].to_broadcast([P, hi.shape[1]]), ALU.mult).then_inc(split_hi, 1)
                        pool.wait_ge(split_hi, own)
                    pool.tensor_tensor(lo, raw, hi.bitcast(F32), ALU.subtract).then_inc(split_ready, 1)
                pool.wait_ge(split_ready, NUNIT)
                pool.nop().then_inc(layer_end, 1)
                pool.wait_ge(layer_go, L + 2)

        @block.tensor
        def _(pe):
            def mm(o, w, a, start=True, stop=True):
                return pe.matmul(o, w, a, start=start, stop=stop, skip_group_check=True)

            pe.wait_ge(p_x, 16 * 5)
            for n in range(8):
                if n >= 4:
                    pe.wait_ge(p_act, 1 + n - 4)
                for t in range(TT):
                    i = pe.transpose(M[n % 4][:, t * P:(t + 1) * P], Rf(2 * t + n // 4, 1)[:, (n % 4) * P:(n % 4 + 1) * P], ident)
                i.then_inc(p_pe, 1)
            pe.wait_ge(p_act, 8)
            pe.wait_ge(p_vec, 2)
            for n in range(4):
                for k in range(2):
                    for t in range(2):
                        kc = 2 * n + k
                        i = pe.transpose(M[n][:, k * 256 + t * P:k * 256 + (t + 1) * P],
                                         Rf(8 + 2 * t + kc // 4, 1)[:, (kc % 4) * P:(kc % 4 + 1) * P], ident)
                i.then_inc(p_pe, 1)
            pe.wait_ge(p_rows, 16 * 21 * DEPTH)
            for l in range(DEPTH):
                i = pe.transpose(G[0][l][:, 0:P], Rf(20 + l, 1)[:, 0:P], ident)
            i.then_inc(p_pe, 1)
            pe.wait_ge(layer_go, 1)

            def gemm(name, hi, lo, kind="fm", n=SEQ, ready=None, ready_at=0, kcs=4):
                s, used = psum_set(name)
                if used:
                    pe.wait_ge(gemm_free[s], 2 * used)
                u0, units = UNIT[name], (1 if name.startswith("branch") else 2)
                for un in range(units):
                    u = u0 + un
                    wide = NARROW if kind == "narrow" else BW
                    w_at = lambda W, k, c, m: W[:, 4 * SLOT[u] * BW + k * wide + c:4 * SLOT[u] * BW + k * wide + c + m]
                    nt = {"fm": 2, "tm": n // P, "narrow": 1}[kind]
                    first = True
                    for reg in range(nt):
                        for k in range(kcs):
                            kc = kcs * un + k
                            if ready is not None and reg == 0:
                                pe.wait_ge(ready, ready_at + kc + 1)
                            if first:
                                pe.wait_ge(split_ready, u + 1)
                                first = False
                            last = kc == kcs * units - 1
                            if kind == "fm":
                                o = G[s][reg][:, 0:n]
                                ops = ((w_at(WHi, k, reg * P, P), hi(kc)), (w_at(WHi, k, reg * P, P), lo(kc)),
                                       (w_at(WLo, k, reg * P, P), hi(kc)))
                                start = kc == 0
                                ends = last
                            elif kind == "narrow":
                                o = G[s][0][0:NARROW, :]
                                ops = ((w_at(WHi, k, 0, NARROW), hi(kc)), (w_at(WHi, k, 0, NARROW), lo(kc)),
                                       (w_at(WLo, k, 0, NARROW), hi(kc)))
                                start = kc == 0
                                ends = last
                            else:
                                per = 2 if nt == 4 else 1
                                o = G[s][reg // per][:, (reg % per) * BW:(reg % per) * BW + BW]
                                tok = slice(reg * P, reg * P + P)
                                ops = ((hi(kc)[:, tok], w_at(WHi, k, 0, BW)), (lo(kc)[:, tok], w_at(WHi, k, 0, BW)),
                                       (hi(kc)[:, tok], w_at(WLo, k, 0, BW)))
                                start = kc == 0 and reg % per == 0
                                ends = last and reg % per == per - 1
                            for q, (a, b) in enumerate(ops):
                                i = mm(o, a, b, start=start and q == 0, stop=last and q == 2)
                            if ends:
                                i.then_inc(gemm_done[s], 2 if kind == "narrow" else 1)
                    if un < units - 1:
                        i.then_inc(split_used, 1)

            def norm(n):
                if n:
                    pe.wait_ge(sq_used, 7 * n)
                mm(M[3][:, :], mean_w, NS).then_inc(ms_done, 1)

            def scores(m, l):
                if l == 0:
                    pe.wait_ge(m.kq_ready, 3 - m.J)
                    if m.J == 2:
                        pe.wait_ge(m.g_ready, 5)
                    else:
                        pe.wait_ge(head_rs, 4)
                else:
                    pe.wait_ge(m.x_ready, l)
                if m.J == 2 and l >= 2:
                    pe.wait_ge(m.picked, 2 * (l - 1))
                if m.J == 1 and l >= 1:
                    pe.wait_ge(m.picked, 4 * l)
                kk, qq = (m.K, m.Q) if l == 0 else (m.X[l % 2], m.X[l % 2])
                for h in range(4):
                    rows = slice(m.dk * (h % m.per), m.dk * (h % m.per) + m.dk)
                    base = (h // m.per) * SEQ
                    for c in range(NCH):
                        at_ = m.score_cols(h) + (c // 2) * CH
                        tok = slice(base + c * CH, base + c * CH + CH)
                        i = mm(m.score_bank(l, h)[64 * (c % 2):64 * (c % 2) + 64, at_:at_ + CH], kk[rows, tok], qq[rows, tok])
                i.then_inc(m.lev_done, 1)

            def state_in(m):
                pe.wait_ge(m.kd_ready, 1)
                pe.wait_ge(m.picked, 2 * 7 if m.J == 2 else 4 * 7)
                for j in range(m.J):
                    for t in range(TT):
                        i = pe.transpose(M[j][:, t * P:(t + 1) * P], m.E[0][:, j * SEQ + t * P:j * SEQ + (t + 1) * P], ident)
                    i.then_inc(m.kt_done, 1)
                pe.wait_ge(m.kt_ready, m.J)
                pe.wait_ge(m.v_ready, 2)
                for h in range(4):
                    r0 = m.dk * (h % m.per)
                    for c in range(NCH):
                        p0 = 64 * (c % 2)
                        at_ = (h // m.per) * 256 + (c // 2) * HD
                        i = mm(M[2 + c % 2][r0:r0 + m.dk, at_:at_ + HD], m.KT[p0:p0 + 64, c // 2, m.dk * h:m.dk * h + m.dk],
                               m.V[p0:p0 + 64, c // 2, HD * h:HD * h + HD])
                i.then_inc(m.kv_done, 1)

            def outputs(m):
                pe.wait_ge(m.bd_ready, 1)
                pe.wait_ge(m.s_ready, 2)
                for h in range(4):
                    rows = slice(64 * (h % 2), 64 * (h % 2) + 64)
                    j, jt = h // 2, h // m.per
                    for t in range(TT):
                        mm(M[j][rows, t * P:(t + 1) * P], m.V[:, t, HD * h:HD * h + HD], m.attbd[:, m.slot(h), t, :], stop=False)
                        for c in (2 * t, 2 * t + 1):
                            if c:
                                i = mm(M[j][rows, c * CH:(c + 1) * CH], m.S[:, jt, c - 1, HD * (h % m.per):HD * (h % m.per) + HD],
                                       m.Q[:, jt * SEQ + c * CH:jt * SEQ + (c + 1) * CH], start=False, stop=True)
                    if h % 2:
                        i.then_inc(m.o_done, 1)

            def head_norm(n, sq):
                for j in range(2):
                    pe.wait_ge(head_sq, 2 * n + j + 1)
                    mm(M[2 + j][:, :], head_mean, sq[:, j, :]).then_inc(head_ms, 1)

            H = (lambda k: Hhi[:, k, :], lambda k: Hlo[:, k, :])

            def gate_gemm(n, c):
                gemm(f"gate{n}_{c}", *H)

            def branch_gemm(n, c):
                if c == 0:
                    pe.wait_ge(y_ready, 2 * BRANCH_NO[n] + 2)
                y = YB[BRANCH_AT[n]]
                gemm(f"branch{n}_{c}", lambda k: y[0][:, k, :], lambda k: y[1][:, k, :], kcs=2)

            with pe.Fori(0, DEPTH) as L:
                norm(0)
                gemm("r_f", *H, ready=h_ready)
                gemm("r_q", *H)
                gemm("r_i", *H, kind="tm")
                gemm("g_qk", *H)
                gemm("narrow", *H, kind="narrow")
                scores(hg, 0)
                gemm("g_v", *H, kind="tm")
                pe.wait_ge(ga_ready, 3)
                pe.wait_ge(params_in, 16 * 5)
                mm(M[2][:, :], WA2[:, :], R(32)[0:RANK, 0, :]).then_inc(ga_done, 1)
                gemm("g_r", *H)
                pe.wait_ge(gl.gate_in, 2)
                scores(hg, 1)
                scores(hg, 2)
                gemm("r_g", *H)
                scores(hg, 3)
                scores(hg, 4)
                gate_gemm(3, 0)
                scores(hg, 5)
                scores(hg, 6)
                state_in(hg)
                gemm("m_q", *H)
                outputs(hg)
                head_norm(0, hg.SQ)
                gemm("m_k", *H)
                scores(gl, 0)
                gemm("m_v", *H, kind="tm")
                scores(gl, 1)
                gemm("m_o", *H)
                scores(gl, 2)
                branch_gemm(3, 0)
                scores(gl, 3)
                gate_gemm(3, 1)
                scores(gl, 4)
                branch_gemm(3, 1)
                scores(gl, 5)
                gate_gemm(3, 2)
                scores(gl, 6)
                branch_gemm(3, 2)
                state_in(gl)
                gate_gemm(3, 3)
                branch_gemm(3, 3)
                outputs(gl)
                head_norm(1, gl.SQ)
                gemm("s_u", *H)
                gate_gemm(1, 0)

                pe.wait_ge(ms["stack_ready"], 1)
                for t in range(TT):
                    i = pe.transpose(M[0][:, t * 64:(t + 1) * 64], R(23)[0:64, 0, t * P:(t + 1) * P], ident[0:64, 0:64])
                i.then_inc(ms["aw_done"], 1)
                pe.wait_ge(head_rs, 8)
                for j in range(2):
                    mm(M[1 + j][:, :], pair_sel[0:4, j, :], R(24)[0:4, 0, :]).then_inc(ms["ib_done"], 1)
                pe.wait_ge(ms["aw_ready"], 1)
                for j in range(2):
                    mm(M[3 if j == 0 else 0][:, :], pair_sel[0:4, j, :], R(28)[0:4, 0, :]).then_inc(ms["ib_done"], 1)
                branch_gemm(1, 0)
                gate_gemm(1, 1)
                pe.wait_ge(ms["ib_ready"], 4)
                pe.wait_ge(ms["emb_ready"], 2)
                bm = R(22)[0:4, 0, :].rearrange("p (t a c) -> p t a c", a=2, c=CH)
                for hp in range(2):
                    mm(M[hp][:, :], ident, bc(neg_mask, 1, 8), stop=False)
                    for j in range(2):
                        for a in range(2):
                            i = mm(M[hp][64 * a:64 * a + 64, j * 256:j * 256 + 256], head_sel[0:4, 2 * j + hp, :], bm[:, :, a, :],
                                   start=False, stop=j == 1)
                    i.then_inc(ms["mex_done"], 1)
                for h in range(4):
                    rows = slice(64 * (h % 2), 64 * (h % 2) + 64)
                    for c in range(NCH):
                        tok = slice(c * CH, c * CH + CH)
                        at_ = (h // 2) * 256 + (c // 2) * CH
                        i = mm(M[2 + h % 2][64 * (c % 2):64 * (c % 2) + 64, at_:at_ + CH], MQK[2 + h // 2][rows, tok], MQK[h // 2][rows, tok])
                i.then_inc(ms["mqk_done"], 1)
                branch_gemm(1, 1)
                pe.wait_ge(ms["mex_v"], 2)
                for j in range(2):
                    for t in range(TT):
                        i = pe.transpose(M[j][:, t * P:(t + 1) * P], MQK[2 + j][:, t * P:(t + 1) * P], ident)
                    i.then_inc(ms["mkt_done"], 1)
                gate_gemm(1, 2)
                pe.wait_ge(ms["mkt_ready"], 2)
                pe.wait_ge(ms["matt_ready"], 2)
                pe.wait_ge(ms["mv_ready"], 2)
                for h in range(4):
                    rows = slice(64 * (h % 2), 64 * (h % 2) + 64)
                    for c in range(NCH):
                        p0 = 64 * (c % 2)
                        bank = M[2 * (c % 2) + h // 2]
                        at_ = (c // 2) * 128
                        w = MKT[p0:p0 + 64, c // 2, h // 2, h % 2, :]
                        mm(bank[rows, at_:at_ + 64], w, MV[p0:p0 + 64, c // 2, HD * h:HD * h + HD])
                        i = mm(bank[rows, at_ + 64:at_ + 128], w, ones64[p0:p0 + 64, :])
                i.then_inc(ms["mkv_done"], 1)
                branch_gemm(1, 2)
                gate_gemm(1, 3)
                pe.wait_ge(ms["mbd_ready"], 1)
                pe.wait_ge(ms["ms_ready"], 2)
                for h in range(4):
                    rows = slice(64 * (h % 2), 64 * (h % 2) + 64)
                    j, hp = h // 2, h % 2
                    for part in range(2):
                        bank = M[2 * part + j]
                        for t in range(TT):
                            w = MV[:, t, HD * h:HD * h + HD] if part == 0 else ones64
                            i = mm(bank[rows, t * P:(t + 1) * P], w, MBD[:, hp * 2 + j, t, :], stop=False)
                            for c in (2 * t, 2 * t + 1):
                                if c:
                                    i = mm(bank[rows, c * CH:(c + 1) * CH], MS[j][:, c - 1, hp, 64 * part:64 * part + 64],
                                           MQT[:, j, c * CH:(c + 1) * CH], start=False, stop=True)
                i.then_inc(ms["mo_done"], 1)
                branch_gemm(1, 3)
                gate_gemm(0, 0)
                head_norm(2, MSQ)

                gate_gemm(0, 1)
                branch_gemm(0, 0)
                pe.wait_ge(ss["cp_ready"], 2)
                for r in range(2):
                    for f in range(2):
                        i = pe.transpose(M[0][:, (2 * r + f) * P:(2 * r + f + 1) * P], R(24 + r)[:, 0, f * P:(f + 1) * P], ident)
                i.then_inc(ss["ct_done"], 1)
                pe.wait_ge(head_rs, 12)
                for n in range(8):
                    r, t0 = n // 4, 2 * (n % 4)
                    pe.wait_ge(ss["xp_ready"], r + 1)
                    if n >= 3:
                        pe.wait_ge(ss["bt_ready"], n - 2)
                    for t in range(2):
                        for q in range(2):
                            i = pe.transpose(M[1 + n % 3][:, (2 * t + q) * P:(2 * t + q + 1) * P],
                                             flat(XP[:, r, 4 * q:4 * q + 4, t0 + t, :]), ident)
                    i.then_inc(ss["bt_done"], 1)
                pe.wait_ge(ss["cp_ready"], 3)
                kk = M[0][:, :].rearrange("p (f u c) -> p f u c", f=2, u=8)
                for f in range(2):
                    for u in range(8):
                        for i4 in range(4):
                            t = 4 * f + i4
                            for r in range(2):
                                i = mm(kk[32 * i4:32 * i4 + 32, f, u, :], XP[:, r, u, t, :], CT[:, r, 32 * t:32 * t + 32],
                                       start=r == 0, stop=r == 1)
                i.then_inc(ss["kk_done"], 1)
                branch_gemm(0, 1)
                gate_gemm(0, 2)
                pe.wait_ge(ss["u_ready"], 2)
                pe.wait_ge(ss["bt_ready"], 8)
                pe.wait_ge(ss["kk_ready"], 4)
                pe.wait_ge(ss["u4_in"], 16 * 32)
                un = UU[:, :, :].rearrange("p f (j n) -> p f j n", j=S5_T)
                for t in range(8):
                    for r in range(2):
                        for q in range(2):
                            at_ = (2 * (t // 4) + r) * 64
                            i = mm(M[t % 4][:, at_:at_ + 64], BT[:, t, r, q, :], U4[:, t, q, :], start=q == 0, stop=q == 1)
                i.then_inc(ss["w_done"], 1)
                branch_gemm(0, 2)
                gate_gemm(0, 3)
                branch_gemm(0, 3)
                pe.wait_ge(ss["cl_ready"], 1)
                pe.wait_ge(ss["x_ready"], 1)
                for f in range(2):
                    for d in range(S5_T):
                        mm(M[f][:, d * 64:512], KTm[:, f, d, :], flat(un[:, f, 0:S5_T - d, :]), start=d == 0, stop=False)
                    for j in range(S5_T):
                        for i4 in range(4):
                            t = 4 * f + i4
                            for r in range(2):
                                i = mm(M[f][32 * i4:32 * i4 + 32, j * 64 + 1:j * 64 + 64], CL[:, r, j, t, :], SX[r][:, t, 0:63],
                                       start=False, stop=r == 1)
                    i.then_inc(ss["y_done"], 1)
                gate_gemm(2, 0)
                pe.wait_ge(ss["wglu_in"], 16)
                pe.wait_ge(ss["ge_ready"], 2)
                for n in range(4):
                    for k in range(2):
                        i = mm(M[n][:, :], WGLU[:, k, n * P:(n + 1) * P], GE[:, k, :], start=k == 0, stop=k == 1)
                    i.then_inc(ss["glu_done"], 1)
                gate_gemm(2, 1)
                branch_gemm(2, 0)
                branch_gemm(2, 1)
                for c in (2, 3):
                    gate_gemm(2, c)
                    branch_gemm(2, c)

                for c in range(4):
                    gemm(f"out{c}", lambda k: MHhi[:, k, :], lambda k: MHlo[:, k, :], ready=mgs_ready if c == 0 else None)
                mmin = (lambda k: MMhi[:, k, :], lambda k: MMlo[:, k, :])
                gemm("kv0", *mmin, n=MEM, ready=at["mm_ready"])
                norm(1)
                for c in range(1, 4):
                    gemm(f"kv{c}", *mmin, n=MEM)
                def attn_scores(h):
                    pe.wait_ge(at["q_ready"], 2 * h + 2)
                    if h >= 2:
                        pe.wait_ge(at["p_exp"], 4 * (h - 1))
                    for t in range(TT):
                        for k in range(2):
                            i = mm(ASB[h % 2][t // 2][:, (t % 2) * 256:(t % 2) * 256 + 256], MG[:, 2 * h + k, t * P:(t + 1) * P],
                                   KTt[:, 2 * h + k, :], start=k == 0, stop=k == 1)
                    i.then_inc(at["sc_done"], 1)

                for c in range(4):
                    gemm(f"q{c}", *H, ready=h_ready if c == 0 else None, ready_at=8)
                    gemm(f"kv{4 + c}", *mmin, kind="tm", n=MEM)
                    if c == 2:
                        pe.wait_ge(at["kt_ready"], 8)
                        attn_scores(0)
                pe.wait_ge(at["vm_ready"], 8)
                pe.wait_ge(rstd_ready, 4)

                def attn_transposes(h):
                    pe.wait_ge(at["p_ready"], 4 * h + 4)
                    if h:
                        pe.wait_ge(at["pt_ready"], 2 * h)
                    for m in range(2):
                        for t in range(TT):
                            i = pe.transpose(APT[m][:, t * P:(t + 1) * P], PB[h % 2][:, t, m * P:(m + 1) * P], ident)
                        i.then_inc(at["pt_done"], 1)

                def attn_out(h):
                    pe.wait_ge(at["pt_ready"], 2 * h + 2)
                    if h:
                        pe.wait_ge(at["oc_ready"], 2 * h)
                    for k in range(2):
                        for m in range(2):
                            i = mm(AOB[k][:, :], VM[:, m, h * 256 + k * P:h * 256 + (k + 1) * P], PTB[h % 2][:, m, :],
                                   start=m == 0, stop=m == 1)
                        i.then_inc(at["o_done"], 1)

                attn_scores(1)
                for h in range(4):
                    attn_transposes(h)
                    if h < 2:
                        attn_scores(h + 2)
                    attn_out(h)
                for c in range(4):
                    if c == 1:
                        pe.wait_ge(at["oc_ready"], 8)
                    gemm(f"o{c}", *H, ready=at["osplit_ready"] if c == 0 else None)
                norm(2)
                done = 0
                for q in (0, 1):
                    for c in range(4):
                        gemm(f"up{q}_{c}", *H, ready=h_ready if (q, c) == (0, 0) else None, ready_at=16)

                def down(q):
                    hb = MHID[q % 2]
                    for c in range(4):
                        gemm(f"down{q}_{c}", lambda k: hb[0][:, k, :], lambda k: hb[1][:, k, :],
                             ready=uplo if c == 0 else None, ready_at=8 * q)

                down(0)
                for c in range(4):
                    gemm(f"up2_{c}", *H)
                down(1)
                for c in range(4):
                    gemm(f"up3_{c}", *H)
                down(2)
                down(3)
                pe.nop().then_inc(layer_end, 1)
                pe.wait_ge(layer_go, L + 2)

            mm(M[3][:, :], mean_w, NS).then_inc(f_pe, 1)
            for k in range(KC):
                pe.wait_ge(f_vec, k + 1)
                for t in range(TT):
                    i = pe.transpose(FB[t][k // 4][:, (k % 4) * P:(k % 4 + 1) * P], MG[:, k, t * P:(t + 1) * P], ident)
                    if k == 7:
                        i.then_inc(f_pe, 1)
                if k == 3:
                    i.then_inc(f_pe, 1)

        @block.scalar
        def _(act):
            do = chained(act, a_chain)
            def pdo(ins, n=[0]):
                n[0] += 1
                ins.then_inc(p_act, 1)
                act.wait_ge(p_act, n[0])
            for n in range(8):
                act.wait_ge(p_pe, n + 1)
                pdo(act.activation(X[:, n, :], M[n % 4][:, :], ACT.Copy))
            act.wait_ge(p_dma, 32)
            act.preload_act_table_set(LOG_SET)
            for t in range(2):
                pdo(act.activation(flat(R(12 + 2 * t, 2)), flat(R(8 + 2 * t, 2)), ACT.Square, accum_out=SM[:, 40 + t:41 + t]))
            act.wait_ge(p_vec, 1)
            pdo(act.activation(SM[:, 42:44], SM[:, 40:42], ACT.Ln, scale=1.0 / D, bias=SM[:, 63:64]))
            pdo(act.activation(SM[:, 44:46], SM[:, 42:44], ACT.Exp, scale=-0.5))
            for n in range(8):
                act.activation(MG[:, n, :], X[:, n, :], ACT.Square).then_inc(p_sq, 1)
            for n in range(4):
                act.wait_ge(p_pe, 9 + n)
                pdo(act.activation(R(28 + n)[:, 0, :], M[n][:, :], ACT.Copy))
            act.wait_ge(p_vec, 3)
            pdo(act.activation(PS[:, 0:2, 0:2], PS[:, 0:2, 0:2], ACT.Abs))
            pdo(act.activation(PS[:, 0:2, 0:2], PS[:, 0:2, 0:2], ACT.Exp, scale=-1.0))
            pdo(act.activation(PS[:, 0:2, 0:2], PS[:, 0:2, 0:2], ACT.Ln, bias=SM[:, 62:63]))
            act.wait_ge(layer_go, 1)
            eps, one = SM[:, 63:64], SM[:, 62:63]

            def round_up(u):
                raw, hi, _ = wait_for_half_block(act, u)
                do(act.activation(hi, raw, ACT.Copy), split_hi_scalar)

            def squares(n):
                for k in range(KC):
                    act.wait_ge(x_ready, (0, 0, 8, 40)[n] + k + 1)
                    if k == 1 and n == 1:
                        act.wait_ge(th_used, th_n[0])
                    if k >= 3:
                        act.wait_ge(sq_used, 7 * (n - 1) + k - 2)
                    do(act.activation(TH[:, k % 2, :] if k else NS, X[:, k, :], ACT.Square), sq_ready)

            def factors(n):
                act.preload_act_table_set(LOG_SET)
                act.wait_ge(ms_done, n + 1)
                do(act.activation(NS, M[3][:, :], ACT.Ln, bias=eps), rstd_ready)
                do(act.activation(NS, NS, ACT.Exp, scale=-0.5), rstd_ready)

            def norm_hi(n):
                for k in range(KC):
                    act.wait_ge(hx_ready, 8 * n + k + 1)
                    do(act.activation(Hhi[:, k, :], TH[:, k % 2, :], ACT.Copy), hi_ready)

            def banks(name):
                s, used = psum_set(name)
                for b in range(2):
                    act.wait_ge(gemm_done[s], 2 * used + b + 1)
                    yield b, G[s][b], gemm_free[s]

            th_n = [0]

            def tanh_out(name):
                s, used = psum_set(name)
                for b in range(2):
                    act.wait_ge(gemm_done[s], 2 * used + b + 1)
                    if th_n[0] >= 2:
                        act.wait_ge(th_used, th_n[0] - 1)
                    do(act.activation(TH[:, b, :], G[s][b][:, :], ACT.Tanh, scale=0.5), th_ready)
                    th_n[0] += 1

            def gate(n, c):
                s, used = psum_set(f"gate{n}_{c}")
                t = GATE_AHEAD if (n, c) == (2, 1) else TH
                for b in range(2):
                    act.wait_ge(gemm_done[s], 2 * used + b + 1)
                    if (n, c) != (2, 1):
                        act.wait_ge(th_used, th_n[0] - 1)
                    do(act.activation(t[:, b, :], G[s][b][:, :], ACT.Tanh, scale=0.5), th_ready)
                    act.nop().then_inc(gemm_free[s], 1)
                    th_n[0] += 1

            def level_exp(m, l):
                act.wait_ge(m.d_ready, 2 * l)
                do(act.activation(m.E[l % 2], m.E[l % 2], ACT.Exp, scale=m.gscale), m.e_ready)

            def decays(m):
                act.wait_ge(m.d_ready, 13)
                do(act.activation(m.E[0], m.E[0], ACT.Exp, scale=m.gscale), m.e_ready)
                do(act.activation(m.E[1], m.Gc, ACT.Exp, scale=m.gscale), m.e_ready)

            def kt_copy(m):
                for j in range(m.J):
                    act.wait_ge(m.kt_done, j + 1)
                    do(act.activation(m.KT[:, :, j * P:(j + 1) * P], M[j][:, :].rearrange("p (t c) -> p t c", t=TT), ACT.Copy), m.kt_ready)

            def head_out(m):
                for j in range(2):
                    act.wait_ge(m.o_done, j + 1)
                    do(act.activation(m.O[:, j, :], M[j][:, :], ACT.Copy, scale=m.oscale))
                    do(act.activation(m.SQ[:, j, :], M[j][:, :], ACT.Square, scale=m.oscale), head_sq)

            def head_rstd(n, sq):
                act.preload_act_table_set(LOG_SET)
                for j in range(2):
                    act.wait_ge(head_ms, 2 * n + j + 1)
                    do(act.activation(sq[:, j, :], M[2 + j][:, :], ACT.Ln, bias=eps), head_rs)
                    do(act.activation(sq[:, j, :], sq[:, j, :], ACT.Exp, scale=-0.5), head_rs)

            def y_split(n):
                no = BRANCH_NO[n]
                for j in range(2):
                    act.wait_ge(y_act, 2 * no + j + 1)
                    do(act.activation(YB[BRANCH_AT[n]][0][:, j, :], YSRC[n][:, j, :], ACT.Copy, scale=0.5), y_hi)

            YSRC = {3: hg.O, 1: gl.O, 0: MOO, 2: YS}

            with act.Fori(0, DEPTH) as L:
                factors(0)
                norm_hi(0)
                for b, bank, free in banks("r_f"):
                    do(act.activation(hg.E[0][:, b * SEQ:(b + 1) * SEQ], bank[:, :], ACT.Copy), hg.gate_in)
                    do(act.activation(hg.E[1][:, b * SEQ:(b + 1) * SEQ], bank[:, :], ACT.Abs))
                    act.nop().then_inc(free, 1)
                do(act.activation(hg.E[1], hg.E[1], ACT.Exp, scale=-1.0))
                do(act.activation(hg.E[1], hg.E[1], ACT.Ln, bias=one), hg.gate_in)
                act.wait_ge(hg.g_ready, 4)
                for j in range(2):
                    do(act.activation(hg.K[:, j * SEQ:(j + 1) * SEQ], hg.K[:, j * SEQ:(j + 1) * SEQ], ACT.Exp, bias=col("hg_c1", j)),
                       hg.kq_ready if j else None)
                do(act.activation(hg.X[1], hg.X[1], ACT.Abs))
                do(act.activation(hg.X[1], hg.X[1], ACT.Exp, scale=-1.0))
                do(act.activation(hg.X[1], hg.X[1], ACT.Ln, bias=one), hg.gate_in)
                tanh_out("r_q")
                for b, bank, free in banks("r_i"):
                    do(act.activation(hg.V[:, 2 * b:2 * b + 2, :], bank[:, :].rearrange("p (t c) -> p t c", t=2), ACT.Copy), hg.v_ready)
                    act.nop().then_inc(free, 1)
                for b, bank, free in banks("g_qk"):
                    do(act.activation(gl.Q if b == 0 else gl.K, bank[:, :], ACT.Copy), gl.kq_ready)
                    act.nop().then_inc(free, 1)
                def ps(n, w=1):
                    return PS[:, n:n + w, :]
                act.wait_ge(hx_ready, 1)
                do(act.activation(PS[:, 0, :], PT[:, PROW["step"]:PROW["step"] + 8], ACT.Exp), ss["sin_in"])
                act.wait_ge(ss["prm"], 1)
                for n in range(9):
                    do(act.activation(PS[:, 8 + n, :], PS[:, 1, :], ACT.Exp, scale=float(n)))
                do(act.activation(PS[:, 3, :], PS[:, 2, :], ACT.Abs))
                do(act.activation(PS[:, 4, :], PS[:, 2, :], ACT.Sin), ss["sin_in"])
                do(act.activation(PS[:, 3, :], PS[:, 3, :], ACT.Sin, scale=-1.0, bias=SM[:, 61:62]), ss["sin_ready"])
                s, used = psum_set("narrow")
                act.wait_ge(gemm_done[s], 2 * used + 2)
                act.wait_ge(h_ready, 8)
                do(act.activation(LP[0:4, :], G[s][0][0:4, :], ACT.Identity, bias=colr("if_bias", 0, slice(0, 4))))
                do(act.activation(LP[32:36, :], G[s][0][32:36, :], ACT.Identity, bias=colr("if_bias", 0, slice(32, 36))))
                do(act.activation(R(32)[0:RANK, 0, :], G[s][0][64:80, :], ACT.Copy), ga_ready)
                act.nop().then_inc(gemm_free[s], 2)
                act.wait_ge(hg.lev_done, 1)
                do(act.nop(), ga_ready)
                act.wait_ge(hg.picked, 2)
                do(act.nop(), ga_ready)
                for b, bank, free in banks("g_v"):
                    do(act.activation(gl.V[:, 2 * b:2 * b + 2, :], bank[:, :].rearrange("p (t c) -> p t c", t=2), ACT.Copy), gl.v_ready)
                    act.nop().then_inc(free, 1)
                act.wait_ge(ga_done, 1)
                do(act.activation(R(30)[:, 0, :], M[2][:, :], ACT.Identity, bias=col("gla_b_a")), gl.gate_in)
                do(act.activation(R(31)[:, 0, :], M[2][:, :], ACT.Abs, bias=col("gla_b_a")), gl.gate_in)
                act.preload_act_table_set(LOG_SET)
                do(act.activation(R(31)[:, 0, :], R(31)[:, 0, :], ACT.Exp, scale=-1.0))
                do(act.activation(R(31)[:, 0, :], R(31)[:, 0, :], ACT.Ln, bias=one), gl.gate_in)
                level_exp(hg, 1)
                level_exp(hg, 2)
                tanh_out("g_r")
                level_exp(hg, 3)
                level_exp(hg, 4)
                tanh_out("r_g")
                level_exp(hg, 5)
                level_exp(hg, 6)
                gate(3, 0)
                decays(hg)
                kt_copy(hg)
                head_out(hg)
                head_rstd(0, hg.SQ)
                for name, j0 in (("m_q", 0), ("m_k", 2)):
                    for b, bank, free in banks(name):
                        do(act.activation(CIN[:, j0 + b, 3:515], bank[:, :], ACT.Copy), ms["cin_ready"])
                        act.nop().then_inc(free, 1)
                y_split(3)
                level_exp(gl, 1)
                for b, bank, free in banks("m_v"):
                    do(act.activation(MV[:, 2 * b:2 * b + 2, :], bank[:, :].rearrange("p (t c) -> p t c", t=2), ACT.Copy), ms["mv_ready"])
                    act.nop().then_inc(free, 1)
                level_exp(gl, 2)
                for b, bank, free in banks("m_o"):
                    do(act.activation(MO[b], bank[:, :], ACT.Tanh, scale=0.5))
                    act.nop().then_inc(free, 1)
                level_exp(gl, 3)
                level_exp(gl, 4)
                gate(3, 1)
                level_exp(gl, 5)
                level_exp(gl, 6)
                for j in range(4):
                    act.wait_ge(ms["cv_ready"], j + 1)
                    do(act.activation(MTHG[j], MQK[j], ACT.Tanh, scale=0.5), ms["mth_ready"])
                r32 = slice(32, 36)
                act.preload_act_table_set(LOG_SET)
                do(act.activation(R(21)[r32, 0, :], LP[r32, :], ACT.Abs))
                do(act.activation(R(21)[r32, 0, :], R(21)[r32, 0, :], ACT.Exp, scale=-1.0))
                do(act.activation(R(21)[r32, 0, :], R(21)[r32, 0, :], ACT.Ln, bias=SM[r32, 62:63]), ms["a1"])
                act.wait_ge(ms["v1"], 1)
                gate(3, 2)
                decays(gl)
                kt_copy(gl)
                gate(3, 3)
                head_out(gl)
                head_rstd(1, gl.SQ)
                y_split(1)
                act.wait_ge(y_ready, 4)
                do(act.activation(R(19)[0:4, 0, :], LP[r32, :], ACT.Copy), ms["a1"])
                for b, bank, free in banks("s_u"):
                    do(act.activation(UU[:, b, :].rearrange("p (j n) -> p j n", j=S5_T), bank[:, :].rearrange("p (n j) -> p j n", j=S5_T),
                                      ACT.Copy), ss["u_ready"])
                    act.nop().then_inc(free, 1)

                act.wait_ge(ms["v1"], 2)
                do(act.activation(R(24)[0:4, 0, :], R(24)[0:4, 0, :], ACT.Exp))
                do(act.activation(R(23)[r32, 0, :], R(25)[0:4, 0, :], ACT.Exp))
                do(act.activation(R(28)[0:4, 0, :], R(21)[0:4, 0, :], ACT.Exp, scale=-1.0), ms["stack_ready"])
                gate(1, 0)
                act.wait_ge(ms["aw_done"], 1)
                do(act.activation(flat(MAW), M[0][:, 0:256], ACT.Copy), ms["aw_ready"])
                for j in range(2):
                    act.wait_ge(ms["ib_done"], 3 + j)
                    do(act.activation(MEM_E[:, j, :], M[3 if j == 0 else 0][:, :], ACT.Copy), ms["emb_ready"])
                gate(1, 1)
                act.wait_ge(ms["mex_v"], 2)
                do(act.activation(flat(MATT), flat(MATT), ACT.Exp), ms["mex_ready"])
                act.wait_ge(ms["matt_ready"], 2)
                av = MATT.rearrange("p b (j t c) -> p (b j) t c", j=2, t=TT)
                for a in range(2):
                    rows = slice(64 * a, 64 * a + 64)
                    do(act.activation(MBD[rows, :, :, 64 * a:64 * a + 64], av[rows], ACT.Copy))
                do(act.nop(), ms["mbd_ready"])
                gate(1, 2)
                gate(1, 3)
                for j in range(2):
                    act.wait_ge(ms["mo_done"], 1)
                    do(act.activation(MDA[:, j, :], M[2 + j][:, :], ACT.Abs, scale=MC), ms["mabs_ready"])
                for n in range(2):
                    do(act.activation(R(4 * n, 4), bc(reset, 1, 4), ACT.Copy, scale=0.0), ss["xp_zero"])
                for j in range(2):
                    act.wait_ge(ms["mh_ready"], j + 1)
                    do(act.activation(MSQ[:, j, :], MOO[:, j, :], ACT.Square), head_sq)
                gate(0, 0)
                head_rstd(2, MSQ)
                y_split(0)

                act.wait_ge(ss["ct_done"], 1)
                do(act.activation(flat(CT), M[0][:, :], ACT.Copy), ss["ct_ready"])
                for n in range(8):
                    r, t0 = n // 4, 2 * (n % 4)
                    act.wait_ge(ss["bt_done"], n + 1)
                    do(act.activation(BT[:, t0:t0 + 2, r, :, :].rearrange("p t q s -> p t (q s)"),
                                      M[1 + n % 3][:, :].rearrange("p (t c) -> p t c", t=2), ACT.Copy), ss["bt_ready"])
                gate(0, 1)
                gate(0, 2)
                act.wait_ge(ss["w_done"], 1)
                act.wait_ge(ss["cl_ready"], 1)
                for i4 in range(4):
                    for r in range(2):
                        src = M[i4][:, 0:256].rearrange("p (f r n) -> p f r n", f=2, r=2)[:, :, r, :]
                        do(act.activation(SW[r][:, i4::4, :], src, ACT.Copy), ss["ct_ready"] if (i4, r) == (3, 1) else None)
                gate(0, 3)
                for f in range(2):
                    act.wait_ge(ss["ys_ready"], f + 1)
                    do(act.activation(GE[:, f, :], YS[:, f, :], ACT.Square), ss["sq"])
                for f in range(2):
                    act.wait_ge(ss["poly"], f + 1)
                    do(act.activation(GE[:, f, :], GE[:, f, :], ACT.Tanh, scale=float(np.sqrt(2.0 / np.pi))), ss["tanh"])
                gate(2, 0)
                for j in range(2):
                    act.wait_ge(ss["glu_done"], 3 + j)
                    do(act.activation(R(24 + j)[:, 0, :], M[2 + j][:, :], ACT.Tanh, scale=0.25, bias=SM[:, 48 + j:49 + j]))
                    do(act.activation(R(28 + j)[:, 0, :], M[j][:, :], ACT.Identity, scale=0.5, bias=col("s5_b_glu", j)), ss["val_ready"])
                y_split(2)
                gate(2, 1)
                for c in range(4):
                    if c > 1:
                        gate(2, c)
                    for b in range(2):
                        k = 2 * c + b
                        act.wait_ge(mg_ready, k + 1)
                        do(act.activation(MHhi[:, k, :], MG[:, k, :], ACT.Copy, scale=0.5), mghi_ready)
                for k in range(KC):
                    act.wait_ge(at["mmx"], k + 1)
                    do(act.activation(MMhi[:, k, :], MMX[:, k, :], ACT.Copy), at["mm_hi"])

                def kv_copy(c):
                    for b, bank, free in banks(f"kv{c}"):
                        if c < 4:
                            do(act.activation(KTt[:, 2 * c + b, :], bank[:, 0:MEM], ACT.Copy), at["kt_ready"])
                        else:
                            do(act.activation(VM[:, b, (c - 4) * BW:(c - 3) * BW], bank[:, 0:BW], ACT.Copy), at["vm_ready"])
                        act.nop().then_inc(free, 1)

                squares(1)
                act.wait_ge(at["mm_ready"], 8)
                kv_copy(0)
                factors(1)
                for c in range(1, 4):
                    if c < 3:
                        round_up(BY_SCALAR[2 * c - 2])
                    kv_copy(c)
                    if c < 3:
                        round_up(BY_SCALAR[2 * c - 1])
                norm_hi(1)
                def exponentials(h):
                    if h >= 2:
                        act.wait_ge(at["pt_done"], 2 * (h - 1))
                    act.wait_ge(at["mx_ready"], h + 1)
                    for t in range(TT):
                        do(act.activation(PB[h % 2][:, t, :], ASB[h % 2][t // 2][:, (t % 2) * 256:(t % 2) * 256 + 256], ACT.Exp,
                                          scale=1.0 / 16.0, bias=AST[:, 1, h * 4 + t:h * 4 + t + 1],
                                          accum_out=AST[:, 2, h * 4 + t:h * 4 + t + 1]), at["p_exp"])

                for c in range(4):
                    for b, bank, free in banks(f"q{c}"):
                        do(act.activation(MG[:, 2 * c + b, :], bank[:, :], ACT.Copy), at["q_ready"])
                        act.nop().then_inc(free, 1)
                    if c == 3:
                        exponentials(0)
                    kv_copy(4 + c)
                def transposed(h):
                    for m in range(2):
                        act.wait_ge(at["pt_done"], 2 * h + m + 1)
                        do(act.activation(PTB[h % 2][:, m, :], APT[m][:, :], ACT.Copy), at["pt_ready"])

                def out_hi(h):
                    for k in range(2):
                        act.wait_ge(at["oc_ready"], 2 * h + k + 1)
                        do(act.activation(Hhi[:, 2 * h + k, :], MG[:, 2 * h + k, :], ACT.Copy), at["ohi_ready"])

                exponentials(1)
                transposed(0)
                exponentials(2)
                transposed(1)
                out_hi(0)
                exponentials(3)
                transposed(2)
                out_hi(1)
                transposed(3)
                out_hi(2)
                out_hi(3)
                squares(2)
                factors(2)
                norm_hi(2)
                n = 0
                for q in range(4):
                    for c in range(4):
                        for b, bank, free in banks(f"up{q}_{c}"):
                            if n:
                                act.wait_ge(uplo, n)
                            else:
                                act.wait_ge(h_ready, 24)
                            if q >= 2 and (c, b) == (0, 0):
                                last = f"down{q - 2}_3"
                                s, used = psum_set(last)
                                act.wait_ge(gemm_done[s], 2 * used + 2)
                            do(act.activation(UPX[:, 0, :], bank[:, :], ACT.Relu), up_a)
                            act.nop().then_inc(free, 1)
                            act.wait_ge(up_v, n + 1)
                            do(act.activation(MHID[q % 2][0][:, 2 * c + b, :], UPX[:, 0, :], ACT.Copy), uphi)
                            n += 1
                squares(3)
                act.nop().then_inc(layer_end, 1)
                act.wait_ge(layer_go, L + 2)
            n = [0]

            def fdo(ins):
                n[0] += 1
                ins.then_inc(f_act, 1)
                act.wait_ge(f_act, n[0])
            act.preload_act_table_set(LOG_SET)
            act.wait_ge(f_pe, 1)
            fdo(act.activation(R(32)[:, 0, :], M[3][:, :], ACT.Ln, bias=eps))
            fdo(act.activation(R(32)[:, 0, :], R(32)[:, 0, :], ACT.Exp, scale=-0.5))
            act.wait_ge(f_pe, 2)
            for t in range(TT):
                fdo(act.activation(R(2 * t)[:, 0, :], FB[t][0][:, :], ACT.Copy))

        @block.vector
        def _(dve):
            do = chained(dve, v_chain)
            p_own = whole("pro_vector_steps")
            po = [0]

            def own(ins):
                po[0] += 1
                ins.then_inc(p_own, 1)
                dve.wait_ge(p_own, po[0])

            own(dve.memset(SM[:, 61:62], PI / 2))
            own(dve.memset(SM[:, 62:63], 1.0))
            own(dve.memset(SM[:, 63:64], EPS))
            own(dve.memset(PS[:, :, :], 0.0))
            dve.memset(R(20, 2)[:, :, 0:P], 0.0).then_inc(p_vec, 1)
            dve.wait_ge(p_act, 12)
            for t in range(2):
                i = dve.tensor_scalar(flat(R(8 + 2 * t, 2)), flat(R(8 + 2 * t, 2)), SM[:, 44 + t:45 + t], None, ALU.mult)
                if t == 0:
                    own(i)
            i.then_inc(p_vec, 1)
            dve.wait_ge(p_vec, 2)
            for k in range(1, KC):
                dve.wait_ge(p_sq, k + 1)
                own(dve.tensor_tensor(NS, MG[:, 0, :] if k == 1 else NS, MG[:, k, :], ALU.add))
            dve.wait_ge(p_pe, 13)
            for l in range(DEPTH):
                own(dve.tensor_copy(PTA[:, l, :], G[0][l][:, 0:NROW]))
                own(dve.tensor_copy(PTA[:, l, PROW["step"]:PROW["step"] + 8], SM[:, 16 + 8 * l:24 + 8 * l]))
            l0, l1 = PTA[:, 0, PROW["lb0"]:PROW["lb0"] + 2], PTA[:, 0, PROW["lb1"]:PROW["lb1"] + 2]
            own(dve.tensor_tensor(PS[:, 0, 0:2], l1, l0, ALU.subtract))
            own(dve.tensor_tensor(PS[:, 1, 0:2], l0, l1, ALU.subtract))
            own(dve.tensor_copy(PS[:, 2:4, 0:2], PS[:, 0:2, 0:2]))
            dve.nop().then_inc(p_vec, 1)
            dve.wait_ge(p_act, 19)
            dve.nop().then_inc(p_vec, 1)
            for n, name in enumerate(("hg_c0", "hg_c1")):
                own(dve.scalar_tensor_tensor(PTA[:, 1, PROW[name]:PROW[name] + 2], PS[:, 2 + n, 0:2], 0.0, PS[:, n, 0:2], ALU.min, ALU.subtract))
            own(dve.memset(PTA[:, 0, PROW["hg_c0"]:PROW["hg_c0"] + 2], NEG))
            own(dve.memset(PTA[:, 0, PROW["hg_c1"]:PROW["hg_c1"] + 2], 0.0))
            dve.nop().then_inc(layer_go, 1)

            def tt(o, a, b, op, s=None):
                do(dve.tensor_tensor(o, a, b, op), s)

            def ts(o, a, s1, s2, op0, op1=None, s=None):
                if op1 is None:
                    do(dve.tensor_scalar(o, a, s1, None, op0), s)
                else:
                    do(dve.tensor_scalar(o, a, s1, s2, op0, op1), s)

            def stt(o, a, sc, b, op0, op1, s=None):
                do(dve.scalar_tensor_tensor(out=o, in0=a, scalar=sc, in1=b, op0=op0, op1=op1), s)

            def round_up(u):
                raw, hi, _ = wait_for_half_block(dve, u)
                do(dve.tensor_copy(hi, raw), split_hi_vector)

            def add_squares(n, k0, k1):
                for k in range(max(k0, 1), k1):
                    dve.wait_ge(sq_ready, 8 * (n - 1) + k + 1)
                    tt(NS, NS, TH[:, k % 2, :], ALU.add, sq_used)

            def norm_out(base, gain):
                dve.wait_ge(rstd_ready, base // 4 + 2)
                for k in range(KC + 1):
                    if k < KC:
                        stt(TH[:, k % 2, :], X[:, k, :], col(gain, k), R(32)[:, 0, :], ALU.mult, ALU.mult, hx_ready)
                    if k:
                        dve.wait_ge(hi_ready, base + k)
                        stt(Hlo[:, k - 1, :], TH[:, (k - 1) % 2, :], 1.0, Hhi[:, k - 1, :].bitcast(F32), ALU.mult, ALU.subtract, h_ready)

            th_n = [0]

            def gate_out(name, dst, s=None):
                st, used = psum_set(name)
                for b in range(2):
                    th_n[0] += 1
                    dve.wait_ge(th_ready, th_n[0])
                    stt(dst[:, b, :], TH[:, b, :], 1.0, G[st][b][:, :], ALU.add, ALU.mult, th_used)
                    dve.nop().then_inc(gemm_free[st], 1)

            def merge(n, c):
                s, used = psum_set(f"branch{n}_{c}")
                for b in range(2):
                    th_n[0] += 1
                    dve.wait_ge(th_ready, th_n[0])
                    dve.wait_ge(gemm_done[s], 2 * used + b + 1)
                    k = 2 * c + b
                    if n == 3:
                        stt(MG[:, k, :], TH[:, b, :], 1.0, G[s][b][:, :], ALU.add, ALU.mult, th_used)
                        dve.nop().then_inc(gemm_free[s], 1)
                    else:
                        stt(TH[:, b, :], TH[:, b, :], 1.0, G[s][b][:, :], ALU.add, ALU.mult)
                        dve.nop().then_inc(gemm_free[s], 1)
                        tt(MG[:, k, :], MG[:, k, :], TH[:, b, :], ALU.add, th_used)

            def ends(m):
                return m.Gc.rearrange("p (c t) -> p c t", t=CH)[:, :, CH - 1:CH]

            def level_diff(m, l):
                w = LEVELS[l]
                if l >= 3:
                    dve.wait_ge(m.x_ready, l - 2)
                g = m.Gc.rearrange("p (n a c) -> p n a c", a=2, c=w)
                e = m.E[l % 2].rearrange("p (n a c) -> p n a c", a=2, c=w)
                n = m.W // (2 * w)
                mid = g[:, :, 0, w - 1:w].to_broadcast([P, n, w])
                tt(e[:, :, 0, :], mid, g[:, :, 0, :], ALU.subtract, m.d_ready)
                tt(e[:, :, 1, :], g[:, :, 1, :], mid, ALU.subtract, m.d_ready)

            def level_mul(m, l):
                w = LEVELS[l]
                dve.wait_ge(m.e_ready, l)
                if l >= 3:
                    dve.wait_ge(m.lev_done, l - 1)
                v = lambda ap: ap.rearrange("p (n a c) -> p n a c", a=2, c=w)
                e, xx, k, q = v(m.E[l % 2]), v(m.X[l % 2]), v(m.K), v(m.Q)
                tt(xx[:, :, 0, :], e[:, :, 0, :], k[:, :, 0, :], ALU.mult)
                tt(xx[:, :, 1, :], e[:, :, 1, :], q[:, :, 1, :], ALU.mult, m.x_ready)

            def pick(m, l):
                dve.wait_ge(m.lev_done, l + 1)
                nb = 2 if m.J == 2 else 4
                w = 1024 // nb
                for b in range(nb):
                    bank = m.score_bank(l, b)
                    r = lambda ap: ap.rearrange("p (n c) -> p n c", c=CH)
                    do(dve.copy_predicated(r(m.att[:, b * w:(b + 1) * w]), bc(LM[:, l, :], 1, w // CH), r(bank[:, 0:w])), m.picked)

            def tail(m):
                g = m.Gc.rearrange("p (c t) -> p c t", t=CH)
                e0 = m.E[0].rearrange("p (c t) -> p c t", t=CH)
                tt(e0, ends(m).to_broadcast([P, m.W // CH, CH]), g, ALU.subtract, m.d_ready)
                pick(m, 5)
                dve.wait_ge(m.e_ready, 7)
                tt(m.E[0], m.E[0], m.K, ALU.mult, m.kd_ready)
                pick(m, 6)
                dve.wait_ge(m.e_ready, 8)
                if m.J == 1:
                    merge(3, 2)
                do(dve.memset(m.attbd[0:64, :, :, 64:128], 0.0))
                do(dve.memset(m.attbd[64:128, :, :, 0:64], 0.0))
                av = m.att.rearrange("p (h t c) -> p h t c", h=4, t=TT)
                for a in range(2):
                    rows = slice(64 * a, 64 * a + 64)
                    do(dve.tensor_copy(m.attbd[rows, :, :, 64 * a:64 * a + 64], av[rows]), m.bd_ready if a else None)
                do(dve.memset(m.S.rearrange("p j c v -> p (j c v)"), 0.0))
                do(dve.tensor_tensor(m.Q, m.Q, m.E[1], ALU.mult), m.s_ready)
                dve.wait_ge(m.kv_done, 1)
                eg = m.E[1].rearrange("p (c t) -> p c t", t=CH)
                for c in range(7):
                    for h in range(4):
                        jt, r0 = h // m.per, m.dk * (h % m.per)
                        rows, vs = slice(r0, r0 + m.dk), slice(HD * (h % m.per), HD * (h % m.per) + HD)
                        kv = M[2 + c % 2][rows, (h // m.per) * 256 + (c // 2) * HD:(h // m.per) * 256 + (c // 2) * HD + HD]
                        last = m.s_ready if (c, h) == (6, 3) else None
                        if c == 0:
                            do(dve.tensor_copy(m.S[rows, jt, 0, vs], kv), last)
                        else:
                            stt(m.S[rows, jt, c, vs], m.S[rows, jt, c - 1, vs], eg[rows, jt * NCH + c, CH - 1:CH], kv, ALU.mult, ALU.add, last)

            def branch_out(n, o, rs, order, gain, gate):
                for j in range(2):
                    dve.wait_ge(head_rs, 4 * order + 2 * j + 2)
                    stt(o[:, j, :], o[:, j, :], col(gain, j), rs[:, j, :], ALU.mult, ALU.mult)
                    gate(j)
                y_low(n, o)

            def y_low(n, o):
                for j in range(2):
                    dve.wait_ge(y_hi, 2 * BRANCH_NO[n] + j + 1)
                    b = YB[BRANCH_AT[n]]
                    stt(b[1][:, j, :], o[:, j, :], 0.5, b[0][:, j, :].bitcast(F32), ALU.mult, ALU.subtract, y_ready)

            def conv(j):
                dve.wait_ge(ms["cin_ready"], j + 1)
                ts(MQK[j], CIN[:, j, 3:515], col("mlstm_conv_w", 12 + j), col("mlstm_conv_b", j), ALU.mult, ALU.add)
                for k in range(3):
                    stt(MQK[j], CIN[:, j, k:k + SEQ], col("mlstm_conv_w", 4 * k + j), MQK[j], ALU.mult, ALU.add,
                        ms["cv_ready"] if k == 2 else None)

            with dve.Fori(0, DEPTH) as L:
                do(dve.tensor_copy(PT[:, :], PTA[:, bass.ds(L, 1), :].rearrange("p a c -> p (a c)")))
                round_up(BY_VECTOR[0])
                norm_out(0, "norm_mix")
                E0, E1, X0, X1 = hg.E[0], hg.E[1], hg.X[0], hg.X[1]
                dve.wait_ge(hg.gate_in, 3)
                stt(X0, E0, 0.0, E1, ALU.min, ALU.subtract, hg.g_ready)
                tt(hg.K, X0, E0, ALU.subtract, hg.g_ready)
                for j in range(2):
                    js = slice(j * SEQ, (j + 1) * SEQ)
                    do(dve.tensor_tensor(SM[:, 50 + j:51 + j], col("hg_c1", j), col("hg_c0", j), ALU.subtract))
                    ts(X1[:, js], X0[:, js], SM[:, 50 + j:51 + j], None, ALU.add, s=hg.g_ready)
                for j in range(2):
                    js = slice(j * SEQ, (j + 1) * SEQ)
                    ts(X0[:, js], X0[:, js], col("hg_c1", j), col("hg_c0", j), ALU.add, ALU.max)
                dve.wait_ge(hg.gate_in, 4)
                tt(X0, X0, X1, ALU.add)
                for j in range(2):
                    js = slice(j * SEQ, (j + 1) * SEQ)
                    do(dve.tensor_tensor_scan(hg.Gc[:, js], reset, X0[:, js], 0.0, ALU.mult, ALU.add))
                gate_out("r_q", hg.Q.rearrange("p (j t) -> p j t", j=2))
                do(dve.nop(), hg.g_ready)
                level_diff(hg, 1)
                level_diff(hg, 2)
                do(dve.memset(hg.att, 0.0))
                pick(hg, 0)
                pr = lambda n: PS[:, n, :]
                re_, im_ = PT[:, PROW["s5_lam_re"]:PROW["s5_lam_re"] + 8], PT[:, PROW["s5_lam_im"]:PROW["s5_lam_im"] + 8]
                dve.wait_ge(params_in, 16 * 5)
                dve.wait_ge(ss["sin_in"], 1)
                tt(pr(1), re_, pr(0), ALU.mult)
                tt(pr(2), im_, pr(0), ALU.mult)
                ts(pr(5), pr(2), 1.0 / (2 * PI), None, ALU.mult)
                ts(pr(5), pr(5), 12582912.0, None, ALU.add)
                ts(pr(5), pr(5), 12582912.0, None, ALU.subtract)
                stt(pr(2), pr(5), -6.28125, pr(2), ALU.mult, ALU.add)
                stt(pr(2), pr(5), -(2 * PI - 6.28125), pr(2), ALU.mult, ALU.add)
                ts(pr(2), pr(2), PI, -PI, ALU.min, ALU.max, s=ss["prm"])
                dve.wait_ge(ss["sin_ready"], 1)
                Ur, Ui = PW[:, 0], PW[:, 1]
                do(dve.memset(Ur[:, 0, :], 1.0))
                do(dve.memset(Ui[:, 0, :], 0.0))
                do(dve.tensor_copy(Ur[:, 1, :], pr(3)))
                do(dve.tensor_copy(Ui[:, 1, :], pr(4)))

                def cmul(orr, oi, ar, ai, br, bi, t1, t2, s=None):
                    tt(t1, ar, br, ALU.mult)
                    tt(t2, ai, bi, ALU.mult)
                    tt(orr, t1, t2, ALU.subtract)
                    tt(t1, ar, bi, ALU.mult)
                    tt(t2, ai, br, ALU.mult)
                    tt(oi, t1, t2, ALU.add, s)

                for w in (1, 2, 4):
                    t1, t2 = S5T[0][:, 0:8 * w].rearrange("p (a b) -> p a b", b=8), S5T[1][:, 0:8 * w].rearrange("p (a b) -> p a b", b=8)
                    cmul(Ur[:, w + 1:2 * w + 1, :], Ui[:, w + 1:2 * w + 1, :], Ur[:, 1:w + 1, :], Ui[:, 1:w + 1, :],
                         Ur[:, w:w + 1, :].to_broadcast([P, w, 8]), Ui[:, w:w + 1, :].to_broadcast([P, w, 8]), t1, t2)
                do(dve.tensor_copy(pr(17), Ur[:, 8, :]))
                do(dve.tensor_copy(pr(18), Ui[:, 8, :]))
                tt(Ur[:, :, :], Ur[:, :, :], PS[:, 8:17, :], ALU.mult)
                tt(Ui[:, :, :], Ui[:, :, :], PS[:, 8:17, :], ALU.mult)
                tt(pr(5), re_, re_, ALU.mult)
                tt(pr(6), im_, im_, ALU.mult)
                tt(pr(5), pr(5), pr(6), ALU.add)
                do(dve.reciprocal(pr(5), pr(5)))
                ts(pr(6), Ur[:, 1, :], -1.0, None, ALU.add)
                tt(pr(7), pr(6), re_, ALU.mult)
                tt(pr(19), Ui[:, 1, :], im_, ALU.mult)
                tt(pr(7), pr(7), pr(19), ALU.add)
                tt(pr(7), pr(7), pr(5), ALU.mult)
                tt(pr(19), Ui[:, 1, :], re_, ALU.mult)
                tt(pr(20), pr(6), im_, ALU.mult)
                tt(pr(19), pr(19), pr(20), ALU.subtract)
                tt(pr(19), pr(19), pr(5), ALU.mult)
                c8 = lambda ap: ap.unsqueeze(2).to_broadcast([P, 8, 16])
                bb_r, bb_i, t1, t2 = (Rf(21, 1)[:, n * 128:(n + 1) * 128].rearrange("p (t h) -> p t h", t=8) for n in range(4))
                cmul(bb_r, bb_i, BRI[:, 0], BRI[:, 1], c8(pr(7)), c8(pr(19)), t1, t2)
                do(dve.tensor_copy(BRI[:, 0], bb_r))
                do(dve.tensor_copy(BRI[:, 1], bb_i))
                level_mul(hg, 1)
                level_mul(hg, 2)
                level_diff(hg, 3)
                dve.wait_ge(gl.gate_in, 3)
                stt(R(30)[:, 0, :], R(30)[:, 0, :], 0.0, R(31)[:, 0, :], ALU.min, ALU.subtract)
                do(dve.tensor_tensor_scan(gl.Gc, reset, R(30)[:, 0, :], 0.0, ALU.mult, ALU.add))
                pick(hg, 1)
                level_diff(hg, 4)
                gate_out("g_r", gl.GR)
                level_mul(hg, 3)
                pick(hg, 2)
                level_diff(hg, 5)
                level_mul(hg, 4)
                pick(hg, 3)
                level_diff(hg, 6)
                gate_out("r_g", hg.GR)
                level_mul(hg, 5)
                pick(hg, 4)
                level_mul(hg, 6)
                tail(hg)

                def silu_gate(m):
                    return lambda j: tt(m.O[:, j, :], m.O[:, j, :], m.GR[:, j, :], ALU.mult, y_act)
                do(dve.tensor_copy(TB[0][:, :, 0], pr(17)))
                do(dve.tensor_copy(TB[1][:, :, 0], pr(18)))
                w = 1
                while w < S5_N:
                    t1, t2 = (Rf(20 + n, 1)[:, 0:8 * w].rearrange("p (t n) -> p t n", t=8) for n in range(2))
                    cmul(TB[0][:, :, w:2 * w], TB[1][:, :, w:2 * w], TB[0][:, :, 0:w], TB[1][:, :, 0:w],
                         TB[0][:, :, w - 1:w].to_broadcast([P, 8, w]), TB[1][:, :, w - 1:w].to_broadcast([P, 8, w]), t1, t2)
                    w *= 2
                branch_out(3, hg.O, hg.SQ, 0, "hgrn_norm", silu_gate(hg))
                level_diff(gl, 1)
                level_diff(gl, 2)
                do(dve.memset(CIN[:, :, 0:3], 0.0))
                do(dve.memset(gl.att, 0.0))
                pick(gl, 0)
                level_mul(gl, 1)
                level_diff(gl, 3)
                pick(gl, 1)
                level_mul(gl, 2)
                level_diff(gl, 4)
                pick(gl, 2)
                level_mul(gl, 3)
                level_mul(gl, 4)
                level_diff(gl, 5)
                level_diff(gl, 6)
                pick(gl, 3)
                merge(3, 0)
                conv(0)
                conv(1)
                pick(gl, 4)
                level_mul(gl, 5)
                level_mul(gl, 6)
                conv(2)
                conv(3)
                merge(3, 1)
                for j in range(4):
                    dve.wait_ge(ms["mth_ready"], j + 1)
                    stt(MQK[j], MTHG[j], 1.0, MQK[j], ALU.add, ALU.mult)
                dve.wait_ge(ms["a1"], 1)
                stt(LP[32:36, :], LP[32:36, :], 0.0, R(21)[32:36, 0, :], ALU.min, ALU.subtract, ms["v1"])
                tail(gl)
                merge(3, 3)
                branch_out(1, gl.O, gl.SQ, 1, "gla_norm", silu_gate(gl))

                dve.wait_ge(ms["a1"], 2)
                lf, bb, mt, bmr, st, it, wx = (R(n)[0:4, 0, :] for n in (19, 20, 21, 22, 23, 24, 25))
                do(dve.memset(R(23)[0:64, 0, :], 0.0))
                do(dve.tensor_tensor_scan(bb, reset[0:4, :], lf, 0.0, ALU.mult, ALU.add))
                do(dve.tensor_tensor_scan(mt, lf, LP[0:4, :], 0.0, ALU.add, ALU.max))
                tt(bmr, bb, mt, ALU.subtract)
                tt(st, LP[0:4, :], bb, ALU.subtract)
                ck = lambda ap: ap.rearrange("p (c t) -> p c t", t=CH)
                do(dve.memset(SM[0:4, 52:53], 0.0))
                do(dve.tensor_copy(SM[0:4, 53:60], ck(mt)[:, 0:7, CH - 1]))
                tt(ck(it), ck(bmr), SM[0:4, 52:60].unsqueeze(2).to_broadcast([4, NCH, CH]), ALU.add)
                tt(ck(wx), ck(st), ck(bmr)[:, :, CH - 1:CH].to_broadcast([4, NCH, CH]), ALU.add, ms["v1"])
                for j in range(2):
                    dve.wait_ge(ms["ib_done"], j + 1)
                    tt(MQT[:, j, :], MQK[j], M[1 + j][:, :], ALU.mult)
                    do(dve.tensor_copy(MDEC[:, j, :], ck(M[1 + j][:, :])[:, :, CH - 1]), ms["ib_ready"])
                do(dve.nop(), ms["ib_ready"])
                do(dve.nop(), ms["ib_ready"])
                merge(1, 0)
                for hp in range(2):
                    dve.wait_ge(ms["mex_done"], hp + 1)
                    for j in range(2):
                        o = MATT[:, hp, j * 256:(j + 1) * 256].rearrange("p (t c) -> p t c", t=TT)
                        a = MAW[:, :, 2 * j + hp:2 * j + hp + 1].to_broadcast([P, TT, CH])
                        tt(o, M[hp][:, j * 256:(j + 1) * 256].rearrange("p (t c) -> p t c", t=TT), a, ALU.add, ms["mex_v"] if j else None)
                do(dve.memset(MBD[0:64, :, :, 64:128], 0.0))
                do(dve.memset(MBD[64:128, :, :, 0:64], 0.0))
                dve.wait_ge(ms["mex_ready"], 1)
                dve.wait_ge(ms["mqk_done"], 1)
                for hp in range(2):
                    tt(MATT[:, hp, :], MATT[:, hp, :], M[2 + hp][:, :], ALU.mult, ms["matt_ready"])
                merge(1, 1)
                for j in range(2):
                    dve.wait_ge(ms["mkt_done"], j + 1)
                    w = MAW[:, :, 32 + 2 * j:34 + 2 * j].unsqueeze(3).to_broadcast([P, TT, 2, HD])
                    tt(MKT[:, :, j, :, :], M[j][:, :].rearrange("p (t b v) -> p t b v", t=TT, b=2), w, ALU.mult, ms["mkt_ready"])
                for j in range(2):
                    do(dve.memset(MS[j].rearrange("p c b v -> p (c b v)"), 0.0))
                dve.wait_ge(ms["mkv_done"], 1)
                for c in range(7):
                    for h in range(4):
                        j, hp = h // 2, h % 2
                        rows = slice(64 * hp, 64 * hp + 64)
                        kv = M[2 * (c % 2) + j][rows, (c // 2) * 128:(c // 2) * 128 + 128]
                        last = ms["ms_ready"] if c == 6 and h >= 2 else None
                        if c == 0:
                            do(dve.tensor_copy(MS[j][rows, 0, hp, :], kv))
                        else:
                            stt(MS[j][rows, c, hp, :], MS[j][rows, c - 1, hp, :], MDEC[rows, j, c:c + 1], kv, ALU.mult, ALU.add, last)
                merge(1, 2)
                for j in range(2):
                    dve.wait_ge(ms["mabs_ready"], j + 1)
                    tt(MDA[:, j, :], MDA[:, j, :], MEM_E[:, j, :], ALU.max)
                    do(dve.reciprocal(MDA[:, j, :], MDA[:, j, :]))
                    stt(MOO[:, j, :], M[j][:, :], MC, MDA[:, j, :], ALU.mult, ALU.mult, ms["mh_ready"])
                merge(1, 3)
                for r in range(2):
                    for f in range(2):
                        for a in range(2):
                            ts(R(24 + r)[:, 0, f * P + 64 * a:f * P + 64 * a + 64], CRI[:, r, f, :], parity[:, a:a + 1], None, ALU.mult,
                               s=ss["cp_ready"] if (f, a) == (1, 1) else None)
                branch_out(0, MOO, MSQ, 2, "mlstm_norm",
                           lambda j: stt(MOO[:, j, :], MO[j], 1.0, MOO[:, j, :], ALU.add, ALU.mult, y_act))

                dve.wait_ge(ss["xp_zero"], 2)
                four = [Rf(20 + 2 * n, 2).rearrange("p (u t h) -> p u t h", u=8, t=8) for n in range(2)]
                pw = lambda n: PW[:, n, 0:8, :].unsqueeze(3).to_broadcast([P, 8, 8, 16])
                bx = lambda ap: ap.unsqueeze(1).to_broadcast([P, 8, 8, 16])
                for r, (b1, b2, op) in enumerate(((BRI[:, 0], BRI[:, 1], ALU.subtract), (BRI[:, 1], BRI[:, 0], ALU.add))):
                    tt(four[0], pw(0), bx(b1), ALU.mult)
                    tt(four[1], pw(1), bx(b2), ALU.mult)
                    for a in range(2):
                        rows = slice(64 * a, 64 * a + 64)
                        tt(XP[rows, r, :, :, 16 * a:16 * a + 16], four[0][rows], four[1][rows], op, ss["xp_ready"] if a else None)
                merge(0, 0)
                dve.wait_ge(ss["ct_ready"], 1)
                ts(CT[:, 1, :], CT[:, 1, :], -1.0, None, ALU.mult, s=ss["cp_ready"])
                do(dve.memset(KTm.rearrange("p a u c -> p (a u c)"), 0.0))
                dve.wait_ge(ss["kk_done"], 1)
                kk = M[0][:, :].rearrange("p (f u c) -> p f u c", f=2, u=8)
                for i4 in range(4):
                    rows = slice(32 * i4, 32 * i4 + 32)
                    do(dve.tensor_copy(KTm[rows, :, :, 32 * i4:32 * i4 + 32], kk[rows]), ss["kk_ready"])
                merge(0, 1)
                t1, t2 = (a.rearrange("p (j t c) -> p j t c", j=8, t=8) for a in T4)
                pj = lambda n: PW[:, n, 1:9, :].unsqueeze(3).to_broadcast([P, 8, 8, 32])
                cx = lambda n: CT[:, n, :].rearrange("p (t c) -> p t c", t=8).unsqueeze(1).to_broadcast([P, 8, 8, 32])
                tt(t1, pj(0), cx(0), ALU.mult)
                tt(t2, pj(1), cx(1), ALU.mult)
                tt(CL[:, 0], t1, t2, ALU.add)
                tt(t1, pj(0), cx(1), ALU.mult)
                tt(t2, pj(1), cx(0), ALU.mult)
                tt(CL[:, 1], t1, t2, ALU.subtract, ss["cl_ready"])
                rr = ST[2].rearrange("p (t n) -> p t n", t=8)
                do(dve.tensor_copy(rr, PS[:, 16, :].unsqueeze(2).to_broadcast([P, 8, S5_N])))
                do(dve.memset(rr[:, :, 0:1], 0.0))
                merge(0, 2)
                dve.wait_ge(ss["ct_ready"], 2)
                w3 = lambda ap: ap.rearrange("p (t n) -> p t n", t=8)
                a0, a1 = w3(ST[0]), w3(ST[1])
                tt(a0, TB[0], SW[0], ALU.mult)
                tt(a1, TB[1], SW[1], ALU.mult)
                tt(w3(SZ[0]), a0, a1, ALU.add)
                tt(a0, TB[0], SW[1], ALU.mult)
                tt(a1, TB[1], SW[0], ALU.mult)
                tt(w3(SZ[1]), a0, a1, ALU.subtract)
                for r in range(2):
                    do(dve.tensor_tensor_scan(SZ[r], ST[2], SZ[r], 0.0, ALU.mult, ALU.add))
                cmul(SX[0], SX[1], w3(SZ[0]), w3(SZ[1]), TB[0], TB[1], a0, a1, ss["x_ready"])
                merge(0, 3)
                for f in range(2):
                    dve.wait_ge(ss["y_done"], f + 1)
                    ys = YS[:, f, :].rearrange("p (n j) -> p j n", j=S5_T)
                    uf = UU[:, f, :].rearrange("p (j n) -> p j n", j=S5_T)
                    stt(ys, uf, col("s5_d", f), M[f][:, :].rearrange("p (j n) -> p j n", j=S5_T), ALU.mult, ALU.add, ss["ys_ready"])
                for f in range(2):
                    dve.wait_ge(ss["sq"], f + 1)
                    ts(GE[:, f, :], GE[:, f, :], 0.044715, 1.0, ALU.mult, ALU.add)
                    tt(GE[:, f, :], GE[:, f, :], YS[:, f, :], ALU.mult, ss["poly"])
                do(dve.tensor_scalar(SM[:, 48:50], PT[:, PROW["s5_b_glu"] + 2:PROW["s5_b_glu"] + 4], 0.5, None, ALU.mult))
                for f in range(2):
                    dve.wait_ge(ss["tanh"], f + 1)
                    stt(GE[:, f, :], GE[:, f, :], 1.0, YS[:, f, :], ALU.add, ALU.mult, ss["ge_ready"])
                for j in range(2):
                    dve.wait_ge(ss["val_ready"], j + 1)
                    stt(YS[:, j, :], R(24 + j)[:, 0, :], 1.0, R(28 + j)[:, 0, :], ALU.add, ALU.mult, y_act)
                do(dve.nop(), at["base_free"])
                y_low(2, YS)
                for c in range(4):
                    s, used = psum_set(f"branch2_{c}")
                    for b in range(2):
                        th_n[0] += 1
                        dve.wait_ge(th_ready, th_n[0])
                        dve.wait_ge(gemm_done[s], 2 * used + b + 1)
                        k = 2 * c + b
                        t = GATE_AHEAD if c == 1 else TH
                        stt(t[:, b, :], t[:, b, :], 1.0, G[s][b][:, :], ALU.add, ALU.mult)
                        dve.nop().then_inc(gemm_free[s], 1)
                        tt(MG[:, k, :], MG[:, k, :], t[:, b, :], ALU.add, mg_ready)
                        do(dve.nop(), th_used)
                    for b in range(2):
                        k = 2 * c + b
                        dve.wait_ge(mghi_ready, k + 1)
                        stt(MHlo[:, k, :], MG[:, k, :], 0.5, MHhi[:, k, :].bitcast(F32), ALU.mult, ALU.subtract, mgs_ready)
                dve.wait_ge(at["mem_base_in"], 16)
                for k in range(KC):
                    ts(MMX[:, k, :], MBASE[:, k, :], col("norm_mem", k), None, ALU.mult, s=at["mmx"])
                for k in range(KC):
                    dve.wait_ge(at["mm_hi"], k + 1)
                    stt(MMlo[:, k, :], MMX[:, k, :], 1.0, MMhi[:, k, :].bitcast(F32), ALU.mult, ALU.subtract, at["mm_ready"])

                def residual(name, norm=None):
                    s, used = psum_set(name)
                    c = int(name[-1])
                    for b in range(2):
                        dve.wait_ge(gemm_done[s], 2 * used + b + 1)
                        tt(X[:, 2 * c + b, :], X[:, 2 * c + b, :], G[s][b][:, :], ALU.add, x_ready)
                        dve.nop().then_inc(gemm_free[s], 1)
                        if norm:
                            add_squares(norm, 2 * c + b - 1, 2 * c + b)

                for c in range(4):
                    if c == 3:
                        round_up(BY_VECTOR[1])
                        round_up(BY_VECTOR[2])
                    residual(f"out{c}", norm=1)
                add_squares(1, 7, 8)
                for u in BY_VECTOR[3:5]:
                    round_up(u)
                norm_out(8, "norm_xattn")
                for u in BY_VECTOR[5:-1]:
                    round_up(u)
                def maxima(h):
                    dve.wait_ge(at["sc_done"], h + 1)
                    for b in range(2):
                        do(dve.tensor_reduce(AST[:, 0, h * 4 + 2 * b:h * 4 + 2 * b + 2],
                                             ASB[h % 2][b][:, :].rearrange("p (t m) -> p t m", t=2), mybir.AxisListType.X, ALU.max))
                    ts(AST[:, 1, h * 4:h * 4 + 4], AST[:, 0, h * 4:h * 4 + 4], -1.0 / 16.0, None, ALU.mult, s=at["mx_ready"])

                def normalise(h):
                    dve.wait_ge(at["p_exp"], 4 * h + 4)
                    do(dve.reciprocal(AST[:, 3, h * 4:h * 4 + 4], AST[:, 2, h * 4:h * 4 + 4]))
                    for t in range(TT):
                        ts(PB[h % 2][:, t, :], PB[h % 2][:, t, :], AST[:, 3, h * 4 + t:h * 4 + t + 1], None, ALU.mult, s=at["p_ready"])

                def out_copy(h):
                    for k in range(2):
                        dve.wait_ge(at["o_done"], 2 * h + k + 1)
                        do(dve.tensor_copy(MG[:, 2 * h + k, :], AOB[k][:, :]), at["oc_ready"])

                def out_lo(h):
                    for k in range(2):
                        dve.wait_ge(at["ohi_ready"], 2 * h + k + 1)
                        stt(Hlo[:, 2 * h + k, :], MG[:, 2 * h + k, :], 1.0, Hhi[:, 2 * h + k, :].bitcast(F32), ALU.mult, ALU.subtract,
                            at["osplit_ready"])

                maxima(0)
                round_up(BY_VECTOR[-1])
                normalise(0)
                maxima(1)
                maxima(2)
                normalise(1)
                out_copy(0)
                maxima(3)
                normalise(2)
                out_lo(0)
                out_copy(1)
                normalise(3)
                out_lo(1)
                out_copy(2)
                out_lo(2)
                out_copy(3)
                out_lo(3)
                for c in range(4):
                    residual(f"o{c}", norm=2)
                add_squares(2, 7, 8)
                norm_out(16, "norm_mlp")
                n = [0]

                def up(q):
                    for c in range(4):
                        for b in range(2):
                            dve.wait_ge(up_a, n[0] + 1)
                            tt(UPX[:, 0, :], UPX[:, 0, :], UPX[:, 0, :], ALU.mult, up_v)
                            dve.wait_ge(uphi, n[0] + 1)
                            hb = MHID[q % 2]
                            stt(hb[1][:, 2 * c + b, :], UPX[:, 0, :], 1.0, hb[0][:, 2 * c + b, :].bitcast(F32), ALU.mult, ALU.subtract, uplo)
                            n[0] += 1

                def down(q):
                    for c in range(4):
                        residual(f"down{q}_{c}", norm=3 if q == 3 else None)
                    if q == 3:
                        add_squares(3, 7, 8)

                up(0)
                up(1)
                down(0)
                up(2)
                down(1)
                up(3)
                down(2)
                down(3)
                dve.nop().then_inc(layer_end, 1)
                dve.wait_ge(layer_go, L + 2)

            dve.wait_ge(f_act, 2)
            for k in range(KC):
                dve.scalar_tensor_tensor(out=MG[:, k, :], in0=X[:, k, :], scalar=col("norm_final", k), in1=R(32)[:, 0, :],
                                         op0=ALU.mult, op1=ALU.mult).then_inc(f_vec, 1)
            for t in range(TT):
                dve.wait_ge(f_pe, 3 + t)
                dve.tensor_copy(R(2 * t + 1)[:, 0, :], FB[t][1][:, :]).then_inc(f_vec, 1)


_INS = ['x', 'mem', 'norm_mix', 'w_in', 'mlstm_conv_w', 'mlstm_conv_b', 'mlstm_i_bias', 'mlstm_f_bias', 'mlstm_norm',
        'gla_w_a2', 'gla_b_a', 'gla_norm', 's5_lam_re', 's5_lam_im', 's5_b_re', 's5_b_im', 's5_c_re', 's5_c_im', 's5_d',
        's5_log_step', 's5_w_glu', 's5_b_glu', 'hgrn_lb_logits', 'hgrn_norm', 'w_branch', 'w_out', 'norm_xattn',
        'norm_mem', 'xattn_w_q', 'xattn_w_kv', 'xattn_w_o', 'norm_mlp', 'mlp_w1', 'mlp_w2', 'norm_final']


def kernel(**inputs):
    import numpy as _np
    import concourse.bacc as _bacc
    from concourse import mybir as _mybir
    from concourse.bass_utils import run_bass_kernel_spmd as _run

    nc = _bacc.Bacc("TRN2", target_bir_lowering=False, num_devices=1)
    arrays, args = {}, []
    consts, masks = shape_constants()
    for name, a in [(n, inputs[n]) for n in _INS] + [("consts", consts), ("level_masks", masks)]:
        a = _np.ascontiguousarray(a)
        arrays[f"in_{name}_dram"] = a
        args.append(nc.dram_tensor(f"in_{name}_dram", a.shape, _mybir.dt.from_np(a.dtype), kind="ExternalInput").ap())
    out = nc.dram_tensor("out_0_dram", (1, SEQ, D), _mybir.dt.float32, kind="ExternalOutput").ap()
    build(nc, args, out)
    r = _run(nc, [arrays], core_ids=[0])
    return r.results[0]["out_0_dram"]
```
